# Optimizing a Trainium2 kernel written in Bass

```python
import math
import jax
import jax.numpy as jnp
from jax import lax
import numpy as np
import jax, jax.numpy as jnp

D_MODEL = 1024
BATCH = 1
SEQ = 256
DEPTH = 2

EPS = 1e-6
ROPE_THETA = 10000.0
D_FF = 2816
GDN_HEADS = 4
GDN_DK = 128
GDN_DV = 128
GDN_CONV = 4
GDN_CHUNK = 64
RET_HEADS = 4
RET_DK = 64
RET_DV = 128
RET_CHUNK = 64
DIL_HEADS = 4
DIL_DH = 128
DIL_PATTERNS = ((128, 1), (512, 4), (2048, 16))
DIFF_HEADS = 4
DIFF_DK = 64
DIFF_DV = 128
Q_BLOCK = 128

GDN_QK_W = GDN_HEADS * GDN_DK
GDN_V_W = GDN_HEADS * GDN_DV
GDN_CONV_W = 2 * GDN_QK_W + GDN_V_W
RET_QK_W = RET_HEADS * RET_DK
RET_V_W = RET_HEADS * RET_DV
IN0_SPLITS = (GDN_CONV_W, GDN_V_W, GDN_HEADS, GDN_HEADS, RET_QK_W, RET_QK_W, RET_V_W, RET_V_W)
IN0_W = sum(IN0_SPLITS)
MIX0_W = GDN_V_W + RET_V_W
DIL_W = DIL_HEADS * DIL_DH
DIFF_QK_W = DIFF_HEADS * 2 * DIFF_DK
DIFF_V_W = DIFF_HEADS * DIFF_DV
IN1_SPLITS = (DIL_W, DIL_W, DIL_W, DIFF_QK_W, DIFF_QK_W, DIFF_V_W)
IN1_W = sum(IN1_SPLITS)
MIX1_W = DIL_W + DIFF_V_W


def rmsnorm(x, w=None):
    xf = x.astype(jnp.float32)
    y = xf * lax.rsqrt(jnp.mean(xf * xf, axis=-1, keepdims=True) + EPS)
    if w is not None:
        y = y * w.astype(jnp.float32)
    return y.astype(x.dtype)

def l2norm(t):
    tf = t.astype(jnp.float32)
    return (tf * lax.rsqrt(jnp.sum(tf * tf, axis=-1, keepdims=True) + EPS)).astype(t.dtype)

def split_cols(t, sizes):
    offs = np.cumsum(sizes)[:-1].tolist()
    return jnp.split(t, offs, axis=-1)

def swiglu(h, w_up, w_down):
    gate, up = jnp.split(h @ w_up, 2, axis=-1)
    return (jax.nn.silu(gate) * up) @ w_down

def rope_tables(seq, dim):
    inv = ROPE_THETA ** (-jnp.arange(0, dim, 2, dtype=jnp.float32) / dim)
    ang = jnp.arange(seq, dtype=jnp.float32)[:, None] * inv[None, :]
    return jnp.cos(ang), jnp.sin(ang)

def apply_rope(x, cos, sin):
    x1, x2 = jnp.split(x, 2, axis=-1)
    c = cos[None, :, None, :].astype(x.dtype)
    s = sin[None, :, None, :].astype(x.dtype)
    return jnp.concatenate([x1 * c - x2 * s, x1 * s + x2 * c], axis=-1)

def causal_depthwise_conv(x, w):
    K, C = w.shape
    return lax.conv_general_dilated(x, w[:, None, :].astype(x.dtype), window_strides=(1,),
                                    padding=[(K - 1, 0)], dimension_numbers=('NWC', 'WIO', 'NWC'),
                                    feature_group_count=C)

def to_chunks(t, c):
    B, S = t.shape[:2]
    t = t.reshape(B, S // c, c, *t.shape[2:])
    return jnp.swapaxes(t, 2, 3)

def from_chunks(t):
    t = jnp.swapaxes(t, 2, 3)
    return t.reshape(t.shape[0], t.shape[1] * t.shape[2], *t.shape[3:])

def gated_delta_rule_chunked(q, k, v, g, beta):
    B, S, H, dk = q.shape
    dv = v.shape[-1]
    C = GDN_CHUNK
    f32 = jnp.float32
    qc, kc, vc = (to_chunks(t.astype(f32), C) for t in (q, k, v))
    gc, bc = (to_chunks(t.astype(f32), C) for t in (g, beta))
    gcum = jnp.cumsum(gc, axis=-1)
    idx = jnp.arange(C)
    causal = idx[:, None] >= idx[None, :]
    strict = idx[:, None] > idx[None, :]
    gdiff = gcum[..., :, None] - gcum[..., None, :]
    decay = jnp.where(causal, jnp.exp(jnp.where(causal, gdiff, 0.0)), 0.0)
    a_strict = jnp.where(strict, jnp.einsum('bnhid,bnhjd->bnhij', kc, kc) * decay * bc[..., :, None], 0.0)
    rhs = jnp.concatenate([vc * bc[..., None], kc * (bc * jnp.exp(gcum))[..., None]], axis=-1)
    sol = lax.linalg.triangular_solve(a_strict + jnp.eye(C, dtype=f32), rhs, left_side=True,
                                      lower=True, unit_diagonal=True)
    u, w = sol[..., :dv], sol[..., dv:]
    qk = jnp.einsum('bnhid,bnhjd->bnhij', qc, kc) * decay
    q_dec = qc * jnp.exp(gcum)[..., None]
    g_last = gcum[..., -1]
    k_dec = kc * jnp.exp(g_last[..., None] - gcum)[..., None]

    def step(state, xs):
        qk_n, q_n, w_n, u_n, k_n, gl_n = xs
        v_new = u_n - jnp.einsum('bhcd,bhde->bhce', w_n, state)
        o_n = jnp.einsum('bhcd,bhde->bhce', q_n, state) + jnp.einsum('bhij,bhje->bhie', qk_n, v_new)
        state = state * jnp.exp(gl_n)[..., None, None] + jnp.einsum('bhcd,bhce->bhde', k_n, v_new)
        return state, o_n

    xs = tuple(jnp.moveaxis(t, 1, 0) for t in (qk, q_dec, w, u, k_dec, g_last))
    _, o = lax.scan(step, jnp.zeros((B, H, dk, dv), f32), xs)
    return from_chunks(jnp.moveaxis(o, 0, 1)).astype(v.dtype)

def retention_chunked(q, k, v):
    B, S, H, dk = q.shape
    dv = v.shape[-1]
    C = RET_CHUNK
    f32 = jnp.float32
    log_gamma = jnp.log(1.0 - 2.0 ** (-5.0 - jnp.arange(H, dtype=f32)))
    qc, kc, vc = (to_chunks(t.astype(f32), C) for t in (q, k, v))
    idx = jnp.arange(C, dtype=f32)
    rel = idx[:, None] - idx[None, :]
    causal = rel >= 0
    dmask = jnp.where(causal, jnp.exp(jnp.where(causal, rel, 0.0)[None] * log_gamma[:, None, None]), 0.0)
    intra = jnp.einsum('bnhij,bnhje->bnhie', jnp.einsum('bnhid,bnhjd->bnhij', qc, kc) * dmask, vc)
    k_scale = jnp.exp((C - 1 - idx)[None, :] * log_gamma[:, None])
    q_scale = jnp.exp((idx + 1)[None, :] * log_gamma[:, None])
    chunk_decay = jnp.exp(C * log_gamma)
    kv = jnp.einsum('bnhcd,bnhce->bnhde', kc * k_scale[..., None], vc)

    def step(state, kv_n):
        return state * chunk_decay[:, None, None] + kv_n, state

    _, prev = lax.scan(step, jnp.zeros((B, H, dk, dv), f32), jnp.moveaxis(kv, 1, 0))
    prev = jnp.moveaxis(prev, 0, 1)
    inter = jnp.einsum('bnhcd,bnhde->bnhce', qc, prev) * q_scale[..., None]
    return from_chunks(intra + inter).astype(v.dtype)

def dilated_branch(q, k, v, window, dilation):
    B, S, H, d = q.shape
    L = S // dilation
    n_keys = window // dilation
    blk = min(n_keys, L)
    nb = -(-L // blk)
    Lp = nb * blk

    def strided(t):
        t = t.reshape(B, L, dilation, H, d).swapaxes(1, 2)
        t = jnp.pad(t, ((0, 0), (0, 0), (0, Lp - L), (0, 0), (0, 0)))
        return t.reshape(B, dilation, nb, blk, H, d)

    def with_prev(t):
        prev = jnp.pad(t, ((0, 0), (0, 0), (1, 0), (0, 0), (0, 0), (0, 0)))[:, :, :-1]
        return jnp.concatenate([prev, t], axis=3)

    qs = strided(q)
    kb, vb = with_prev(strided(k)), with_prev(strided(v))
    s = jnp.einsum('brnqhd,brnkhd->brnhqk', qs, kb).astype(jnp.float32)
    qi = jnp.arange(blk)[:, None] + blk
    kj = jnp.arange(2 * blk)[None, :]
    dist = qi - kj
    band = (dist >= 0) & (dist <= n_keys)
    has_prev = (jnp.arange(nb) > 0)[:, None, None] | (kj >= blk)[None]
    valid = band[None] & has_prev
    s = jnp.where(valid[:, None], s, -jnp.inf)
    m = jnp.max(s, axis=-1)
    p = jnp.exp(s - m[..., None])
    l = jnp.sum(p, axis=-1)
    o = jnp.einsum('brnhqk,brnkhd->brnqhd', p.astype(v.dtype), vb).astype(jnp.float32)

    def unstrided(t):
        t = t.reshape(B, dilation, Lp, *t.shape[4:])[:, :, :L]
        return t.swapaxes(1, 2).reshape(B, S, *t.shape[3:])

    return unstrided(o), unstrided(m.swapaxes(3, 4)), unstrided(l.swapaxes(3, 4))

def dilated_attention(q, k, v):
    outs = [dilated_branch(q, k, v, w, r) for (w, r) in DIL_PATTERNS]
    m_all = jnp.max(jnp.stack([o[1] for o in outs]), axis=0)
    num = jnp.zeros_like(outs[0][0])
    den = jnp.zeros_like(outs[0][2])
    for o_g, m_g, l_g in outs:
        scale = jnp.exp(m_g - m_all)
        num = num + o_g * scale[..., None]
        den = den + l_g * scale
    return (num / den[..., None]).astype(v.dtype)

def differential_attention(q1, q2, k1, k2, v, lam):
    B, S, H, dk = q1.shape
    nq = S // Q_BLOCK

    def blocks(t):
        return jnp.moveaxis(t.reshape(B, nq, Q_BLOCK, H, t.shape[-1]), 1, 0)

    key_pos = jnp.arange(S)

    def one_block(args):
        i, qa, qb = args
        q_pos = i * Q_BLOCK + jnp.arange(Q_BLOCK)
        causal = (q_pos[:, None] >= key_pos[None, :])[None, None]
        s1 = jnp.where(causal, jnp.einsum('bqhd,bkhd->bhqk', qa, k1).astype(jnp.float32), -jnp.inf)
        s2 = jnp.where(causal, jnp.einsum('bqhd,bkhd->bhqk', qb, k2).astype(jnp.float32), -jnp.inf)
        attn = jax.nn.softmax(s1, axis=-1) - lam * jax.nn.softmax(s2, axis=-1)
        return jnp.einsum('bhqk,bkhe->bqhe', attn.astype(v.dtype), v)

    o = lax.map(one_block, (jnp.arange(nq), blocks(q1), blocks(q2)))
    return jnp.moveaxis(o, 0, 1).reshape(B, S, H, v.shape[-1])

def mixer_delta_retention(h, w_in, conv_w, a_log, dt_bias, gdn_norm, w_out, cos, sin):
    B, S, _ = h.shape
    qkv, z, b, a, rq, rk, rv, rg = split_cols(h @ w_in, IN0_SPLITS)
    qkv = jax.nn.silu(causal_depthwise_conv(qkv, conv_w))
    q, k, v = split_cols(qkv, (GDN_QK_W, GDN_QK_W, GDN_V_W))
    q = l2norm(q.reshape(B, S, GDN_HEADS, GDN_DK)) * GDN_DK ** -0.5
    k = l2norm(k.reshape(B, S, GDN_HEADS, GDN_DK))
    v = v.reshape(B, S, GDN_HEADS, GDN_DV)
    beta = jax.nn.sigmoid(b)
    g = -jnp.exp(a_log) * jax.nn.softplus(a + dt_bias)
    o_a = gated_delta_rule_chunked(q, k, v, g, beta)
    o_a = rmsnorm(o_a, gdn_norm) * jax.nn.silu(z.reshape(B, S, GDN_HEADS, GDN_DV))
    rq = apply_rope(rq.reshape(B, S, RET_HEADS, RET_DK), cos, sin) * RET_DK ** -0.5
    rk = apply_rope(rk.reshape(B, S, RET_HEADS, RET_DK), cos, sin)
    o_b = retention_chunked(rq, rk, rv.reshape(B, S, RET_HEADS, RET_DV))
    o_b = rmsnorm(o_b) * jax.nn.silu(rg.reshape(B, S, RET_HEADS, RET_DV))
    o = jnp.concatenate([o_a.reshape(B, S, GDN_V_W), o_b.reshape(B, S, RET_V_W)], axis=-1)
    return o @ w_out

def mixer_dilated_differential(h, w_in, lambda_q1, lambda_k1, lambda_q2, lambda_k2, diff_norm, w_out,
                               cos128, sin128, cos64, sin64, lambda_init):
    B, S, _ = h.shape
    cq, ck, cv, dq, dk, dv = split_cols(h @ w_in, IN1_SPLITS)
    cq = apply_rope(cq.reshape(B, S, DIL_HEADS, DIL_DH), cos128, sin128) * DIL_DH ** -0.5
    ck = apply_rope(ck.reshape(B, S, DIL_HEADS, DIL_DH), cos128, sin128)
    o_c = dilated_attention(cq, ck, cv.reshape(B, S, DIL_HEADS, DIL_DH))
    dq = dq.reshape(B, S, DIFF_HEADS, 2, DIFF_DK)
    dk = dk.reshape(B, S, DIFF_HEADS, 2, DIFF_DK)
    q1 = apply_rope(dq[..., 0, :], cos64, sin64) * DIFF_DK ** -0.5
    q2 = apply_rope(dq[..., 1, :], cos64, sin64) * DIFF_DK ** -0.5
    k1 = apply_rope(dk[..., 0, :], cos64, sin64)
    k2 = apply_rope(dk[..., 1, :], cos64, sin64)
    lam = (jnp.exp(jnp.sum(lambda_q1 * lambda_k1).astype(jnp.float32))
           - jnp.exp(jnp.sum(lambda_q2 * lambda_k2).astype(jnp.float32)) + lambda_init)
    o_d = differential_attention(q1, q2, k1, k2, dv.reshape(B, S, DIFF_HEADS, DIFF_DV), lam)
    o_d = rmsnorm(o_d, diff_norm) * (1.0 - lambda_init)
    o = jnp.concatenate([o_c.reshape(B, S, DIL_W), o_d.reshape(B, S, DIFF_V_W)], axis=-1)
    return o @ w_out

def first_inputs(seed: int = 0) -> dict:
    key = jax.random.key(seed)
    ks = iter(jax.random.split(key, 64))

    def nrm(shape, scale):
        return jax.random.normal(next(ks), shape, jnp.float32) * scale

    def gain(n):
        return 1.0 + 0.02 * jax.random.normal(next(ks), (n,), jnp.float32)

    inp = {}
    inp['x'] = nrm((BATCH, SEQ, D_MODEL), 1.0)

    def ffn(prefix):
        inp[prefix + '_norm'] = gain(D_MODEL)
        inp[prefix + '_w_up'] = nrm((D_MODEL, 2 * D_FF), D_MODEL ** -0.5)
        inp[prefix + '_w_down'] = nrm((D_FF, D_MODEL), D_FF ** -0.5)

    ffn('l0_ffn1')
    inp['l0_mix_norm'] = gain(D_MODEL)
    inp['l0_w_in'] = nrm((D_MODEL, IN0_W), D_MODEL ** -0.5)
    inp['l0_conv_w'] = nrm((GDN_CONV, GDN_CONV_W), GDN_CONV ** -0.5)
    inp['l0_a_log'] = jnp.log(jax.random.uniform(next(ks), (GDN_HEADS,), jnp.float32, 1.0, 16.0))
    dt = jnp.exp(jax.random.uniform(next(ks), (GDN_HEADS,), jnp.float32, math.log(1e-3), math.log(1e-1)))
    inp['l0_dt_bias'] = dt + jnp.log(-jnp.expm1(-dt))
    inp['l0_gdn_norm'] = gain(GDN_DV)
    inp['l0_w_out'] = nrm((MIX0_W, D_MODEL), MIX0_W ** -0.5)
    ffn('l0_ffn2')
    ffn('l1_ffn1')
    inp['l1_mix_norm'] = gain(D_MODEL)
    inp['l1_w_in'] = nrm((D_MODEL, IN1_W), D_MODEL ** -0.5)
    inp['l1_lambda_q1'] = nrm((DIFF_DK,), 0.1)
    inp['l1_lambda_k1'] = nrm((DIFF_DK,), 0.1)
    inp['l1_lambda_q2'] = nrm((DIFF_DK,), 0.1)
    inp['l1_lambda_k2'] = nrm((DIFF_DK,), 0.1)
    inp['l1_diff_norm'] = gain(DIFF_DV)
    inp['l1_w_out'] = nrm((MIX1_W, D_MODEL), MIX1_W ** -0.5)
    ffn('l1_ffn2')
    inp['final_norm'] = gain(D_MODEL)
    return inp

def first_block(x, l0_ffn1_norm, l0_ffn1_w_up, l0_ffn1_w_down, l0_mix_norm, l0_w_in, l0_conv_w, l0_a_log,
              l0_dt_bias, l0_gdn_norm, l0_w_out, l0_ffn2_norm, l0_ffn2_w_up, l0_ffn2_w_down,
              l1_ffn1_norm, l1_ffn1_w_up, l1_ffn1_w_down, l1_mix_norm, l1_w_in, l1_lambda_q1, l1_lambda_k1,
              l1_lambda_q2, l1_lambda_k2, l1_diff_norm, l1_w_out, l1_ffn2_norm, l1_ffn2_w_up, l1_ffn2_w_down,
              final_norm):
    S = x.shape[1]
    cos64, sin64 = rope_tables(S, 64)
    cos128, sin128 = rope_tables(S, 128)
    ffn1 = ((l0_ffn1_norm, l0_ffn1_w_up, l0_ffn1_w_down), (l1_ffn1_norm, l1_ffn1_w_up, l1_ffn1_w_down))
    ffn2 = ((l0_ffn2_norm, l0_ffn2_w_up, l0_ffn2_w_down), (l1_ffn2_norm, l1_ffn2_w_up, l1_ffn2_w_down))
    mix_norm = (l0_mix_norm, l1_mix_norm)
    for i in range(DEPTH):
        n1, wu1, wd1 = ffn1[i]
        x = x + 0.5 * swiglu(rmsnorm(x, n1), wu1, wd1)
        h = rmsnorm(x, mix_norm[i])
        if i % 2 == 0:
            mix = mixer_delta_retention(h, l0_w_in, l0_conv_w, l0_a_log, l0_dt_bias, l0_gdn_norm, l0_w_out,
                                        cos64, sin64)
        else:
            lambda_init = 0.8 - 0.6 * math.exp(-0.3 * i)
            mix = mixer_dilated_differential(h, l1_w_in, l1_lambda_q1, l1_lambda_k1, l1_lambda_q2, l1_lambda_k2,
                                             l1_diff_norm, l1_w_out, cos128, sin128, cos64, sin64, lambda_init)
        x = x + mix
        n2, wu2, wd2 = ffn2[i]
        x = x + 0.5 * swiglu(rmsnorm(x, n2), wu2, wd2)
    return rmsnorm(x, final_norm)


MEM_LEN = 256
GROUP_WIDTH = D_MODEL // 2
D_MIX = 3 * GROUP_WIDTH
MOBA_HEAD_DIM = 64
MOBA_HEADS = GROUP_WIDTH // MOBA_HEAD_DIM
MOBA_BLOCK = 256
MOBA_TOPK = 3
MOBA_Q_CHUNK = 16
HGRN_HEAD_DIM = 128
HGRN_HEADS = GROUP_WIDTH // HGRN_HEAD_DIM
HGRN_CHUNK = 64
MEM_HEAD_DIM = 128
MEM_HEADS = GROUP_WIDTH // MEM_HEAD_DIM
ROPE_THETA_2 = 500000.0
ROPE_DIM = MOBA_HEAD_DIM // 4
NORM_EPS = 1e-6
IN_COLS = 3 * GROUP_WIDTH + 3 * GROUP_WIDTH + GROUP_WIDTH + D_MIX


def rms_norm(x, g):
    xf = x.astype(jnp.float32)
    y = xf * lax.rsqrt(jnp.mean(xf * xf, axis=-1, keepdims=True) + NORM_EPS)
    return (y * g.astype(jnp.float32)).astype(x.dtype)

def partial_rope(x, positions):
    half = ROPE_DIM // 2
    inv_freq = ROPE_THETA_2 ** (-jnp.arange(half, dtype=jnp.float32) / half)
    ang = positions.astype(jnp.float32)[..., None] * inv_freq
    cos = jnp.cos(ang)[:, :, None, :]
    sin = jnp.sin(ang)[:, :, None, :]
    xr = x[..., :ROPE_DIM].astype(jnp.float32)
    x1, x2 = xr[..., :half], xr[..., half:]
    rot = jnp.concatenate([x1 * cos - x2 * sin, x2 * cos + x1 * sin], axis=-1).astype(x.dtype)
    return jnp.concatenate([rot, x[..., ROPE_DIM:]], axis=-1)

def moba_attention(q, k, v):
    B, S, H, D = q.shape
    BLK, QC = MOBA_BLOCK, MOBA_Q_CHUNK
    nb = -(-S // BLK)
    pad = nb * BLK - S
    topk = min(MOBA_TOPK, nb)
    kbh = jnp.pad(k, ((0, 0), (0, pad), (0, 0), (0, 0))).reshape(B, nb, BLK, H, D).transpose(0, 3, 1, 2, 4)
    vbh = jnp.pad(v, ((0, 0), (0, pad), (0, 0), (0, 0))).reshape(B, nb, BLK, H, D).transpose(0, 3, 1, 2, 4)
    kmean = jnp.mean(kbh.astype(jnp.float32), axis=3)
    scale = D ** -0.5
    nqc = S // QC
    qch = q.reshape(B, nqc, QC, H, D).transpose(1, 0, 3, 2, 4)
    bi = jnp.arange(B)[:, None, None, None]
    hi = jnp.arange(H)[None, :, None, None]
    blk_ids = jnp.arange(nb)

    def one_chunk(args):
        ci, qi = args
        start = ci * QC
        own = start // BLK
        qpos = start + jnp.arange(QC)
        gate = jnp.einsum('bhqd,bhnd->bhqn', qi.astype(jnp.float32), kmean)
        gate = jnp.where(blk_ids < own, gate, -jnp.inf)
        _, sel = lax.top_k(gate, topk)
        sel_ok = sel < own
        k_sel = kbh[bi, hi, sel]
        v_sel = vbh[bi, hi, sel]
        s_sel = jnp.einsum('bhqd,bhqkld->bhqkl', qi, k_sel).astype(jnp.float32) * scale
        s_sel = jnp.where(sel_ok[..., None], s_sel, -jnp.inf).reshape(B, H, QC, topk * BLK)
        k_own = lax.dynamic_index_in_dim(kbh, own, axis=2, keepdims=False)
        v_own = lax.dynamic_index_in_dim(vbh, own, axis=2, keepdims=False)
        kpos = own * BLK + jnp.arange(BLK)
        s_own = jnp.einsum('bhqd,bhld->bhql', qi, k_own).astype(jnp.float32) * scale
        s_own = jnp.where(kpos[None, :] <= qpos[:, None], s_own, -jnp.inf)
        p = jax.nn.softmax(jnp.concatenate([s_sel, s_own], axis=-1), axis=-1).astype(v.dtype)
        p_sel = p[..., :topk * BLK].reshape(B, H, QC, topk, BLK)
        p_own = p[..., topk * BLK:]
        return (jnp.einsum('bhqkl,bhqkld->bhqd', p_sel, v_sel)
                + jnp.einsum('bhql,bhld->bhqd', p_own, v_own))

    o = lax.map(one_chunk, (jnp.arange(nqc), qch))
    return o.transpose(1, 0, 3, 2, 4).reshape(B, S, H, D)

def hgrn2_chunkwise(q, f_logit, i, lb):
    B, S, H, DK = q.shape
    DV = i.shape[-1]
    C = HGRN_CHUNK
    NC = S // C
    fl = f_logit.astype(jnp.float32)
    qf = jax.nn.silu(q.astype(jnp.float32))
    log_f = jnp.logaddexp(jnp.log(lb), jnp.log1p(-lb) + jax.nn.log_sigmoid(fl))
    kf = (1.0 - lb) * jax.nn.sigmoid(-fl)
    vf = i.astype(jnp.float32)

    def to_chunks(t):
        return t.reshape(B, NC, C, H, t.shape[-1]).transpose(1, 0, 3, 2, 4)

    causal = jnp.tril(jnp.ones((C, C), dtype=bool))

    def step(state, inp):
        qc, lfc, kc, vc = inp
        A = jnp.cumsum(lfc, axis=2)
        diff = A[:, :, :, None, :] - A[:, :, None, :, :]
        decay = jnp.exp(jnp.where(causal[:, :, None], diff, -jnp.inf))
        scores = jnp.einsum('bhtd,bhtsd,bhsd->bhts', qc, decay, kc)
        o = (jnp.einsum('bhts,bhsv->bhtv', scores, vc)
             + jnp.einsum('bhtd,bhdv->bhtv', qc * jnp.exp(A), state))
        A_end = A[:, :, -1:, :]
        state = (jnp.exp(A_end[:, :, 0, :])[..., None] * state
                 + jnp.einsum('bhsd,bhsv->bhdv', kc * jnp.exp(A_end - A), vc))
        return state, o

    s0 = jnp.zeros((B, H, DK, DV), jnp.float32)
    _, o = lax.scan(step, s0, (to_chunks(qf), to_chunks(log_f), to_chunks(kf), to_chunks(vf)))
    return o.transpose(1, 0, 3, 2, 4).reshape(B, S, H, DV)

def memory_attention(q, k, v):
    scale = q.shape[-1] ** -0.5
    s = jnp.einsum('bshd,bmhd->bhsm', q, k).astype(jnp.float32) * scale
    p = jax.nn.softmax(s, axis=-1).astype(v.dtype)
    return jnp.einsum('bhsm,bmhd->bshd', p, v)

def second_inputs(seed: int = 0) -> dict:
    key = jax.random.key(seed)
    ks = jax.random.split(key, 14)
    f32 = jnp.float32

    def gain(k, shape):
        return 1.0 + 0.02 * jax.random.normal(k, shape, f32)

    return {
        "x": jax.random.normal(ks[0], (BATCH, SEQ, D_MODEL), f32),
        "mem": jax.random.normal(ks[1], (BATCH, MEM_LEN, D_MODEL), f32),
        "positions": jnp.tile(jnp.arange(SEQ, dtype=jnp.int32)[None, :], (BATCH, 1)),
        "norm_g": gain(ks[2], (DEPTH, D_MODEL)),
        "w_in": jax.random.normal(ks[3], (DEPTH, D_MODEL, IN_COLS), f32) * D_MODEL ** -0.5,
        "w_out": jax.random.normal(ks[4], (DEPTH, D_MIX, D_MODEL), f32) * D_MIX ** -0.5,
        "moba_q_norm": gain(ks[5], (DEPTH, MOBA_HEAD_DIM)),
        "moba_k_norm": gain(ks[6], (DEPTH, MOBA_HEAD_DIM)),
        "hgrn_lb_logits": 0.5 * jax.random.normal(ks[7], (DEPTH, GROUP_WIDTH), f32),
        "hgrn_o_norm": gain(ks[8], (DEPTH, HGRN_HEAD_DIM)),
        "mem_norm_g": gain(ks[9], (DEPTH, D_MODEL)),
        "w_mem_kv": jax.random.normal(ks[10], (DEPTH, D_MODEL, 2 * GROUP_WIDTH), f32) * D_MODEL ** -0.5,
        "mem_q_norm": gain(ks[11], (DEPTH, MEM_HEAD_DIM)),
        "mem_k_norm": gain(ks[12], (DEPTH, MEM_HEAD_DIM)),
    }

def second_block(x, mem, positions, norm_g, w_in, w_out, moba_q_norm, moba_k_norm, hgrn_lb_logits,
              hgrn_o_norm, mem_norm_g, w_mem_kv, mem_q_norm, mem_k_norm):
    B, S, _ = x.shape
    M = mem.shape[1]
    G = GROUP_WIDTH
    lb_all = jnp.cumsum(jax.nn.softmax(hgrn_lb_logits.astype(jnp.float32), axis=0), axis=0)
    lb_all = lb_all - lb_all[0:1]
    split_points = [G * n for n in range(1, 8)]
    for l in range(DEPTH):
        h = rms_norm(x, norm_g[l])
        proj = h @ w_in[l]
        q_a, k_a, v_a, q_h, f_h, i_h, q_m, z = jnp.split(proj, split_points, axis=-1)

        qa = partial_rope(rms_norm(q_a.reshape(B, S, MOBA_HEADS, MOBA_HEAD_DIM), moba_q_norm[l]), positions)
        ka = partial_rope(rms_norm(k_a.reshape(B, S, MOBA_HEADS, MOBA_HEAD_DIM), moba_k_norm[l]), positions)
        va = v_a.reshape(B, S, MOBA_HEADS, MOBA_HEAD_DIM)
        o_a = moba_attention(qa, ka, va).reshape(B, S, G)

        o_h = hgrn2_chunkwise(q_h.reshape(B, S, HGRN_HEADS, HGRN_HEAD_DIM),
                              f_h.reshape(B, S, HGRN_HEADS, HGRN_HEAD_DIM),
                              i_h.reshape(B, S, HGRN_HEADS, HGRN_HEAD_DIM),
                              lb_all[l].reshape(HGRN_HEADS, HGRN_HEAD_DIM))
        o_h = rms_norm(o_h, hgrn_o_norm[l]).astype(x.dtype).reshape(B, S, G)

        kv_m = rms_norm(mem, mem_norm_g[l]) @ w_mem_kv[l]
        k_m, v_m = jnp.split(kv_m, 2, axis=-1)
        km = rms_norm(k_m.reshape(B, M, MEM_HEADS, MEM_HEAD_DIM), mem_k_norm[l])
        vm = v_m.reshape(B, M, MEM_HEADS, MEM_HEAD_DIM)
        qm = rms_norm(q_m.reshape(B, S, MEM_HEADS, MEM_HEAD_DIM), mem_q_norm[l])
        o_m = memory_attention(qm, km, vm).reshape(B, S, G)

        y = jnp.concatenate([o_a, o_h, o_m], axis=-1) * jax.nn.silu(z)
        x = x + y @ w_out[l]
    return x


def setup_inputs(seed=0):
    out = dict(first_inputs(seed))
    for name, value in second_inputs(seed + 1).items():
        if name != "x":
            out[name + "_2"] = value
    return out


def reference(
    x, l0_ffn1_norm, l0_ffn1_w_up, l0_ffn1_w_down, l0_mix_norm, l0_w_in, l0_conv_w, l0_a_log,
    l0_dt_bias, l0_gdn_norm, l0_w_out, l0_ffn2_norm, l0_ffn2_w_up, l0_ffn2_w_down, l1_ffn1_norm,
    l1_ffn1_w_up, l1_ffn1_w_down, l1_mix_norm, l1_w_in, l1_lambda_q1, l1_lambda_k1,
    l1_lambda_q2, l1_lambda_k2, l1_diff_norm, l1_w_out, l1_ffn2_norm, l1_ffn2_w_up,
    l1_ffn2_w_down, final_norm, mem_2, positions_2, norm_g_2, w_in_2, w_out_2, moba_q_norm_2,
    moba_k_norm_2, hgrn_lb_logits_2, hgrn_o_norm_2, mem_norm_g_2, w_mem_kv_2, mem_q_norm_2,
    mem_k_norm_2,
):
    x = first_block(
        x, l0_ffn1_norm, l0_ffn1_w_up, l0_ffn1_w_down, l0_mix_norm, l0_w_in, l0_conv_w,
        l0_a_log, l0_dt_bias, l0_gdn_norm, l0_w_out, l0_ffn2_norm, l0_ffn2_w_up, l0_ffn2_w_down,
        l1_ffn1_norm, l1_ffn1_w_up, l1_ffn1_w_down, l1_mix_norm, l1_w_in, l1_lambda_q1,
        l1_lambda_k1, l1_lambda_q2, l1_lambda_k2, l1_diff_norm, l1_w_out, l1_ffn2_norm,
        l1_ffn2_w_up, l1_ffn2_w_down, final_norm,
    )
    return second_block(
        x, mem_2, positions_2, norm_g_2, w_in_2, w_out_2, moba_q_norm_2, moba_k_norm_2,
        hgrn_lb_logits_2, hgrn_o_norm_2, mem_norm_g_2, w_mem_kv_2, mem_q_norm_2, mem_k_norm_2,
    )


_drawn_inputs = setup_inputs


def setup_inputs(seed=0):
    import zlib

    import numpy as np

    out = dict(_drawn_inputs(seed))
    spreads = {}
    factors = {'l0_ffn1_norm': 3.757,
     'l0_gdn_norm': 5.034,
     'l0_ffn2_norm': 6.21,
     'l1_ffn1_norm': 6.699,
     'l1_mix_norm': 3.939,
     'l1_lambda_q1': 5.287,
     'l1_lambda_k1': 7.792,
     'l1_lambda_q2': 4.146,
     'l1_lambda_k2': 7.163,
     'l1_diff_norm': 6.354,
     'l1_ffn2_norm': 8.0,
     'norm_g_2': 4.076,
     'moba_q_norm_2': 8.0,
     'moba_k_norm_2': 8.0,
     'hgrn_lb_logits_2': 3.26,
     'hgrn_o_norm_2': 6.318,
     'mem_norm_g_2': 8.0,
     'mem_q_norm_2': 8.0,
     'mem_k_norm_2': 8.0}
    for name, (base, spread) in spreads.items():
        noise = np.random.default_rng([zlib.crc32(name.encode()), seed]).standard_normal(out[name].shape)
        drawn = base * np.exp(spread * noise) if base else spread * noise
        out[name] = jnp.asarray(drawn.astype(out[name].dtype))
    for name, factor in factors.items():
        out[name] = (out[name] * factor).astype(out[name].dtype)
    return out
```

```python
import math
from contextlib import ExitStack

import numpy as np

import concourse.bass as bass
from concourse import mybir

F32 = mybir.dt.float32
F32R = mybir.dt.float32r
I32 = mybir.dt.int32
U32 = mybir.dt.uint32
ALU = mybir.AluOpType
ACT = mybir.ActivationFunctionType
AX = mybir.AxisListType.X

P = 128
SEQ = 256
TILES = SEQ // P
D = 1024
DC = D // P
D_FF = 2816
UPW = 256
UPS = D_FF // UPW
PANEL = DC * UPW
SLOTS = 3
EPS = 1e-6
LAMBDA_INIT = 0.8 - 0.6 * math.exp(-0.3)
MAGIC = 12582912.0
TWO_PI = (6.28125, 0.0019354820251464844, -1.7484556025237907e-07)
PI_IN = 3.1415925
WORK = 15360

COUNTS = [("ffn0", 3 * UPS), ("in0", 14), ("out0", 4), ("ffn1", 3 * UPS), ("ffn2", 3 * UPS),
          ("in1", 12), ("out1", 4), ("ffn3", 3 * UPS), ("mem0", 4), ("in2_0", 20), ("out2_0", 6),
          ("mem1", 4), ("in2_1", 20), ("out2_1", 6)]
BASE = {}
PANELS = 0
for _name, _n in COUNTS:
    BASE[_name] = PANELS
    PANELS += _n
N_OF = dict(COUNTS)

GAINS = ["ffn0", "mix0", "ffn1", "ffn2", "mix1", "ffn3", "final", "mem0", "pre0", "mem1", "pre1"]

SMALL = {}
_at = 0
for _name, _n in [("conv", 48), ("wab", 64), ("alog", 4), ("dt", 4), ("gdn", 1), ("diff", 1), ("lam", 4),
                  ("lb", 8), ("mq0", 1), ("mk0", 1), ("sq0", 1), ("sk0", 1), ("ho0", 1),
                  ("mq1", 1), ("mk1", 1), ("sq1", 1), ("sk1", 1), ("ho1", 1)]:
    SMALL[_name] = (_at, _n)
    _at += _n
SMALL_W = _at


def tables():
    i = np.arange(P)
    part, free = i[:, None], i[None, :]
    f = np.float32
    upper = (part <= free).astype(f)
    strict_low = (part > free).astype(f)

    def swap(n, half, signs=True, width=None):
        m = np.zeros((P, P), f)
        for g in range(0, P, n):
            for d in range(half):
                m[g + d + half, g + d] = -1.0
                m[g + d, g + d + half] = 1.0
        return m

    def rope(dim):
        inv = (np.float32(10000.0) ** (-np.arange(0, dim, 2, dtype=f) / f(dim))).astype(f)
        ang = (np.arange(SEQ, dtype=f)[None, :] * inv[:, None]).astype(f)
        reps = P // (dim // 2)
        return np.tile(np.cos(ang), (reps, 1)).astype(f), np.tile(np.sin(ang), (reps, 1)).astype(f)

    q0 = part - free
    q1 = part + P - np.arange(SEQ)[None, :]
    dist = np.concatenate([q0, q1], axis=1)
    causal = np.where(dist >= 0, 0.0, -1e38).astype(f)
    times = ((dist >= 0) & (dist <= 128)).astype(f)
    for r in (4, 16):
        times = times + ((dist >= 0) & (dist % r == 0)).astype(f)
    union = np.where(times > 0, 0.0, -1e38).astype(f)
    rel = np.concatenate([np.arange(SEQ)[None, :] - part, free - part], axis=1).astype(np.float64)
    ret = [np.where(rel >= 0, np.exp(np.maximum(rel, 0) * math.log(1 - 2.0 ** (-5 - h))), 0.0) * 0.125
           for h in range(4)]
    cos64, sin64 = rope(64)
    cos128, sin128 = rope(128)
    diag16 = (part // 16 == free // 16).astype(f)

    def below(b):
        return ((part // (2 * b) == free // (2 * b)) & (part % (2 * b) >= b) & (free % (2 * b) < b)).astype(f)

    levels = [((part // (2 * b) == free // (2 * b)) & (part % (2 * b) < b) & (free % (2 * b) >= b)).astype(f)
              for b in (64, 32, 16, 8, 4, 2, 1)]
    keep = np.ones((P, SEQ), f)
    keep[:, ::P] = 0
    half = 8
    inv2 = (f(500000.0) ** (-np.arange(half, dtype=f) / f(half))).astype(f)
    freq = np.zeros((P, 1), f)
    for g in (0, 64):
        freq[g:g + half, 0] = inv2
        freq[g + half:g + 2 * half, 0] = inv2
    sets = [
        [("ident", np.eye(P)), ("ones", np.ones((P, P))), ("ones64", part // 64 == free // 64),
         ("eps", np.full((P, 1), EPS)), ("one", np.ones((P, 1)))],
        [("upper", upper), ("strict", strict_low), ("diag16", diag16), ("e16", below(16)), ("e32", below(32)),
         ("e64", below(64)), ("ret", np.concatenate(ret, axis=1)), ("cos64", cos64), ("sin64", sin64),
         ("swap64", swap(64, 32))],
        [("causal", causal), ("times", times), ("union", union), ("cos64", cos64), ("sin64", sin64),
         ("swap64", swap(64, 32)), ("cos128", cos128), ("sin128", sin128), ("swap128", swap(128, 64))],
        [("causal", causal), ("swapp", swap(64, 8)), ("levels", np.concatenate(levels, axis=1)),
         ("keep", keep), ("freq", freq)],
    ]
    arrays, places = [], []
    for s in sets:
        where, at_ = {}, 0
        for name, a in s:
            where[name] = (at_, a.shape[1])
            at_ += a.shape[1]
        arrays.append(np.ascontiguousarray(np.concatenate([np.asarray(a, f) for _, a in s], axis=1)))
        places.append(where)
    return arrays, places


TABLES, PLACES = tables()
TABLE_W = max(t.shape[1] for t in TABLES[1:])

RESIDUALS = {"mix0": "ffn0", "ffn1": "out0", "ffn2": "ffn1", "mix1": "ffn2", "ffn3": "out1", "final": "ffn3",
             "pre1": "out2_0", "end": "out2_1"}
DOWNS = list(RESIDUALS.values())
LATE = {name: (BASE[name] + N_OF[name] + SLOTS - 1, min(BASE[name] + N_OF[name] + SLOTS, PANELS)) for name in DOWNS}
UNCOUNTED = {"logs", "split_hi", "split_lo", "ffn", "panel", "load", "store"}


def rounds(steps, units):
    return [[(engine, kind, (units[r - lag],)) for engine, kind, lag in steps if 0 <= r - lag < len(units)]
            for r in range(len(units) + max(lag for _, _, lag in steps))]


def lagged(steps, units):
    return sum(rounds(steps, units), [])


NORM_COLS = [("pe", "cn_sum", 1), ("act", "cn_rstd", 1), ("act", "cn_sq", 0), ("dve", "cn_use", 1)]
ATTEND = [("pe", "turn_p", 2), ("pe", "attend", 3), ("pe", "scores", 0), ("act", "p_cols", 2), ("dve", "divide", 1),
          ("dve", "mask_max", 0), ("act", "exp", 0)]
ROPE = [("pe", "swap", 0), ("dve", "rope", 0)]
NORM_ROPE = NORM_COLS + [("pe", "swap", 2), ("dve", "rope", 2)]


def next_gain(tag):
    i = GAINS.index(tag) + 1
    return [("pool", "load", ("gain_" + GAINS[i],))] if i < len(GAINS) else []


def norm_steps(tag):
    out = [("act", "logs", ())]
    before = RESIDUALS.get(tag) if tag != "pre1" else None
    for t in range(TILES):
        out += [("dve", "residual", (before, t))] if before else []
        out += [("act", "sumsq", (tag, t)), ("act", "rstd", (tag, t))]
    for t in range(TILES):
        for half in range(2):
            out += [(e, k, (tag, t, half)) for e, k in (("dve", "scale"), ("pe", "turn_x"))]
    for t in range(TILES):
        for half in range(2):
            out += [("act", "x_hi", (tag, t, half)), ("dve", "x_lo", (tag, t, half))]
    for n in range(*LATE.get(before, (0, 0))):
        out += [("act", "split_hi", (n,)), ("dve", "split_lo", (n,))]
    return out + next_gain(tag)


def panel_steps(name, extra=None, start=0, stop=None):
    out = []
    for k in range(start, N_OF[name] if stop is None else stop):
        n = BASE[name] + k
        out.append(("pe", "panel", (name, k)))
        if not name.startswith("out"):
            out.append(("act", "evacuate", (name, k)))
        late = LATE.get(name, (0, 0))
        if n + SLOTS < PANELS and not late[0] <= n + SLOTS < late[1]:
            out += [("act", "split_hi", (n + SLOTS,)), ("dve", "split_lo", (n + SLOTS,))]
        out += (extra or {}).get(k, [])
    return out


def ffn_steps(f):
    return norm_steps(f"ffn{f}") + [(e, "ffn", (f,)) for e in ("pe", "act", "dve")]


def delta_steps():
    both = lambda *steps: [(e, k, (*a, t)) for e, k, *a in steps for t in range(TILES)]
    out = [("act", "softplus", ()), ("dve", "g", ()), ("pe", "cumsum", ())]
    out += lagged(NORM_COLS, [("dq", 0), ("dq", 1), ("dk", 0), ("dk", 1)])
    out += [("dve", "gc", ())] + both(("dve", "gap"), ("act", "decay"), ("dve", "decay_mask")) + [("dve", "q_decayed", ())]
    out += [("pe", "turn_v", (0,)), ("pe", "turn_v", (1,)), ("dve", "v_beta", (0,)), ("dve", "v_beta", (1,)),
            ("pe", "turn_k", ()), ("dve", "k_decayed", ())]
    out += both(("pe", "kk"), ("dve", "a_low"), ("pe", "turn_a"), ("dve", "base16"), ("pe", "pow2"), ("act", "pow2_n"),
                ("dve", "pow2_a"), ("pe", "pow4"), ("act", "pow4_n"), ("dve", "pow4_a"), ("pe", "pow8"), ("act", "pow8_a"),
                ("dve", "pow8_m"), ("pe", "pow16"), ("dve", "pow16_m"), ("pe", "turn_m"), ("act", "t_rows"))
    out += both(("pe", "kq"), ("dve", "qk_decay"))
    for s in range(3):
        out += both(("dve", "corner", s), ("pe", "double_y", s), ("act", "y", s), ("pe", "double", s), ("dve", "doubled", s))
    out += [("pe", "u", (0,)), ("act", "v_new", (0,)), ("pe", "state", ()), ("act", "state_copy", ()),             ("pe", "from_state", ()), ("dve", "v_less", ()), ("pe", "u", (1,)), ("act", "v_new", (1,)),
            ("pe", "delta_out", (0,)), ("pe", "delta_out", (1,))]
    out += lagged(NORM_COLS, [("do", 0), ("do", 1)])
    return out


def retention_steps():
    out = lagged(ROPE, [("r64", 0), ("r64", 1)])
    out += lagged([("pe", "ret_scores", 0), ("dve", "ret_decay", 0), ("pe", "ret_out", 1)], [0, 1, 2, 3])
    out += lagged(NORM_COLS, [("ro", 0), ("ro", 1)])
    return out


def hgrn_steps(l):
    out = [("dve", "f_abs", (l,)), ("act", "f_ln", (l,)), ("dve", "f_log", (l,))]
    if l:
        out += [("act", "f_ln2", (l,)), ("dve", "f_log2", (l,))]
    out += [("act", "k_gate", (l,)), ("dve", "cum_f", (l,)), ("pe", "diagonal", (l,)), ("dve", "diagonal_in", (l,))]
    out += [(e, k, (l, v)) for e, k, v in
            [s for r in range(8 + 2) for s in
             [("dve", "gap_f", r), ("act", "decay_f", r), ("dve", "q_level", r - 1), ("pool", "k_level", r - 1),
              ("pe", "level", r - 1), ("dve", "level_in", r - 2)] if 0 <= s[2] < 8]]
    out += [("pe", "hgrn_out", (l, g)) for g in (0, 1)]
    out += lagged(NORM_COLS, [(f"ho{l}", 0), (f"ho{l}", 1)])
    return out


def order():
    out = [("pool", "load", (x,)) for x in ("x", "gain_ffn0", "const", "small", "tab1")] + [("pool", "zero", ())]
    out += [("act", "wab_hi", ()), ("dve", "wab_lo", ())]
    for n in range(SLOTS):
        out += [("act", "split_hi", (n,)), ("dve", "split_lo", (n,))]
    out += ffn_steps(0)
    conv = {p + 0: [("act", "tap", (p,)), ("dve", "conv", (p,)), ("act", "conv_silu", (p,))] for p in range(6)}
    out += norm_steps("mix0") + panel_steps("in0", conv) + [("pe", "ab_mm", ()), ("act", "logs", ()), ("act", "ab_exp", ()), ("dve", "ab", ())]
    out += retention_steps() + delta_steps()
    out += [("pool", "load", ("tab2",))] + panel_steps("out0")
    out += ffn_steps(1) + ffn_steps(2) + norm_steps("mix1") + panel_steps("in1")
    out += [("act", "logs", ())]
    out += [("dve", "lam_mul", ()), ("pe", "lam_sum", ()), ("act", "lam_exp", ()), ("dve", "lam", ())]
    out += lagged(ROPE, [("r128", g) for g in range(4)] + [("r64b", g) for g in range(4)])
    out += lagged(ATTEND, [("dil", h) for h in range(4)])
    out += [("dve", "gate_out", (("dil", g),)) for g in (0, 1)]
    out += lagged(ATTEND, [("dif", h) for h in range(4)])
    out += lagged(NORM_COLS, [("fo", 0), ("fo", 1)])
    out += [("pool", "load", ("tab3",)), ("pool", "load", ("pos",))] + panel_steps("out1")
    out += [("dve", "angle", ()), ("act", "sines", ())]
    out += ffn_steps(3)
    for t in range(TILES):
        out += [("dve", "residual", ("ffn3", t)), ("act", "sumsq", ("final", t)), ("act", "rstd", ("final", t))]
    out += [("dve", "scale", ("final", t, half)) for t in (0, 1) for half in (0, 1)] + next_gain("final")
    for n in range(*LATE["ffn3"]):
        out += [("act", "split_hi", (n,)), ("dve", "split_lo", (n,))]
    for l in range(2):
        out += [("pool", "load", (f"mem{l}",))] + norm_steps(f"mem{l}") + panel_steps(f"mem{l}")
        out += norm_steps(f"pre{l}") + panel_steps(f"in2_{l}") + [("act", "logs", ())]
        out += lagged(NORM_COLS, [(f"mq{l}", 0), (f"mq{l}", 1), (f"mk{l}", 0), (f"mk{l}", 1)])
        out += lagged(ROPE, [(f"rp{l}", g) for g in range(4)])
        out += lagged(ATTEND, [(f"moba{l}", h) for h in range(8)])
        out += [("dve", "gate_out", ((f"moba{l}", g),)) for g in (0, 1)]
        out += lagged(NORM_COLS, [(f"sq{l}", 0), (f"sq{l}", 1), (f"sk{l}", 0), (f"sk{l}", 1)])
        out += lagged(ATTEND, [(f"matt{l}", h) for h in range(4)])
        out += [("dve", "gate_out", ((f"matt{l}", g),)) for g in (0, 1)]
        out += hgrn_steps(l)
        out += panel_steps(f"out2_{l}")
        if not l:
            out += [("dve", "residual", ("out2_0", t)) for t in range(TILES)]
            for n in range(*LATE["out2_0"]):
                out += [("act", "split_hi", (n,)), ("dve", "split_lo", (n,))]
    for t in range(TILES):
        out += [("dve", "residual", ("out2_1", t)), ("pool", "store", (t,))]
    return out


ORDER = order()
COUNT_AT = {}
_counts = {}
for _e, _k, _a in ORDER:
    if _k not in UNCOUNTED:
        _counts[_e] = _counts.get(_e, 0) + 1
        assert (_e, _k, _a) not in COUNT_AT, (_e, _k, _a)
        COUNT_AT[_e, _k, _a] = _counts[_e]


def at(engine, kind, *args):
    return COUNT_AT[engine, kind, args]


def build(nc, x_in, mem_in, pos_in, panels, gains, small_in, tab0, tab1, tab2, tab3, out):
    with ExitStack() as ctx:
        def sb(name, shape, dt=F32):
            return ctx.enter_context(nc.sbuf_tensor(name, shape, dt))

        def sem(name):
            return ctx.enter_context(nc.semaphore(name))

        raw = sb("raw", [P, SLOTS, PANEL])
        w_hi = sb("w_hi", [P, SLOTS, PANEL], F32R)
        w_lo = sb("w_lo", [P, SLOTS, PANEL], F32R)
        x = sb("x", [P, TILES, D])
        act_hi = sb("act_hi", [P, 12, SEQ], F32R)
        act_lo = sb("act_lo", [P, 12, SEQ], F32R)
        g_hi = sb("g_hi", [P, 2, 2, SEQ], F32R)
        g_lo = sb("g_lo", [P, 2, 2, SEQ], F32R)
        pair = sb("pair", [P, 2048])
        xn = sb("xn", [P, TILES * D])
        gain = sb("gain", [P, D])
        const = sb("const", [P, tab0.shape[1]])
        table = sb("table", [P, TABLE_W])
        small = sb("small", [P, SMALL_W])
        wab_h = sb("wab_h", [P, 64], F32R)
        wab_l = sb("wab_l", [P, 64], F32R)
        stat = sb("stat", [P, 98])
        work = sb("work", [P, WORK])
        ps = ctx.enter_context(nc.psum_tensor("ps", [P, 8, 512], F32))

        silu_buf, g32 = pair[:, 0:512], pair[:, 512:1024]
        sq = [pair[:, 0:512], pair[:, 512:1024]]
        rs = [pair[:, 1024:1536], pair[:, 1536:2048]]
        y32 = xn[:, 0:512]

        def cst(name):
            a, n = PLACES[0][name]
            return const[:, a:a + n]

        def tab(s, name):
            a, n = PLACES[s][name]
            return table[:, a:a + n]

        def sm(name, j=0, n=1):
            a, _ = SMALL[name]
            return small[:, a + j:a + j + n]

        def region(a, *shape):
            n = int(np.prod(shape))
            v = work[:, a:a + n]
            if len(shape) == 2:
                return v.rearrange("p (a b) -> p a b", a=shape[0])
            if len(shape) == 3:
                return v.rearrange("p (a b c) -> p a b c", a=shape[0], b=shape[1])
            return v

        def grid(ap, a):
            return ap.rearrange("p (a b) -> p a b", a=a)

        def spread(ap, n):
            return ap.rearrange("p (a b) -> p a b", a=1).broadcast_to([P, n, ap.shape[1]])

        def along(ap, n):
            return ap.rearrange("p (b o) -> p b o", o=1).broadcast_to([P, ap.shape[1], n])

        ident = cst("ident")

        raw_qkv = region(0, 12, 260)
        qk = region(3120, 8, SEQ)
        vc = region(5168, 4, SEQ)
        z0 = region(6192, 4, SEQ)
        rqk = region(7216, 4, SEQ)
        rv = region(8240, TILES, 512)
        rg = region(9264, 4, SEQ)
        a_low = region(10288, TILES, 4, P)
        decay_t = region(11312, TILES, 4, P)
        pw_a = region(12336, TILES, 4, P)
        pw_n = region(13360, TILES, 4, P)
        assert 14384 <= WORK
        pw_a4 = region(5168, TILES, 4, P)
        pw_n4 = region(7216, TILES, 4, P)
        t_mat = region(8240, TILES, 4, P)
        m_mat = region(9264, TILES, 4, P)
        v_beta = region(0, TILES, 4, P)
        v_new = region(1024, TILES, 4, P)
        state = region(2048, 4, P)
        k_dec = region(2560, 4, P)
        q_dec = region(14384, 4, P)
        ret_p = region(12336, 4, 384)

        cqk = region(0, 8, SEQ)
        cv = region(2048, TILES, 512)
        dqk = region(3072, 8, SEQ)
        dv = region(5120, TILES, 512)
        mo_qk = region(0, 8, SEQ)
        mo_v = region(2048, TILES, 512)
        qm = region(3072, 4, SEQ)
        km = region(4096, 4, SEQ)
        vm = region(5120, TILES, 512)
        probs = region(6144, 2, 2, 512)
        p_t = region(8192, 2, 512)
        qh = region(9216, 4, SEQ)
        fh = region(10240, 4, SEQ)
        ih = region(11264, TILES, 512)
        z2 = region(12288, 12, SEQ)
        assert 15360 <= WORK
        hg = [region(1024 * i, 4, SEQ) for i in range(9)]
        k_g, dec_f, q_l, k_l = hg[0], (hg[1], hg[2]), (hg[3], hg[4]), (hg[5], hg[6])
        h_s = region(7 * 1024, TILES, 4, P)
        h_s01 = region(8 * 1024, 4, P)
        positions = region(0, SEQ).bitcast(I32)
        cos_a = table[:, TABLE_W - 512:TABLE_W - 256]
        sin_a = table[:, TABLE_W - 256:TABLE_W]
        ang, turns = region(1024, SEQ), region(2048, SEQ)

        sumsq, rstd = stat[:, 0:2], stat[:, 2:4]
        b_exp, beta, xa, e_sp = (stat[:, 4 + 8 * i:12 + 8 * i] for i in range(4))
        g_col, gc, e_gc, bge = (stat[:, 36 + 8 * i:44 + 8 * i] for i in range(4))
        e_alog, e_kd = stat[:, 68:72], stat[:, 72:76]
        nmax = (stat[:, 76:80], stat[:, 80:84])
        dens = (stat[:, 84:88], stat[:, 88:92])
        lam_c = stat[:, 92:96]
        dgain = stat[:, 96:97]
        zero4 = stat[:, 97:98]
        lbd, lbn, lbl = stat[:, 4:12], stat[:, 12:20], stat[:, 20:28]

        done = {e: sem(f"{e}_done") for e in ("pe", "act", "dve", "pool")}
        pe_done, act_done, dve_done, pool_done = (done[e] for e in ("pe", "act", "dve", "pool"))
        act_chain, dve_chain = sem("act_chain"), sem("dve_chain")
        panel_loaded = [sem(f"panel_loaded_{i}") for i in range(SLOTS)]
        panel_hi, panel_lo, panel_used = sem("panel_hi"), sem("panel_lo"), sem("panel_used")
        silu_done, gate_read, gate_hi, gate_ready = (sem(n) for n in ("silu_done", "gate_read", "gate_hi", "gate_ready"))
        loads = [a[0] for e, k, a in ORDER if k == "load"]
        loaded = {n: sem(f"loaded_{n}") for n in loads}
        stored = sem("stored")
        tile_ready = sem("tile_ready")

        def evac(name, k):
            return ("act", "evacuate", name, k)

        ropes = {}
        for g in range(2):
            ropes["r64", g] = (rqk[:, 2 * g:2 * g + 2], tab(1, "swap64"), tab(1, "cos64"), tab(1, "sin64"), evac("in0", 8 + g))
        for g in range(4):
            ropes["r128", g] = (cqk[:, 2 * g:2 * g + 2], tab(2, "swap128"), tab(2, "cos128"), tab(2, "sin128"), evac("in1", g))
            ropes["r64b", g] = (dqk[:, 2 * g:2 * g + 2], tab(2, "swap64"), tab(2, "cos64"), tab(2, "sin64"), evac("in1", 6 + g))
            for l in range(2):
                ropes[f"rp{l}", g] = (mo_qk[:, 2 * g:2 * g + 2], tab(3, "swapp"), cos_a, sin_a,
                                      ("dve", "cn_use", ((f"mq{l}", f"mk{l}")[g // 2], g % 2)))
        rope_list = [a for e, k, a in ORDER if k == "swap"]
        rope_index = {a[0]: i for i, a in enumerate(rope_list)}

        norms = {}
        for g in range(2):
            s2 = slice(2 * g, 2 * g + 2)
            s4 = slice(4 + 2 * g, 6 + 2 * g)
            ones, ones64 = cst("ones"), cst("ones64")
            norms["dq", g] = (qk[:, s2], ones, 1.0, P ** -0.5, qk[:, s2], None, None, 4 + g, ("act", "conv_silu", g))
            norms["dk", g] = (qk[:, s4], ones, 1.0, 1.0, qk[:, s4], None, None, 4 + g, ("act", "conv_silu", 2 + g))
            norms["do", g] = (grid(ps[:, 6 + g], 2), ones, 1 / P, sm("gdn"), None, z0[:, s2], 2 * g, g, ("pe", "delta_out", g))
            norms["ro", g] = (grid(ps[:, 2 + g], 2), ones, 1 / P, 1.0, None, rg[:, s2], 4 + 2 * g, g, ("pe", "ret_out", 2 * g + 1))
            norms["fo", g] = (grid(ps[:, 6 + g], 2), ones, 1 / P, dgain, None, None, 4 + 2 * g, 4 + g, ("pe", "attend", ("dif", 2 * g + 1)))
            for l in range(2):
                norms[f"mq{l}", g] = (mo_qk[:, s2], ones64, 1 / 64, sm(f"mq{l}"), mo_qk[:, s2], None, None, 2 + g, evac(f"in2_{l}", g))
                norms[f"mk{l}", g] = (mo_qk[:, s4], ones64, 1 / 64, sm(f"mk{l}"), mo_qk[:, s4], None, None, 2 + g, evac(f"in2_{l}", 2 + g))
                norms[f"sq{l}", g] = (qm[:, s2], ones, 1 / P, sm(f"sq{l}"), qm[:, s2], None, None, 4 + g, evac(f"in2_{l}", 12 + g))
                norms[f"sk{l}", g] = (km[:, s2], ones, 1 / P, sm(f"sk{l}"), km[:, s2], None, None, 4 + g, evac(f"mem{l}", g))
                norms[f"ho{l}", g] = (grid(ps[:, 6 + g], 2), ones, 1 / P, sm(f"ho{l}"), None, z2[:, 4 + 2 * g:6 + 2 * g], 4 + 2 * g, 4 + g,
                                      ("pe", "hgrn_out", l, g))
        norm_list = [a[0] for e, k, a in ORDER if k == "cn_sum"]
        norm_index = {u: i for i, u in enumerate(norm_list)}

        atts = {}
        for h in range(4):
            o = lambda b, j: ps[:, b, SEQ * j:SEQ * (j + 1)]
            col = slice(P * h, P * h + P)
            atts["dil", h] = ([(cqk[:, h], cqk[:, 4 + h])], cv[:, :, col], o(6 + h // 2, h % 2), False, tab(2, "union"),
                              tab(2, "times"), P ** -0.5, ("dve", "rope", ("r64b", 3)))
            atts["dif", h] = ([(dqk[0:64, h], dqk[0:64, 4 + h]), (dqk[64:128, h], dqk[64:128, 4 + h])], dv[:, :, col],
                              o(6 + h // 2, h % 2), False, tab(2, "causal"), None, 0.125, ("dve", "rope", ("r64b", 3)))
            for l in range(2):
                atts[f"matt{l}", h] = ([(qm[:, h], km[:, h])], vm[:, :, col], o(6 + h // 2, h % 2), True, None, None, P ** -0.5,
                                       ("dve", "cn_use", (f"sk{l}", 1)))
        for h in range(8):
            r = slice(64 * (h % 2), 64 * (h % 2) + 64)
            for l in range(2):
                atts[f"moba{l}", h] = ([(mo_qk[r, h // 2], mo_qk[r, 4 + h // 2])], mo_v[:, :, 64 * h:64 * h + 64],
                                       ps[r, 6 + h // 4, SEQ * (h // 2 % 2):SEQ * (h // 2 % 2) + SEQ], False, tab(3, "causal"), None, 0.125,
                                       ("dve", "rope", (f"rp{l}", 3)))
        att_list = [a[0] for e, k, a in ORDER if k == "scores"]
        att_index = {u: i for i, u in enumerate(att_list)}
        gates = {}
        for g in range(2):
            gates["dil", g] = (None, 2 * g, ("dil", 2 * g + 1))
            for l in range(2):
                gates[f"moba{l}", g] = (z2[:, 2 * g:2 * g + 2], 2 * g, (f"moba{l}", 4 * g + 3))
                gates[f"matt{l}", g] = (z2[:, 8 + 2 * g:10 + 2 * g], 8 + 2 * g, (f"matt{l}", 2 * g + 1))

        def spans(full):
            return [(0, 256), (256, 512)] if full else [(0, 128), (128, 384)]

        dest = {}
        for k in range(6):
            dest["in0", k] = (raw_qkv[:, 2 * k:2 * k + 2, 4:260], "cols", ACT.Copy)
        rows = lambda r, k: r[:, :, UPW * k:UPW * (k + 1)]
        blocks = lambda r, k: r[:, 2 * k:2 * k + 2]
        for k in range(2):
            dest["in0", 6 + k] = (blocks(z0, k), "cols", ACT.Silu)
            dest["in0", 8 + k] = (blocks(rqk, k), "cols", ACT.Copy)
            dest["in0", 10 + k] = (rows(rv, k), "rows", ACT.Copy)
            dest["in0", 12 + k] = (blocks(rg, k), "cols", ACT.Silu)
            dest["in1", 4 + k] = (rows(cv, k), "rows", ACT.Copy)
            dest["in1", 10 + k] = (rows(dv, k), "rows", ACT.Copy)
            for l in range(2):
                dest[f"in2_{l}", 4 + k] = (rows(mo_v, k), "rows", ACT.Copy)
                dest[f"in2_{l}", 6 + k] = (blocks(qh, k), "cols", ACT.Silu)
                dest[f"in2_{l}", 8 + k] = (blocks(fh, k), "cols", ACT.Copy)
                dest[f"in2_{l}", 10 + k] = (rows(ih, k), "rows", ACT.Copy)
                dest[f"in2_{l}", 12 + k] = (blocks(qm, k), "cols", ACT.Copy)
                dest[f"mem{l}", k] = (blocks(km, k), "cols", ACT.Copy)
                dest[f"mem{l}", 2 + k] = (rows(vm, k), "rows", ACT.Copy)
        for k in range(4):
            dest["in1", k] = (blocks(cqk, k), "cols", ACT.Copy)
            dest["in1", 6 + k] = (blocks(dqk, k), "cols", ACT.Copy)
            for l in range(2):
                dest[f"in2_{l}", k] = (blocks(mo_qk, k), "cols", ACT.Copy)
        for k in range(6):
            for l in range(2):
                dest[f"in2_{l}", 14 + k] = (blocks(z2, k), "cols", ACT.Silu)

        def bank_of(name, k):
            return 4 + (BASE[name] + k) % 2

        def source_of(tag, t):
            if tag == "ffn0":
                return x, ("load", "x")
            if tag.startswith("mem"):
                return xn[:, :].rearrange("p (t d) -> p t d", t=TILES), ("load", tag)
            return x, (("dve", "scale", "final", t, 1) if tag == "pre0" else ("dve", "residual", RESIDUALS[tag], t))

        xn_rows = xn[:, :].rearrange("p (t d) -> p t d", t=TILES)
        last_use = {}
        for i, g in enumerate(GAINS[1:]):
            last_use["gain_" + g] = ("dve", "scale", GAINS[i], 1, 1)
        last_use["tab2"] = ("dve", "cn_use", ("do", 1))
        last_use["tab3"] = last_use["pos"] = ("dve", "cn_use", ("fo", 1))
        last_use["mem0"] = ("dve", "scale", "final", 1, 1)
        last_use["mem1"] = ("dve", "residual", "out2_0", 1)

        def of(j, const, step):
            return const if j is None else j * step + const

        def steps(engine, handlers):
            for e, kind, args in ORDER:
                if e == engine:
                    handlers[kind](*args)

        def turned(t):
            return ps[:, 2 * t:2 * t + 2].rearrange("p b (c n) -> p (b c) n", n=P)

        def both_banks(t):
            return ps[:, 2 * t:2 * t + 2].rearrange("p b n -> p (b n)")

        def conv_out(b):
            return qk[:, b] if b < 8 else vc[:, b - 8]

        block = ctx.enter_context(nc.Block())

        @block.sync
        def _(sp):
            def load_panel(s, g):
                if isinstance(g, int) and g == 0:
                    sp.dma_start(raw[:, s], panels[s]).then_inc(panel_loaded[s], 16)
                    return
                sp.wait_ge(panel_lo, g * SLOTS + (s + 1 - SLOTS))
                sp.dma_start(raw[:, s], panels[g * SLOTS + s]).then_inc(panel_loaded[s], 16)

            for s in range(SLOTS):
                load_panel(s, 0)
            with sp.Fori(1, PANELS // SLOTS) as g:
                for s in range(SLOTS):
                    load_panel(s, g)
            for s in range(PANELS % SLOTS):
                load_panel(s, PANELS // SLOTS)

        @block.gpsimd
        def _(pool):
            places = {"x": (x[:], x_in), "const": (const[:], tab0), "small": (small[:], small_in),
                      "tab1": (table[:, 0:tab1.shape[1]], tab1), "tab2": (table[:, 0:tab2.shape[1]], tab2),
                      "tab3": (table[:, 0:tab3.shape[1]], tab3),
                      "pos": (positions, pos_in.rearrange("(a n) -> a n", a=1).broadcast_to([P, SEQ])),
                      "mem0": (xn_rows, mem_in), "mem1": (xn_rows, mem_in)}
            for i, g in enumerate(GAINS):
                places["gain_" + g] = (gain[:], gains[i:i + 1].broadcast_to([P, D]))

            def load(tag):
                if tag in last_use:
                    pool.wait_ge(done[last_use[tag][0]], at(*last_use[tag]))
                to, of_ = places[tag]
                pool.dma_start(to, of_).then_inc(loaded[tag], 16)

            def zero():
                nc.gpsimd.memset(raw_qkv[:, :, 0:4], 0.0)
                nc.gpsimd.memset(zero4, 0.0).then_inc(pool_done, 1)

            def k_level(l, v):
                if v == 0:
                    pool.wait_ge(act_done, at("act", "k_gate", l))
                pool.wait_ge(act_done, at("act", "decay_f", l, v))
                if v >= 2:
                    pool.wait_ge(pe_done, at("pe", "level", l, v - 2))
                nc.gpsimd.tensor_tensor(k_l[v % 2], k_g, dec_f[v % 2], ALU.mult).then_inc(pool_done, 1)

            def store(t):
                pool.wait_ge(dve_done, at("dve", "residual", "out2_1", t))
                pool.dma_start(out[:, t], x[:, t]).then_inc(stored, 16)
                if t == TILES - 1:
                    pool.wait_ge(stored, 16 * TILES)

            steps("pool", {"load": load, "zero": zero, "k_level": k_level, "store": store})

        @block.tensor
        def _(pe):
            def three(o, l, r, start, stop):
                pe.matmul(o, l[0], r[0], start=start, stop=False)
                pe.matmul(o, l[0], r[1], start=False, stop=False)
                return pe.matmul(o, l[1], r[0], start=False, stop=stop)

            def weight(slot, c, a, n, width):
                return [w[:, slot, c * width + a:c * width + a + n] for w in (w_hi, w_lo)]

            def up(slot, bank, form, n, j=None, step=0, tag=None):
                pe.wait_ge(panel_lo, of(j, n + 1, step))
                for half in range(2):
                    o = ps[:, bank, SEQ * half:SEQ * (half + 1)]
                    for c in range(DC):
                        if tag and half == 0 and c % 4 == 0:
                            pe.wait_ge(dve_done, at("dve", "x_lo", tag, 1, c // 4))
                        if form == "cols":
                            l = weight(slot, c, P * half, P, UPW)
                            r = [a[:, c, :] for a in (act_hi, act_lo)]
                        else:
                            l = [a[:, c, P * half:P * half + P] for a in (act_hi, act_lo)]
                            r = weight(slot, c, 0, UPW, UPW)
                        ins = three(o, l, r, c == 0, c == DC - 1)
                ins.then_inc(panel_used, 1)

            def down(slot, parts, first, last, n, j=None, step=0):
                pe.wait_ge(panel_lo, of(j, n + 1, step))
                for t in range(TILES):
                    for half in range(2):
                        for c in range(2):
                            l = [a[:, c, P * t:P * t + P] for a in parts]
                            ins = three(ps[:, 2 * t + half], l, weight(slot, c, 512 * half, 512, D),
                                        first and c == 0, last and c == 1)
                    if last and t == 0:
                        ins.then_inc(tile_ready, 1)
                ins.then_inc(panel_used, 1)

            def ffn(f):
                b, c = BASE[f"ffn{f}"], f * UPS
                tag = f"ffn{f}"

                def gate_up(i, j=None):
                    n = b + (0 if i == 0 else 3 * i - 1)
                    if i:
                        pe.wait_ge(gate_read, of(j, c + i, 2))
                    up(n % SLOTS, 4, "cols", n, j, 6, None if i else tag)
                    up((n + 1) % SLOTS, 5, "cols", n + 1, j, 6)

                def down_of(i, j=None):
                    n = b + (3 * i + 4 if i < UPS - 1 else 3 * UPS - 1)
                    pe.wait_ge(gate_ready, of(j, c + i + 1, 2))
                    down(n % SLOTS, (g_hi[:, i % 2], g_lo[:, i % 2]), i == 0, i == UPS - 1, n, j, 6)

                gate_up(0)
                gate_up(1)
                down_of(0)
                with pe.Fori(0, (UPS - 3) // 2) as j:
                    for i in (2, 3):
                        gate_up(i, j)
                        down_of(i - 1, j)
                gate_up(UPS - 1)
                down_of(UPS - 2)
                down_of(UPS - 1)

            def panel(name, k):
                n = BASE[name] + k
                if name.startswith("out"):
                    if k == 0:
                        last = {"out0": ("cn_use", ("do", 1)), "out1": ("cn_use", ("fo", 1)),
                                "out2_0": ("cn_use", ("ho0", 1)), "out2_1": ("cn_use", ("ho1", 1))}[name]
                        pe.wait_ge(dve_done, at("dve", *last))
                    parts = (act_hi[:, 2 * k:2 * k + 2], act_lo[:, 2 * k:2 * k + 2])
                    down(n % SLOTS, parts, k == 0, k == N_OF[name] - 1, n)
                else:
                    tag = {"in0": "mix0", "in1": "mix1", "in2_0": "pre0", "in2_1": "pre1"}.get(name, name)
                    if k >= 2:
                        pe.wait_ge(act_done, at("act", "evacuate", name, k - 2))
                    up(n % SLOTS, bank_of(name, k), dest[name, k][1], n, tag=None if k else tag)

            def turn_x(tag, t, half):
                pe.wait_ge(dve_done, at("dve", "scale", tag, t, half))
                pe.wait_ge(loaded["const"], 16)
                for c in range(4 * half, 4 * half + 4):
                    ins = pe.transpose(ps[:, 2 * t + c // 4, P * (c % 4):P * (c % 4) + P], xn_rows[:, t, P * c:P * c + P], ident)
                ins.then_inc(pe_done, 1)

            def ab_mm():
                pe.wait_ge(dve_done, at("dve", "wab_lo"))
                for t in range(TILES):
                    for c in range(DC):
                        l = [a[:, c, P * t:P * t + P] for a in (act_hi, act_lo)]
                        ins = three(ps[:, 6, 8 * t:8 * t + 8], l, [w[:, 8 * c:8 * c + 8] for w in (wab_h, wab_l)], c == 0, c == DC - 1)
                ins.then_inc(pe_done, 1)

            def heads(o, lhs, rhs, turn=False):
                for h in range(4):
                    oh = o[:, P * h:P * h + P]
                    ins = pe.transpose(oh, lhs(h), ident) if turn else pe.matmul(oh, lhs(h), rhs(h), start=True, stop=True)
                return ins

            def cumsum():
                pe.wait_ge(dve_done, at("dve", "g"))
                pe.wait_ge(loaded["tab1"], 16)
                up_ = tab(1, "upper")
                for t in range(TILES):
                    pe.matmul(ps[:, 6, 4 * t:4 * t + 4], up_, g_col[:, 4 * t:4 * t + 4], start=True, stop=True)
                for t in range(TILES):
                    ins = heads(ps[:, 2 + t], lambda h: g_col[:, 4 * t + h:4 * t + h + 1].broadcast_to([P, P]), lambda h: up_)
                ins.then_inc(pe_done, 1)

            tok = lambda t: slice(P * t, P * t + P)

            def turn_v(t):
                pe.wait_ge(act_done, at("act", "conv_silu", 5))
                pe.wait_ge(dve_done, at("dve", "decay_mask", 1))
                heads(ps[:, 6 + t], lambda h: vc[:, h, tok(t)], None, turn=True).then_inc(pe_done, 1)

            def turn_k():
                pe.wait_ge(dve_done, at("dve", "v_beta", 0))
                heads(ps[:, 6], lambda h: qk[:, 4 + h, tok(0)], None, turn=True).then_inc(pe_done, 1)

            def kk(t):
                pe.wait_ge(dve_done, at("dve", "k_decayed"))
                heads(ps[:, 3 * t], lambda h: qk[:, 4 + h, tok(t)], lambda h: qk[:, 4 + h, tok(t)]).then_inc(pe_done, 1)

            def turn_a(t):
                pe.wait_ge(dve_done, at("dve", "a_low", t))
                heads(ps[:, 3 * t + 1], lambda h: a_low[:, t, h], None, turn=True).then_inc(pe_done, 1)

            def pow2(t):
                pe.wait_ge(dve_done, at("dve", "base16", t))
                heads(ps[:, 3 * t], lambda h: pw_a4[:, t, h], lambda h: t_mat[:, t, h])
                heads(ps[:, 3 * t + 1], lambda h: t_mat[:, t, h], lambda h: pw_a4[:, t, h]).then_inc(pe_done, 1)

            def pow4(t):
                pe.wait_ge(act_done, at("act", "pow2_n", t))
                pe.wait_ge(dve_done, at("dve", "pow2_a", t))
                heads(ps[:, 3 * t], lambda h: pw_a[:, t, h], lambda h: pw_n[:, t, h])
                heads(ps[:, 3 * t + 1], lambda h: pw_n[:, t, h], lambda h: pw_a[:, t, h])
                heads(ps[:, 3 * t + 2], lambda h: pw_a[:, t, h], lambda h: m_mat[:, t, h]).then_inc(pe_done, 1)

            def pow8(t):
                pe.wait_ge(act_done, at("act", "pow4_n", t))
                pe.wait_ge(dve_done, at("dve", "pow4_a", t))
                heads(ps[:, 3 * t], lambda h: pw_n4[:, t, h], lambda h: pw_a4[:, t, h])
                heads(ps[:, 3 * t + 2], lambda h: pw_a4[:, t, h], lambda h: m_mat[:, t, h]).then_inc(pe_done, 1)

            def pow16(t):
                pe.wait_ge(act_done, at("act", "pow8_a", t))
                pe.wait_ge(dve_done, at("dve", "pow8_m", t))
                heads(ps[:, 3 * t + 2], lambda h: pw_a[:, t, h], lambda h: m_mat[:, t, h]).then_inc(pe_done, 1)

            def turn_m(t):
                pe.wait_ge(dve_done, at("dve", "pow16_m", t))
                heads(ps[:, 3 * t], lambda h: m_mat[:, t, h], None, turn=True).then_inc(pe_done, 1)

            def kq(t):
                pe.wait_ge(dve_done, at("dve", "k_decayed"))
                heads(ps[:, 6 + t], lambda h: qk[:, 4 + h, tok(t)], lambda h: qk[:, h, tok(t)]).then_inc(pe_done, 1)

            def double_y(s, t):
                pe.wait_ge(act_done, at("act", "t_rows", t))
                pe.wait_ge(dve_done, at("dve", "corner", s, t))
                heads(ps[:, 3 * t], lambda h: pw_n[:, t, h], lambda h: m_mat[:, t, h]).then_inc(pe_done, 1)

            def double(s, t):
                pe.wait_ge(act_done, at("act", "y", s, t))
                ins = heads(ps[:, 3 * t + 1], lambda h: t_mat[:, t, h], lambda h: pw_a[:, t, h])
                if s < 2:
                    ins = heads(ps[:, 3 * t + 2], lambda h: pw_a[:, t, h], lambda h: t_mat[:, t, h])
                ins.then_inc(pe_done, 1)

            def u(t):
                if t == 0:
                    pe.wait_ge(dve_done, at("dve", "doubled", 2, 1))
                else:
                    pe.wait_ge(dve_done, at("dve", "v_less"))
                heads(ps[:, t], lambda h: m_mat[:, t, h], lambda h: v_beta[:, t, h]).then_inc(pe_done, 1)

            def state_mm():
                pe.wait_ge(act_done, at("act", "v_new", 0))
                heads(ps[:, 2], lambda h: k_dec[:, h], lambda h: v_new[:, 0, h]).then_inc(pe_done, 1)

            def from_state():
                pe.wait_ge(act_done, at("act", "state_copy"))
                heads(ps[:, 3], lambda h: qk[:, 4 + h, tok(1)], lambda h: state[:, h]).then_inc(pe_done, 1)

            def delta_out(g):
                pe.wait_ge(act_done, at("act", "v_new", 1))
                pe.wait_ge(dve_done, at("dve", "q_decayed"))
                for i in range(2):
                    h, o = 2 * g + i, ps[:, 6 + g, SEQ * i:SEQ * i + SEQ]
                    pe.matmul(o[:, 0:P], v_new[:, 0, h], decay_t[:, 0, h], start=True, stop=True)
                    pe.matmul(o[:, P:SEQ], v_new[:, 1, h], decay_t[:, 1, h], start=True, stop=False)
                    ins = pe.matmul(o[:, P:SEQ], state[:, h], q_dec[:, h], start=False, stop=True)
                ins.then_inc(pe_done, 1)

            def ret_scores(h):
                pe.wait_ge(dve_done, at("dve", "rope", ("r64", 1)))
                if h >= 2:
                    pe.wait_ge(dve_done, at("dve", "ret_decay", h - 2))
                r = slice(64 * (h % 2), 64 * (h % 2) + 64)
                q, k = rqk[r, h // 2], rqk[r, 2 + h // 2]
                pe.matmul(ps[:, 4 + h % 2, 0:SEQ], k[:, 0:P], q, start=True, stop=True)
                pe.matmul(ps[:, 4 + h % 2, SEQ:384], k[:, P:SEQ], q[:, P:SEQ], start=True, stop=True).then_inc(pe_done, 1)

            def weighted(o, v0, v1, first, second, full=False):
                pe.matmul(o, v0, first, start=True, stop=False, skip_group_check=True)
                return pe.matmul(o if full else o[:, P:SEQ], v1, second, start=False, stop=True, skip_group_check=True)

            def ret_out(h):
                pe.wait_ge(dve_done, at("dve", "ret_decay", h))
                weighted(ps[:, 2 + h // 2, SEQ * (h % 2):SEQ * (h % 2) + SEQ], rv[:, 0, P * h:P * h + P], rv[:, 1, P * h:P * h + P],
                         ret_p[:, h, 0:SEQ], ret_p[:, h, SEQ:384]).then_inc(pe_done, 1)

            def swap(unit):
                values, matrix, _, _, ready = ropes[unit]
                pe.wait_ge(done[ready[0]], at(*ready))
                if unit == ("r64", 0):
                    pe.wait_ge(dve_done, at("dve", "ab"))
                if unit == ("r128", 0):
                    pe.wait_ge(dve_done, at("dve", "lam"))
                if rope_index[unit] >= 2:
                    pe.wait_ge(dve_done, at("dve", "rope", rope_list[rope_index[unit] - 2][0]))
                for t_ in ("tab1", "tab2", "tab3"):
                    if unit[0] in {"tab1": ("r64",), "tab2": ("r128", "r64b"), "tab3": ("rp0", "rp1")}[t_]:
                        pe.wait_ge(loaded[t_], 16)
                pe.matmul(ps[:, 6 + rope_index[unit] % 2], matrix, values, start=True, stop=True).then_inc(pe_done, 1)

            def cn_sum(unit):
                src, ones, _, _, _, _, _, bank, _ = norms[unit]
                pe.wait_ge(act_done, at("act", "cn_sq", unit))
                pe.matmul(ps[:, bank], ones, sq[norm_index[unit] % 2], start=True, stop=True).then_inc(pe_done, 1)

            def scores(unit):
                maps, _, _, full, _, _, _, ready = atts[unit]
                pe.wait_ge(done[ready[0]], at(*ready))
                i = att_index[unit]
                if i >= 2:
                    pe.wait_ge(dve_done, at("dve", "mask_max", att_list[i - 2]))
                for m, (q, k) in enumerate(maps):
                    bank = ps[:, 2 * (i % 2) + m]
                    pe.matmul(bank[:, 0:SEQ if full else P], q[:, 0:P], k if full else k[:, 0:P], start=True, stop=True)
                    a = SEQ if full else P
                    ins = pe.matmul(bank[:, a:a + SEQ], q[:, P:SEQ], k, start=True, stop=True)
                ins.then_inc(pe_done, 1)

            def turn_p(unit):
                i, full = att_index[unit], atts[unit][3]
                pe.wait_ge(dve_done, at("dve", "divide", unit))
                if i >= 2:
                    pe.wait_ge(act_done, at("act", "p_cols", att_list[i - 2]))
                p, bank = probs[:, i % 2, 0], ps[:, 4 + i % 2]
                second = SEQ if full else P
                pe.transpose(bank[:, 0:P], p[:, 0:P], ident)
                pe.transpose(bank[:, P:SEQ], p[:, second:second + P], ident)
                if full:
                    pe.transpose(bank[:, SEQ:384], p[:, P:SEQ], ident)
                    ins = pe.transpose(bank[:, 384:512], p[:, 384:512], ident)
                else:
                    ins = pe.transpose(bank[:, SEQ:384], p[:, second + P:second + SEQ], ident)
                ins.then_inc(pe_done, 1)

            def attend(unit):
                _, v, o, full, *_ = atts[unit]
                i = att_index[unit]
                pe.wait_ge(act_done, at("act", "p_cols", unit))
                if unit[0] in ("dif",) and unit[1] == 0:
                    pe.wait_ge(dve_done, at("dve", "gate_out", ("dil", 1)))
                if unit[0].startswith("matt") and unit[1] == 0:
                    pe.wait_ge(dve_done, at("dve", "gate_out", ("moba" + unit[0][4:], 1)))
                p = p_t[:, i % 2]
                weighted(o, v[:, 0], v[:, 1], p[:, 0:SEQ], p[:, SEQ:512] if full else p[:, SEQ:384], full).then_inc(pe_done, 1)

            def lam_sum():
                pe.wait_ge(dve_done, at("dve", "lam_mul"))
                pe.matmul(ps[:, 6, 0:2], cst("ones")[0:64, :], lam_c[0:64, 0:2], start=True, stop=True).then_inc(pe_done, 1)

            def diagonal(l):
                pe.wait_ge(act_done, at("act", "k_gate", l))
                for t in range(TILES):
                    ins = heads(ps[:, 4 + t], lambda h: k_g[:, h, tok(t)], lambda h: qh[:, h, tok(t)])
                ins.then_inc(pe_done, 1)

            def level(l, v):
                pe.wait_ge(dve_done, at("dve", "q_level", l, v))
                pe.wait_ge(pool_done, at("pool", "k_level", l, v))
                if v >= 2:
                    pe.wait_ge(dve_done, at("dve", "level_in", l, v - 2))
                k, q = k_l[v % 2], q_l[v % 2]
                if v < 7:
                    for t in range(TILES):
                        ins = heads(ps[:, 2 * (v % 2) + t], lambda h: k[:, h, tok(t)], lambda h: q[:, h, tok(t)])
                else:
                    ins = heads(ps[:, 2], lambda h: k[:, h, tok(0)], lambda h: q[:, h, tok(1)])
                ins.then_inc(pe_done, 1)

            def hgrn_out(l, g):
                pe.wait_ge(dve_done, at("dve", "level_in", l, 7))
                for i in range(2):
                    h, o = 2 * g + i, ps[:, 6 + g, SEQ * i:SEQ * i + SEQ]
                    v0, v1 = ih[:, 0, P * h:P * h + P], ih[:, 1, P * h:P * h + P]
                    pe.matmul(o[:, 0:P], v0, h_s[:, 0, h], start=True, stop=True)
                    pe.matmul(o[:, P:SEQ], v0, h_s01[:, h], start=True, stop=False)
                    ins = pe.matmul(o[:, P:SEQ], v1, h_s[:, 1, h], start=False, stop=True)
                ins.then_inc(pe_done, 1)

            steps("pe", {"ffn": ffn, "panel": panel, "turn_x": turn_x, "ab_mm": ab_mm, "cumsum": cumsum, "turn_v": turn_v,
                         "turn_k": turn_k, "kk": kk, "turn_a": turn_a, "pow2": pow2, "pow4": pow4, "pow8": pow8, "pow16": pow16,
                         "turn_m": turn_m, "kq": kq, "double_y": double_y, "double": double, "u": u, "state": state_mm,
                         "from_state": from_state, "delta_out": delta_out, "ret_scores": ret_scores, "ret_out": ret_out,
                         "swap": swap, "cn_sum": cn_sum, "scores": scores, "turn_p": turn_p, "attend": attend,
                         "lam_sum": lam_sum, "diagonal": diagonal, "level": level, "hgrn_out": hgrn_out})

        @block.scalar
        def _(act):
            chained = [0]

            def step(ins):
                chained[0] += 1
                ins.then_inc(act_chain, 1)
                act.wait_ge(act_chain, chained[0])

            def split_hi(n, j=None, step_=0):
                s = n % SLOTS
                act.wait_ge(panel_loaded[s], of(j, 16 * (n // SLOTS + 1), 16 * step_ // SLOTS))
                if n >= SLOTS:
                    act.wait_ge(panel_used, of(j, n - SLOTS + 1, step_))
                nc.scalar.activation(w_hi[:, s], raw[:, s], ACT.Copy).then_inc(panel_hi, 1)

            def ffn(f):
                b, c = BASE[f"ffn{f}"], f * UPS

                def gate_up(i, j=None):
                    n = b + (0 if i == 0 else 3 * i - 1)
                    split_hi(n + 3, j, 6)
                    act.wait_ge(panel_used, of(j, n + 2, 6))
                    nc.scalar.activation(silu_buf, ps[:, 4], ACT.Silu).then_inc(silu_done, 1)
                    split_hi(n + 4, j, 6)

                def down_of(i, j=None):
                    split_hi(b + (3 * i + 4 if i < UPS - 1 else 3 * UPS - 1) + 3, j, 6)

                gate_up(0)
                gate_up(1)
                down_of(0)
                with act.Fori(0, (UPS - 3) // 2) as j:
                    for i in (2, 3):
                        gate_up(i, j)
                        down_of(i - 1, j)
                gate_up(UPS - 1)
                logs_and_exps()
                down_of(UPS - 2)

            def wab_hi():
                act.wait_ge(loaded["small"], 16)
                nc.scalar.activation(wab_h[:], sm("wab", 0, 64), ACT.Copy).then_inc(act_done, 1)

            def sumsq_(tag, t):
                src, (e, *ready) = source_of(tag, t)
                if e == "load":
                    act.wait_ge(loaded[ready[0]], 16)
                else:
                    act.wait_ge(done[e], at(e, *ready))
                step(nc.scalar.activation(pair[:, D * t:D * t + D], src[:, t], ACT.Square, accum_out=sumsq[:, t:t + 1]))
                act.sem_inc(act_done, 1)

            def rstd_(tag, t):
                act.wait_ge(loaded["const"], 16)
                step(nc.scalar.activation(rstd[:, t:t + 1], sumsq[:, t:t + 1], ACT.Ln, bias=cst("eps"), scale=1 / D))
                nc.scalar.activation(rstd[:, t:t + 1], rstd[:, t:t + 1], ACT.Exp, scale=-0.5).then_inc(act_done, 1)

            def x_hi(tag, t, half):
                act.wait_ge(pe_done, at("pe", "turn_x", tag, t, half))
                to = act_hi[:, 4 * half:4 * half + 4, P * t:P * t + P]
                nc.scalar.activation(to, grid(ps[:, 2 * t + half], 4), ACT.Copy).then_inc(act_done, 1)

            def evacuate(name, k):
                to, form, func = dest[name, k]
                act.wait_ge(panel_used, BASE[name] + k + 1)
                nc.scalar.activation(to, grid(ps[:, bank_of(name, k)], 2), func).then_inc(act_done, 1)

            def tap(p):
                act.wait_ge(pool_done, at("pool", "zero"))
                act.wait_ge(loaded["small"], 16)
                act.wait_ge(act_done, at("act", "evacuate", "in0", p))
                for i in range(2):
                    b = 2 * p + i
                    ins = nc.scalar.activation(conv_out(b), raw_qkv[:, b, 4:260], ACT.Copy, scale=sm("conv", 4 * b + 3))
                ins.then_inc(act_done, 1)

            def conv_silu(p):
                act.wait_ge(dve_done, at("dve", "conv", p))
                for i in range(2):
                    ins = nc.scalar.activation(conv_out(2 * p + i), conv_out(2 * p + i), ACT.Silu)
                ins.then_inc(act_done, 1)

            def logs_and_exps():
                nc.scalar.preload_act_table_set("natural_log_exp_and_others")

            def ab_exp():
                act.wait_ge(pe_done, at("pe", "ab_mm"))
                ab = grid(ps[:, 6, 0:16], 2)
                nc.scalar.activation(grid(b_exp, 2), ab[:, :, 0:4], ACT.Exp, scale=-1.0).then_inc(act_done, 1)

            def softplus():
                act.wait_ge(dve_done, at("dve", "ab"))
                step(nc.scalar.activation(e_sp, e_sp, ACT.Exp))
                nc.scalar.activation(e_sp, e_sp, ACT.Ln, bias=cst("one"))
                nc.scalar.activation(e_alog, sm("alog", 0, 4), ACT.Exp).then_inc(act_done, 1)

            def decay(t):
                act.wait_ge(dve_done, at("dve", "gap", t))
                nc.scalar.activation(decay_t[:, t], decay_t[:, t], ACT.Exp)
                ins = nc.scalar.activation(a_low[:, t], a_low[:, t], ACT.Exp, scale=-1.0)
                if t == 0:
                    nc.scalar.activation(e_gc, gc, ACT.Exp)
                    ins = nc.scalar.activation(e_kd, e_kd, ACT.Exp)
                else:
                    ins = nc.scalar.activation(q_dec, grid(ps[:, 3], 4), ACT.Exp)
                ins.then_inc(act_done, 1)

            def copy_back(to, bank, n=4):
                return nc.scalar.activation(to, grid(ps[:, bank], n), ACT.Copy).then_inc(act_done, 1)

            def pow2_n(t):
                act.wait_ge(pe_done, at("pe", "pow2", t))
                copy_back(pw_n[:, t], 3 * t)

            def pow4_n(t):
                act.wait_ge(pe_done, at("pe", "pow4", t))
                copy_back(pw_n4[:, t], 3 * t)

            def pow8_a(t):
                act.wait_ge(pe_done, at("pe", "pow8", t))
                copy_back(pw_a[:, t], 3 * t)

            def t_rows(t):
                act.wait_ge(pe_done, at("pe", "turn_m", t))
                copy_back(t_mat[:, t], 3 * t)

            def y(s, t):
                act.wait_ge(pe_done, at("pe", "double_y", s, t))
                copy_back(pw_a[:, t], 3 * t)

            def v_new_(t):
                act.wait_ge(pe_done, at("pe", "u", t))
                copy_back(v_new[:, t], t)

            def state_copy():
                act.wait_ge(pe_done, at("pe", "state"))
                copy_back(state, 2)

            def cn_sq(unit):
                src, *_, ready = norms[unit]
                act.wait_ge(done[ready[0]], at(*ready))
                nc.scalar.activation(grid(sq[norm_index[unit] % 2], 2), src, ACT.Square).then_inc(act_done, 1)

            def cn_rstd(unit):
                _, _, inv, _, _, _, _, bank, _ = norms[unit]
                i = norm_index[unit]
                act.wait_ge(pe_done, at("pe", "cn_sum", unit))
                if i >= 2:
                    act.wait_ge(dve_done, at("dve", "cn_use", norm_list[i - 2]))
                step(nc.scalar.activation(rs[i % 2], ps[:, bank], ACT.Ln, bias=cst("eps"), scale=inv))
                nc.scalar.activation(rs[i % 2], rs[i % 2], ACT.Exp, scale=-0.5).then_inc(act_done, 1)

            def exp_(unit):
                maps, _, _, full, *_ = atts[unit]
                i = att_index[unit]
                act.wait_ge(dve_done, at("dve", "mask_max", unit))
                for m in range(len(maps)):
                    for q, (a, b) in enumerate(spans(full)):
                        p = probs[:, i % 2, m, a:b]
                        c = 2 * m + q
                        ins = nc.scalar.activation(p, p, ACT.Exp, bias=nmax[i % 2][:, c:c + 1], scale=-1.0,
                                                   accum_out=dens[i % 2][:, c:c + 1])
                step(ins)
                act.sem_inc(act_done, 1)

            def p_cols(unit):
                i, full = att_index[unit], atts[unit][3]
                act.wait_ge(pe_done, at("pe", "turn_p", unit))
                if i >= 2:
                    act.wait_ge(pe_done, at("pe", "attend", att_list[i - 2]))
                n = 512 if full else 384
                nc.scalar.activation(p_t[:, i % 2, 0:n], ps[:, 4 + i % 2, 0:n], ACT.Copy).then_inc(act_done, 1)

            def lam_exp():
                act.wait_ge(pe_done, at("pe", "lam_sum"))
                nc.scalar.activation(lam_c[:, 2:4], ps[:, 6, 0:2], ACT.Exp).then_inc(act_done, 1)

            def sines():
                act.wait_ge(dve_done, at("dve", "angle"))
                nc.scalar.activation(sin_a, sin_a, ACT.Sin)
                nc.scalar.activation(cos_a, cos_a, ACT.Sin).then_inc(act_done, 1)

            def f_ln(l):
                act.wait_ge(dve_done, at("dve", "f_abs", l))
                step(nc.scalar.activation(hg[1], hg[1], ACT.Exp))
                ins = nc.scalar.activation(hg[1], hg[1], ACT.Ln, bias=cst("one"))
                if l:
                    step(nc.scalar.activation(lbn, lbn, ACT.Exp))
                    ins = nc.scalar.activation(lbn, lbn, ACT.Ln, bias=cst("one"))
                ins.then_inc(act_done, 1)

            def f_ln2(l):
                act.wait_ge(dve_done, at("dve", "f_log", l))
                step(nc.scalar.activation(hg[2], hg[2], ACT.Exp))
                nc.scalar.activation(hg[2], hg[2], ACT.Ln, bias=cst("one")).then_inc(act_done, 1)

            def k_gate(l):
                act.wait_ge(dve_done, at("dve", "f_log2" if l else "f_log", l))
                nc.scalar.activation(k_g, k_g, ACT.Exp).then_inc(act_done, 1)

            def decay_f(l, v):
                act.wait_ge(dve_done, at("dve", "gap_f", l, v))
                nc.scalar.activation(dec_f[v % 2], dec_f[v % 2], ACT.Exp).then_inc(act_done, 1)

            steps("act", {"split_hi": split_hi, "ffn": ffn, "wab_hi": wab_hi, "sumsq": sumsq_, "rstd": rstd_, "x_hi": x_hi,
                          "evacuate": evacuate, "logs": logs_and_exps, "tap": tap, "conv_silu": conv_silu, "ab_exp": ab_exp, "softplus": softplus,
                          "decay": decay, "pow2_n": pow2_n, "pow4_n": pow4_n, "pow8_a": pow8_a, "t_rows": t_rows, "y": y,
                          "v_new": v_new_, "state_copy": state_copy, "cn_sq": cn_sq, "cn_rstd": cn_rstd, "exp": exp_,
                          "p_cols": p_cols, "lam_exp": lam_exp, "sines": sines, "f_ln": f_ln, "f_ln2": f_ln2,
                          "k_gate": k_gate, "decay_f": decay_f})

        @block.vector
        def _(dve):
            chained = [0]

            def step(ins):
                chained[0] += 1
                ins.then_inc(dve_chain, 1)
                dve.wait_ge(dve_chain, chained[0])

            tt = nc.vector.tensor_tensor
            ts = nc.vector.tensor_scalar
            stt = nc.vector.scalar_tensor_tensor

            def finish(ins):
                finished[0] += 1
                ins.then_inc(dve_done, 1)
                dve.wait_ge(dve_done, finished[0])

            finished = [0]

            def split_lo(n, j=None, step_=0):
                s = n % SLOTS
                dve.wait_ge(panel_hi, of(j, n + 1, step_))
                tt(w_lo[:, s], raw[:, s], w_hi[:, s].bitcast(F32), ALU.subtract).then_inc(panel_lo, 1)

            def ffn(f):
                b, c = BASE[f"ffn{f}"], f * UPS

                def gate_up(i, j=None):
                    n = b + (0 if i == 0 else 3 * i - 1)
                    split_lo(n + 3, j, 6)
                    dve.wait_ge(silu_done, of(j, c + i + 1, 2))
                    if c + i:
                        dve.wait_ge(gate_ready, of(j, c + i, 2))
                    tt(g32, silu_buf, ps[:, 5], ALU.mult).then_inc(gate_read, 1)
                    dve.wait_ge(gate_read, of(j, c + i + 1, 2))
                    nc.vector.tensor_copy(g_hi[:, i % 2], grid(g32, 2)).then_inc(gate_hi, 1)
                    dve.wait_ge(gate_hi, of(j, c + i + 1, 2))
                    tt(g_lo[:, i % 2], grid(g32, 2), g_hi[:, i % 2].bitcast(F32), ALU.subtract).then_inc(gate_ready, 1)
                    split_lo(n + 4, j, 6)

                def down_of(i, j=None):
                    split_lo(b + (3 * i + 4 if i < UPS - 1 else 3 * UPS - 1) + 3, j, 6)

                gate_up(0)
                gate_up(1)
                down_of(0)
                with dve.Fori(0, (UPS - 3) // 2) as j:
                    for i in (2, 3):
                        gate_up(i, j)
                        down_of(i - 1, j)
                gate_up(UPS - 1)
                down_of(UPS - 2)

            def wab_lo():
                dve.wait_ge(act_done, at("act", "wab_hi"))
                finish(tt(wab_l[:], sm("wab", 0, 64), wab_h[:].bitcast(F32), ALU.subtract))

            def residual(name, t):
                if t == 0:
                    dve.wait_ge(tile_ready, DOWNS.index(name) + 1)
                else:
                    dve.wait_ge(panel_used, BASE[name] + N_OF[name])
                if name == "ffn0":
                    dve.wait_ge(loaded["x"], 16)
                k = 0.5 if name.startswith("ffn") else 1.0
                finish(stt(x[:, t], both_banks(t), k, x[:, t], ALU.mult, ALU.add))

            def scale(tag, t, half):
                src, _ = source_of(tag, t)
                dve.wait_ge(act_done, at("act", "rstd", tag, t))
                dve.wait_ge(loaded["gain_" + tag], 16)
                to = x if tag == "final" else xn_rows
                c = slice(512 * half, 512 * half + 512)
                finish(stt(to[:, t, c], src[:, t, c], rstd[:, t:t + 1], gain[:, c], ALU.mult, ALU.mult))

            def x_lo(tag, t, half):
                dve.wait_ge(act_done, at("act", "x_hi", tag, t, half))
                b, c = slice(4 * half, 4 * half + 4), slice(P * t, P * t + P)
                finish(tt(act_lo[:, b, c], grid(ps[:, 2 * t + half], 4), act_hi[:, b, c].bitcast(F32), ALU.subtract))

            def conv(p):
                dve.wait_ge(act_done, at("act", "tap", p))
                for k in (2, 1, 0):
                    for i in range(2):
                        b = 2 * p + i
                        ins = stt(conv_out(b), raw_qkv[:, b, 1 + k:1 + k + SEQ], sm("conv", 4 * b + k), conv_out(b), ALU.mult, ALU.add)
                    (step if k else finish)(ins)

            def ab():
                dve.wait_ge(act_done, at("act", "ab_exp"))
                step(ts(b_exp, b_exp, 1.0, None, ALU.add))
                nc.vector.reciprocal(beta, b_exp)
                step(tt(grid(xa, 2), grid(ps[:, 6, 0:16], 2)[:, :, 4:8], spread(sm("dt", 0, 4), 2), ALU.add))
                step(ts(e_sp, xa, -1.0, None, ALU.mult))
                finish(tt(e_sp, xa, e_sp, ALU.min))

            def g():
                dve.wait_ge(act_done, at("act", "softplus"))
                step(stt(g_col, xa, 0.0, e_sp, ALU.max, ALU.add))
                finish(stt(grid(g_col, 2), grid(g_col, 2), -1.0, spread(e_alog, 2), ALU.mult, ALU.mult))

            def gc_():
                dve.wait_ge(pe_done, at("pe", "cumsum"))
                step(nc.vector.tensor_copy(gc, ps[:, 6, 0:8]))
                finish(tt(e_kd.rearrange("p (a b) -> p a b", b=1), grid(ps[:, 2], 4)[:, :, P - 1:P], gc[:, 0:4].rearrange("p (a b) -> p a b", b=1),
                          ALU.subtract))

            def gap(t):
                step(tt(decay_t[:, t], grid(ps[:, 2 + t], 4), along(gc[:, 4 * t:4 * t + 4], P), ALU.subtract))
                step(ts(a_low[:, t], decay_t[:, t], 0.0, None, ALU.max))
                finish(ts(decay_t[:, t], decay_t[:, t], 0.0, None, ALU.min))

            def decay_mask(t):
                dve.wait_ge(act_done, at("act", "decay", t))
                tt(decay_t[:, t], decay_t[:, t], spread(tab(1, "upper"), 4), ALU.mult)
                step(tt(a_low[:, t], a_low[:, t], spread(tab(1, "strict"), 4), ALU.mult))
                if t:
                    tt(bge[:, 0:4], beta[:, 4:8], e_gc[:, 4:8], ALU.mult)
                finish(tt(a_low[:, t], a_low[:, t], along(beta[:, 4 * t:4 * t + 4], P), ALU.mult))

            def q_decayed():
                finish(tt(q_dec, q_dec, qk[:, 0:4, P:SEQ], ALU.mult))

            def v_beta_(t):
                dve.wait_ge(pe_done, at("pe", "turn_v", t))
                finish(tt(v_beta[:, t], grid(ps[:, 6 + t], 4), along(beta[:, 4 * t:4 * t + 4], P), ALU.mult))

            def k_decayed():
                dve.wait_ge(pe_done, at("pe", "turn_k"))
                finish(tt(k_dec, grid(ps[:, 6], 4), along(e_kd, P), ALU.mult))

            def a_low_(t):
                dve.wait_ge(pe_done, at("pe", "kk", t))
                finish(tt(a_low[:, t], a_low[:, t], grid(ps[:, 3 * t], 4), ALU.mult))

            def base16(t):
                dve.wait_ge(pe_done, at("pe", "turn_a", t))
                m16 = spread(tab(1, "diag16"), 4)
                step(tt(t_mat[:, t], grid(ps[:, 3 * t + 1], 4), m16, ALU.mult))
                tt(pw_a4[:, t], a_low[:, t], m16, ALU.mult)
                finish(tt(m_mat[:, t], spread(ident, 4), t_mat[:, t], ALU.subtract))

            def add_to(to, bank, op=ALU.add):
                return tt(to, to, grid(ps[:, bank], 4), op)

            def pow2_a(t):
                dve.wait_ge(pe_done, at("pe", "pow2", t))
                finish(nc.vector.tensor_copy(pw_a[:, t], grid(ps[:, 3 * t + 1], 4)))

            def pow4_a(t):
                dve.wait_ge(pe_done, at("pe", "pow4", t))
                nc.vector.tensor_copy(pw_a4[:, t], grid(ps[:, 3 * t + 1], 4))
                finish(add_to(m_mat[:, t], 3 * t + 2))

            def pow8_m(t):
                dve.wait_ge(pe_done, at("pe", "pow8", t))
                finish(add_to(m_mat[:, t], 3 * t + 2))

            def pow16_m(t):
                dve.wait_ge(pe_done, at("pe", "pow16", t))
                finish(add_to(m_mat[:, t], 3 * t + 2))

            def qk_decay(t):
                dve.wait_ge(pe_done, at("pe", "kq", t))
                finish(tt(decay_t[:, t], decay_t[:, t], grid(ps[:, 6 + t], 4), ALU.mult))

            def corner(s, t):
                dve.wait_ge(pe_done, at("pe", "double", s - 1, t) if s else at("pe", "turn_m", t))
                finish(tt(pw_n[:, t], a_low[:, t], spread(tab(1, ("e16", "e32", "e64")[s]), 4), ALU.mult))

            def doubled(s, t):
                dve.wait_ge(pe_done, at("pe", "double", s, t))
                if s < 2:
                    add_to(t_mat[:, t], 3 * t + 2, ALU.subtract)
                finish(add_to(m_mat[:, t], 3 * t + 1, ALU.subtract))

            def v_less():
                dve.wait_ge(pe_done, at("pe", "from_state"))
                tmp = grid(xn[:, 0:512], 4)
                step(tt(tmp, grid(ps[:, 3], 4), along(bge[:, 0:4], P), ALU.mult))
                finish(tt(v_beta[:, 1], v_beta[:, 1], tmp, ALU.subtract))

            def ret_decay(h):
                dve.wait_ge(pe_done, at("pe", "ret_scores", h))
                a, _ = PLACES[1]["ret"]
                finish(tt(ret_p[:, h], ps[:, 4 + h % 2, 0:384], table[:, a + 384 * h:a + 384 * h + 384], ALU.mult))

            def rope(unit):
                values, _, cos, sin, _ = ropes[unit]
                i = rope_index[unit]
                dve.wait_ge(pe_done, at("pe", "swap", unit))
                if unit[0].startswith("rp"):
                    dve.wait_ge(act_done, at("act", "sines"))
                tmp = grid(xn[:, 512:1024], 2)
                step(tt(tmp, grid(ps[:, 6 + i % 2], 2), spread(sin, 2), ALU.mult))
                step(tt(values, values, spread(cos, 2), ALU.mult))
                finish(tt(values, values, tmp, ALU.add))

            def split_out(b):
                step(nc.vector.tensor_copy(act_hi[:, b:b + 2], grid(y32, 2)))
                finish(tt(act_lo[:, b:b + 2], grid(y32, 2), act_hi[:, b:b + 2].bitcast(F32), ALU.subtract))

            def cn_use(unit):
                src, _, _, k, to, gate, b, _, _ = norms[unit]
                dve.wait_ge(act_done, at("act", "cn_rstd", unit))
                r = grid(rs[norm_index[unit] % 2], 2)
                if to is not None:
                    finish(stt(to, src, k, r, ALU.mult, ALU.mult))
                    return
                step(stt(grid(y32, 2), src, k, r, ALU.mult, ALU.mult))
                if gate is not None:
                    step(tt(grid(y32, 2), grid(y32, 2), gate, ALU.mult))
                split_out(b)

            def gate_out(unit):
                gate, b, last = gates[unit]
                dve.wait_ge(pe_done, at("pe", "attend", last))
                src = grid(ps[:, 6 + unit[1]], 2)
                if gate is None:
                    step(nc.vector.tensor_copy(grid(y32, 2), src))
                else:
                    step(tt(grid(y32, 2), src, gate, ALU.mult))
                split_out(b)

            def mask_max(unit):
                maps, _, _, full, mask, _, k, _ = atts[unit]
                i = att_index[unit]
                dve.wait_ge(pe_done, at("pe", "scores", unit))
                if i >= 2:
                    dve.wait_ge(pe_done, at("pe", "turn_p", att_list[i - 2]))
                for m in range(len(maps)):
                    for q, (a, b) in enumerate(spans(full)):
                        to, s = probs[:, i % 2, m, a:b], ps[:, 2 * (i % 2) + m, a:b]
                        low = nmax[i % 2][:, 2 * m + q:2 * m + q + 1]
                        if full:
                            ins = ts(to, s, -k, None, ALU.mult, ALU.min, accum_out=low)
                        else:
                            ins = nc.vector.tensor_tensor_reduce(to, s, mask[:, a:b], -k, 3e38, ALU.add, ALU.min, low)
                finish(ins)

            def divide(unit):
                maps, _, _, full, _, times, _, _ = atts[unit]
                i = att_index[unit]
                p, den = probs[:, i % 2], dens[i % 2]
                dve.wait_ge(act_done, at("act", "exp", unit))
                if times is not None:
                    for q, (a, b) in enumerate(spans(full)):
                        ins = nc.vector.tensor_tensor_reduce(p[:, 0, a:b], p[:, 0, a:b], times[:, a:b], 1.0, 0.0, ALU.mult, ALU.add,
                                                             den[:, q:q + 1])
                    step(ins)
                step(nc.vector.reciprocal(den[:, 0:2 * len(maps)], den[:, 0:2 * len(maps)]))
                if len(maps) == 2:
                    step(ts(den[:, 2:4], den[:, 2:4], lam_c[:, 3:4], None, ALU.mult))
                for q, (a, b) in enumerate(spans(full)):
                    ins = ts(p[:, 0, a:b], p[:, 0, a:b], den[:, q:q + 1], None, ALU.mult)
                if len(maps) == 2:
                    step(ins)
                    for q, (a, b) in enumerate(spans(full)):
                        ins = stt(p[:, 0, a:b], p[:, 1, a:b], den[:, 2 + q:3 + q], p[:, 0, a:b], ALU.mult, ALU.add)
                finish(ins)

            def lam_mul():
                v = sm("lam", 0, 4)[0:64, :]
                step(tt(lam_c[0:64, 0:2], v[:, 0:2], v[:, 2:4], ALU.mult))
                finish(ts(dgain, sm("diff"), 1.0 - LAMBDA_INIT, None, ALU.mult))

            def lam():
                dve.wait_ge(act_done, at("act", "lam_exp"))
                step(tt(lam_c[:, 3:4], lam_c[:, 3:4], lam_c[:, 2:3], ALU.subtract))
                finish(ts(lam_c[:, 3:4], lam_c[:, 3:4], LAMBDA_INIT, None, ALU.subtract))

            def angle():
                dve.wait_ge(loaded["pos"], 16)
                dve.wait_ge(loaded["tab3"], 16)
                step(nc.vector.tensor_copy(ang, positions))
                step(ts(ang, ang, tab(3, "freq"), None, ALU.mult))
                for to, quarter in ((sin_a, 0.0), (cos_a, 0.25)):
                    step(ts(turns, ang, 1 / (2 * math.pi), quarter, ALU.mult, ALU.add))
                    step(ts(turns, turns, MAGIC, None, ALU.add))
                    step(ts(turns, turns, MAGIC, None, ALU.subtract))
                    step(stt(to, turns, -TWO_PI[0], ang, ALU.mult, ALU.add))
                    step(stt(to, turns, -TWO_PI[1], to, ALU.mult, ALU.add))
                    step(stt(to, turns, -TWO_PI[2], to, ALU.mult, ALU.add))
                    if quarter:
                        step(ts(to, to, math.pi / 2, None, ALU.add))
                    ins = ts(to, to, -PI_IN, PI_IN, ALU.max, ALU.min)
                    (finish if quarter else step)(ins)

            def f_abs(l):
                dve.wait_ge(act_done, at("act", "evacuate", f"in2_{l}", 9))
                dve.wait_ge(pe_done, at("pe", "attend", (f"matt{l}", 3)))
                step(ts(hg[1], fh, -1.0, None, ALU.mult))
                step(tt(hg[1], fh, hg[1], ALU.min))
                if l:
                    a, b = sm("lb", 0, 4), sm("lb", 4, 4)
                    tt(lbd[:, 0:4], b, a, ALU.subtract)
                    step(tt(lbd[:, 4:8], a, b, ALU.subtract))
                    step(tt(lbn[:, 0:4], lbd[:, 0:4], lbd[:, 4:8], ALU.min))
                    step(tt(lbn[:, 4:8], lbd[:, 0:4], lbd[:, 4:8], ALU.min))
                finish(nc.vector.memset(zero4, 0.0))

            def f_log(l):
                dve.wait_ge(act_done, at("act", "f_ln", l))
                step(stt(hg[1], fh, 0.0, hg[1], ALU.min, ALU.subtract))
                if l:
                    step(stt(lbl, lbd, 0.0, lbn, ALU.min, ALU.subtract))
                    step(tt(hg[1], hg[1], along(lbl[:, 4:8], SEQ), ALU.add))
                    step(tt(hg[2], hg[1], along(lbl[:, 0:4], SEQ), ALU.subtract))
                    step(ts(hg[3], hg[2], -1.0, None, ALU.mult))
                    step(tt(hg[2], hg[2], hg[3], ALU.min))
                finish(tt(k_g, hg[1], fh, ALU.subtract))

            def f_log2(l):
                dve.wait_ge(act_done, at("act", "f_ln2", l))
                step(tt(hg[1], hg[1], along(lbl[:, 0:4], SEQ), ALU.max))
                finish(tt(hg[1], hg[1], hg[2], ALU.add))

            def cum_f(l):
                for h in range(4):
                    ins = nc.vector.tensor_tensor_scan(fh[:, h], tab(3, "keep"), hg[1][:, h], 0.0, ALU.mult, ALU.add)
                finish(ins)

            def diagonal_in(l):
                dve.wait_ge(pe_done, at("pe", "diagonal", l))
                for t in range(TILES):
                    ins = tt(h_s[:, t], grid(ps[:, 4 + t], 4), spread(ident, 4), ALU.mult)
                finish(ins)

            def gap_f(l, v):
                if v >= 2:
                    dve.wait_ge(pool_done, at("pool", "k_level", l, v - 2))
                to = dec_f[v % 2]
                if v < 7:
                    b = 64 >> v
                    split = lambda r: r.rearrange("p h (n c) -> p (h n) c", c=2 * b)
                    a_, t_ = split(fh), split(to)
                    edge = a_[:, :, b - 1:b].broadcast_to([P, 4 * SEQ // (2 * b), b])
                    tt(t_[:, :, b:2 * b], a_[:, :, b:2 * b], edge, ALU.subtract)
                    finish(tt(t_[:, :, 0:b], edge, a_[:, :, 0:b], ALU.subtract))
                else:
                    tt(to[:, :, 0:P], fh[:, :, P - 1:P].broadcast_to([P, 4, P]), fh[:, :, 0:P], ALU.subtract)
                    finish(nc.vector.tensor_copy(to[:, :, P:SEQ], fh[:, :, P:SEQ]))

            def q_level(l, v):
                dve.wait_ge(act_done, at("act", "decay_f", l, v))
                if v >= 2:
                    dve.wait_ge(pe_done, at("pe", "level", l, v - 2))
                finish(tt(q_l[v % 2], qh, dec_f[v % 2], ALU.mult))

            def level_in(l, v):
                dve.wait_ge(pe_done, at("pe", "level", l, v))
                if v < 7:
                    a, _ = PLACES[3]["levels"]
                    mask = spread(table[:, a + P * v:a + P * v + P], 4)
                    for t in range(TILES):
                        ins = nc.vector.copy_predicated(h_s[:, t], mask.bitcast(U32), grid(ps[:, 2 * (v % 2) + t], 4))
                else:
                    ins = nc.vector.tensor_copy(h_s01, grid(ps[:, 2], 4))
                finish(ins)

            steps("dve", {"split_lo": split_lo, "ffn": ffn, "wab_lo": wab_lo, "residual": residual, "scale": scale, "x_lo": x_lo,
                          "conv": conv, "ab": ab, "g": g, "gc": gc_, "gap": gap, "decay_mask": decay_mask, "q_decayed": q_decayed,
                          "v_beta": v_beta_, "k_decayed": k_decayed, "a_low": a_low_, "base16": base16, "pow2_a": pow2_a,
                          "pow4_a": pow4_a, "pow8_m": pow8_m, "pow16_m": pow16_m, "qk_decay": qk_decay, "corner": corner,
                          "doubled": doubled, "v_less": v_less, "ret_decay": ret_decay, "rope": rope, "cn_use": cn_use,
                          "gate_out": gate_out, "mask_max": mask_max, "divide": divide, "lam_mul": lam_mul, "lam": lam,
                          "angle": angle, "f_abs": f_abs, "f_log": f_log, "f_log2": f_log2, "cum_f": cum_f,
                          "diagonal_in": diagonal_in, "gap_f": gap_f, "q_level": q_level, "level_in": level_in})


def kernel(**inputs):
    import concourse.bacc as bacc
    from concourse.bass_utils import run_bass_kernel_spmd as run

    a = {k: np.asarray(v) for k, v in inputs.items()}

    def up(w, cols):
        return [w[:, c:c + UPW].reshape(DC, P, UPW).transpose(1, 0, 2).reshape(P, PANEL) for c in cols]

    def down(w):
        return [w[r:r + 2 * P].reshape(2, P, D).transpose(1, 0, 2).reshape(P, PANEL) for r in range(0, w.shape[0], 2 * P)]

    def ffn(name):
        w = a[name + "_w_up"]
        gate, upper = up(w, range(0, D_FF, UPW)), up(w, range(D_FF, 2 * D_FF, UPW))
        low = down(a[name + "_w_down"])
        order = [gate[0], upper[0]]
        for i in range(1, UPS):
            order += [gate[i], upper[i], low[i - 1]]
        return order + [low[-1]]

    in0 = list(range(0, 2048, UPW)) + list(range(2056, 3592, UPW))
    stream = ffn("l0_ffn1") + up(a["l0_w_in"], in0) + down(a["l0_w_out"]) + ffn("l0_ffn2")
    stream += ffn("l1_ffn1") + up(a["l1_w_in"], range(0, 3072, UPW)) + down(a["l1_w_out"]) + ffn("l1_ffn2")
    for l in range(2):
        stream += up(a["w_mem_kv_2"][l], range(0, D, UPW)) + up(a["w_in_2"][l], range(0, 5120, UPW)) + down(a["w_out_2"][l])
    panels = np.stack(stream)
    gains = np.stack([a["l0_ffn1_norm"], a["l0_mix_norm"], a["l0_ffn2_norm"], a["l1_ffn1_norm"], a["l1_mix_norm"],
                      a["l1_ffn2_norm"], a["final_norm"], a["mem_norm_g_2"][0], a["norm_g_2"][0], a["mem_norm_g_2"][1],
                      a["norm_g_2"][1]])
    small = np.zeros((P, SMALL_W), np.float32)

    def put(name, v):
        at_, n = SMALL[name]
        small[:v.shape[0], at_:at_ + n] = v

    put("conv", a["l0_conv_w"].reshape(4, 12, P).transpose(2, 1, 0).reshape(P, 48))
    put("wab", a["l0_w_in"][:, 2048:2056].reshape(DC, P, 8).transpose(1, 0, 2).reshape(P, 64))
    put("alog", np.broadcast_to(a["l0_a_log"], (P, 4)))
    put("dt", np.broadcast_to(a["l0_dt_bias"], (P, 4)))
    put("gdn", a["l0_gdn_norm"][:, None])
    put("diff", a["l1_diff_norm"][:, None])
    put("lam", np.stack([a["l1_lambda_q1"], a["l1_lambda_q2"], a["l1_lambda_k1"], a["l1_lambda_k2"]], axis=1))
    put("lb", a["hgrn_lb_logits_2"].reshape(2, 4, P).transpose(2, 0, 1).reshape(P, 8))
    for l in range(2):
        put(f"mq{l}", np.tile(a["moba_q_norm_2"][l], 2)[:, None])
        put(f"mk{l}", np.tile(a["moba_k_norm_2"][l], 2)[:, None])
        put(f"sq{l}", a["mem_q_norm_2"][l][:, None])
        put(f"sk{l}", a["mem_k_norm_2"][l][:, None])
        put(f"ho{l}", a["hgrn_o_norm_2"][l][:, None])

    def tiles(v):
        return np.ascontiguousarray(v.reshape(TILES, P, D).transpose(1, 0, 2))

    arrays = {"x_in": tiles(a["x"]), "mem_in": tiles(a["mem_2"]), "pos_in": np.ascontiguousarray(a["positions_2"].reshape(SEQ)),
              "panels": panels, "gains": gains, "small_in": small}
    arrays.update({f"tab{i}": t for i, t in enumerate(TABLES)})
    nc = bacc.Bacc("TRN2", target_bir_lowering=False, num_devices=1)
    aps = {k: nc.dram_tensor(k, v.shape, mybir.dt.from_np(v.dtype), kind="ExternalInput").ap() for k, v in arrays.items()}
    out = nc.dram_tensor("out", (P, TILES, D), F32, kind="ExternalOutput").ap()
    build(nc, **aps, out=out)
    r = run(nc, [arrays], core_ids=[0])
    got = np.asarray(r.results[0]["out"])
    return got.transpose(1, 0, 2).reshape(1, SEQ, D)
```

```python
import math
from contextlib import ExitStack

import numpy as np

import concourse.bass as bass
from concourse import mybir

F32 = mybir.dt.float32
F32R = mybir.dt.float32r
I32 = mybir.dt.int32
U32 = mybir.dt.uint32
ALU = mybir.AluOpType
ACT = mybir.ActivationFunctionType
AX = mybir.AxisListType.X

P = 128
SEQ = 256
TILES = SEQ // P
D = 1024
DC = D // P
D_FF = 2816
UPW = 256
UPS = D_FF // UPW
PANEL = DC * UPW
SLOTS = 3
EPS = 1e-6
LAMBDA_INIT = 0.8 - 0.6 * math.exp(-0.3)
MAGIC = 12582912.0
TWO_PI = (6.28125, 0.0019354820251464844, -1.7484556025237907e-07)
PI_IN = 3.1415925
WORK = 15408

COUNTS = [("ffn0", 3 * UPS), ("in0", 14), ("out0", 4), ("ffn1", 3 * UPS), ("ffn2", 3 * UPS),
          ("in1", 12), ("out1", 4), ("ffn3", 3 * UPS), ("mem0", 4), ("in2_0", 20), ("out2_0", 6),
          ("mem1", 4), ("in2_1", 20), ("out2_1", 6)]
BASE = {}
PANELS = 0
for _name, _n in COUNTS:
    BASE[_name] = PANELS
    PANELS += _n
N_OF = dict(COUNTS)

GAINS = ["ffn0", "mix0", "ffn1", "ffn2", "mix1", "ffn3", "mem0", "final", "pre0", "mem1", "pre1"]

SMALL = {}
_at = 0
for _name, _n in [("conv", 48), ("wab", 64), ("alog", 4), ("dt", 4), ("gdn", 1), ("diff", 1), ("lam", 4),
                  ("lb", 8), ("mq0", 1), ("mk0", 1), ("sq0", 1), ("sk0", 1), ("ho0", 1),
                  ("mq1", 1), ("mk1", 1), ("sq1", 1), ("sk1", 1), ("ho1", 1)]:
    SMALL[_name] = (_at, _n)
    _at += _n
SMALL_W = _at


def tables():
    i = np.arange(P)
    part, free = i[:, None], i[None, :]
    f = np.float32
    upper = (part <= free).astype(f)
    strict_low = (part > free).astype(f)

    def swap(n, half, signs=True, width=None):
        m = np.zeros((P, P), f)
        for g in range(0, P, n):
            for d in range(half):
                m[g + d + half, g + d] = -1.0
                m[g + d, g + d + half] = 1.0
        return m

    def rope(dim):
        inv = (np.float32(10000.0) ** (-np.arange(0, dim, 2, dtype=f) / f(dim))).astype(f)
        ang = (np.arange(SEQ, dtype=f)[None, :] * inv[:, None]).astype(f)
        reps = P // (dim // 2)
        return np.tile(np.cos(ang), (reps, 1)).astype(f), np.tile(np.sin(ang), (reps, 1)).astype(f)

    q0 = part - free
    q1 = part + P - np.arange(SEQ)[None, :]
    dist = np.concatenate([q0, q1], axis=1)
    causal = np.where(dist >= 0, 0.0, -1e38).astype(f)
    times = ((dist >= 0) & (dist <= 128)).astype(f)
    for r in (4, 16):
        times = times + ((dist >= 0) & (dist % r == 0)).astype(f)
    union = np.where(times > 0, 0.0, -1e38).astype(f)
    rel = np.concatenate([np.arange(SEQ)[None, :] - part, free - part], axis=1).astype(np.float64)
    ret = [np.where(rel >= 0, np.exp(np.maximum(rel, 0) * math.log(1 - 2.0 ** (-5 - h))), 0.0) * 0.125
           for h in range(4)]
    cos64, sin64 = rope(64)
    cos128, sin128 = rope(128)
    diag16 = (part // 16 == free // 16).astype(f)

    def below(b):
        return ((part // (2 * b) == free // (2 * b)) & (part % (2 * b) >= b) & (free % (2 * b) < b)).astype(f)

    levels = [((part // (2 * b) == free // (2 * b)) & (part % (2 * b) < b) & (free % (2 * b) >= b)).astype(f)
              for b in (64, 32, 16, 8, 4, 2, 1)]
    keep = np.ones((P, SEQ), f)
    keep[:, ::P] = 0
    half = 8
    inv2 = (f(500000.0) ** (-np.arange(half, dtype=f) / f(half))).astype(f)
    freq = np.zeros((P, 1), f)
    for g in (0, 64):
        freq[g:g + half, 0] = inv2
        freq[g + half:g + 2 * half, 0] = inv2
    sets = [
        [("ident", np.eye(P)), ("ones", np.ones((P, P))), ("ones64", part // 64 == free // 64),
         ("eps", np.full((P, 1), EPS)), ("one", np.ones((P, 1)))],
        [("upper", upper), ("strict", strict_low), ("diag16", diag16), ("e16", below(16)), ("e32", below(32)),
         ("e64", below(64)), ("ret", np.concatenate(ret, axis=1)), ("cos64", cos64), ("sin64", sin64),
         ("swap64", swap(64, 32))],
        [("causal", causal), ("times", times), ("union", union), ("cos64", cos64), ("sin64", sin64),
         ("swap64", swap(64, 32)), ("cos128", cos128), ("sin128", sin128), ("swap128", swap(128, 64))],
        [("causal", causal), ("swapp", swap(64, 8)), ("levels", np.concatenate(levels, axis=1)),
         ("keep", keep), ("freq", freq)],
    ]
    arrays, places = [], []
    for s in sets:
        where, at_ = {}, 0
        for name, a in s:
            where[name] = (at_, a.shape[1])
            at_ += a.shape[1]
        arrays.append(np.ascontiguousarray(np.concatenate([np.asarray(a, f) for _, a in s], axis=1)))
        places.append(where)
    return arrays, places


TABLES, PLACES = tables()
TABLE_W = max(t.shape[1] for t in TABLES[1:])

RESIDUALS = {"mix0": "ffn0", "ffn1": "out0", "ffn2": "ffn1", "mix1": "ffn2", "ffn3": "out1", "final": "ffn3",
             "pre1": "out2_0", "end": "out2_1"}
DOWNS = list(RESIDUALS.values())
LATE = {name: (BASE[name] + N_OF[name] + SLOTS - 1, min(BASE[name] + N_OF[name] + SLOTS, PANELS)) for name in DOWNS}
UNCOUNTED = {"ffn_down", "logs", "split_hi", "split_lo", "ffn", "panel", "load", "store"}


def rounds(steps, units):
    return [[(engine, kind, (units[r - lag],)) for engine, kind, lag in steps if 0 <= r - lag < len(units)]
            for r in range(len(units) + max(lag for _, _, lag in steps))]


def lagged(steps, units):
    return sum(rounds(steps, units), [])


def merge(*chains):
    return [sum((c[i] for c in chains if i < len(c)), []) for i in range(max(map(len, chains)))]


def weave(chain, panels, every=1):
    out, rest, panels = [], [], list(panels)
    for i, r in enumerate(chain):
        out += r + rest
        rest = []
        if i % every == every - 1 and panels:
            first, *rest = panels.pop(0)
            out.append(first)
    return out + rest + sum(panels, [])


NORM_COLS = [("pe", "cn_sum", 1), ("act", "cn_rstd", 1), ("act", "cn_sq", 0), ("dve", "cn_use", 1)]
ATTEND = [("pe", "turn_p", 2), ("pe", "attend", 3), ("pe", "scores", 0), ("act", "p_cols", 2), ("dve", "divide", 1),
          ("dve", "mask_max", 0), ("act", "exp", 0)]
ROPE = [("pe", "swap", 0), ("dve", "rope", 0)]
NORM_ROPE = NORM_COLS + [("pe", "swap", 2), ("dve", "rope", 2)]


def next_gain(tag):
    i = GAINS.index(tag) + 1
    if tag == "mix0":
        return []
    return [("pool", "load", ("gain_" + GAINS[i],))] if i < len(GAINS) else []


def norm_steps(tag):
    out = [("act", "logs", ())]
    before = RESIDUALS.get(tag) if tag != "pre1" else None
    for t in range(TILES):
        out += [("dve", "residual", (before, t))] if before else []
        out += [("act", "sumsq", (tag, t)), ("act", "rstd", (tag, t))]
    for t in range(TILES):
        for half in range(2):
            out += [(e, k, (tag, t, half)) for e, k in (("dve", "scale"), ("pe", "turn_x"))]
    for t in range(TILES):
        for half in range(2):
            out += [("act", "x_hi", (tag, t, half)), ("dve", "x_lo", (tag, t, half))]
    for n in range(*LATE.get(before, (0, 0))):
        out += [("act", "split_hi", (n,)), ("dve", "split_lo", (n,))]
    return out + next_gain(tag)


def panel_steps(name, extra=None, start=0, stop=None):
    return sum(panel_list(name, extra, start, stop), [])


def panel_list(name, extra=None, start=0, stop=None):
    all_ = []
    for k in range(start, N_OF[name] if stop is None else stop):
        out = []
        all_.append(out)
        n = BASE[name] + k
        out.append(("pe", "panel", (name, k)))
        if not name.startswith("out"):
            out.append(("act", "evacuate", (name, k)))
        late = LATE.get(name, (0, 0))
        if n + SLOTS < PANELS and not late[0] <= n + SLOTS < late[1]:
            out += [("act", "split_hi", (n + SLOTS,)), ("dve", "split_lo", (n + SLOTS,))]
        out += (extra or {}).get(k, [])
    return all_


def ffn_tail(f):
    return [("pe", "ffn_down", (f, UPS - 2))] + splits(BASE[f"ffn{f}"] + N_OF["ffn0"] + 1) + [("pe", "ffn_down", (f, UPS - 1))]


def ffn_steps(f):
    return norm_steps(f"ffn{f}") + [(e, "ffn", (f,)) for e in ("pe", "act", "dve")]


def delta_rounds():
    both = lambda *steps: [(e, k, (*a, t)) for t in range(TILES) for e, k, *a in steps]
    out = [[("act", "softplus", ()), ("dve", "g", ())]]
    out += merge([[("pe", "cumsum", ())]], rounds(NORM_COLS, [("dq", 0), ("dq", 1), ("dk", 0), ("dk", 1)]))
    out += [[("dve", "gc", ())] + both(("dve", "gap"), ("act", "decay")) + both(("dve", "decay_mask")) + [("dve", "q_decayed", ())],
            [("pe", "turn_v", (0,)), ("pe", "turn_v", (1,)), ("dve", "v_beta", (0,)), ("dve", "v_beta", (1,)),
             ("pe", "turn_k", ()), ("dve", "k_decayed", ())],
            both(("pe", "kq"), ("dve", "qk_decay")),
            both(("pe", "kk"), ("dve", "a_low")), both(("pe", "turn_a"), ("dve", "base16")),
            both(("pe", "pow2"), ("act", "pow2_n"), ("dve", "pow2_a")), both(("pe", "pow4"), ("act", "pow4_n"), ("dve", "pow4_a")),
            both(("pe", "pow8"), ("act", "pow8_a"), ("dve", "pow8_m")), both(("pe", "pow16"), ("dve", "pow16_m")),
            both(("pe", "turn_m"), ("act", "t_rows"), ("dve", "corner", 0))]
    for s in range(3):
        out += [both(("pe", "double_y", s), ("act", "y", s)),
                both(("pe", "double", s), ("dve", "doubled", s), *([("dve", "corner", s + 1)] if s < 2 else []))]
    return out


def delta_end():
    return [[("pe", "u", (0,)), ("act", "v_new", (0,))], [("pe", "state", ()), ("act", "state_copy", ())],
            [("pe", "from_state", ()), ("dve", "v_less", ())], [("pe", "u", (1,)), ("act", "v_new", (1,))],
            [("pe", "delta_out", (0,))]] + merge([[("pe", "delta_out", (1,))]], rounds(NORM_COLS, [("do", 0), ("do", 1)]))


def retention_rounds():
    return (rounds(ROPE, [("r64", 0), ("r64", 1)])
            + rounds([("pe", "ret_out", 1), ("pe", "ret_scores", 0), ("dve", "ret_decay", 0)], [0, 1, 2, 3])
            + rounds(NORM_COLS, [("ro", 0), ("ro", 1)]))


def hgrn_steps(l):
    out = [("act", "k_gate", (l,)), ("dve", "cum_f", (l,)), ("pe", "diagonal", (l,)), ("dve", "diagonal_in", (l,))]
    out += [(e, k, (l, v)) for e, k, v in
            [s for r in range(8 + 2) for s in
             [("dve", "gap_f", r), ("act", "decay_f", r), ("dve", "q_level", r - 1), ("pool", "k_level", r - 1),
              ("pe", "level", r - 1), ("dve", "level_in", r - 2)] if 0 <= s[2] < 8]]
    out += [("pe", "hgrn_out", (l, g)) for g in (0, 1)]
    return out + lagged(NORM_COLS, [(f"ho{l}", 0), (f"ho{l}", 1)])


def splits(*ns):
    return [(e, k, (n,)) for n in ns for e, k in (("act", "split_hi"), ("dve", "split_lo"))]


def mem_norm(l):
    tag = f"mem{l}"
    return [("pool", "load", (tag,))] + [("act", k, (tag, t)) for t in (0, 1) for k in ("sumsq", "rstd")] + \
        [(e, k, (tag, t, half)) for t in (0, 1) for half in (0, 1) for e, k in (("dve", "scale"), ("pe", "turn_x"))] + next_gain(tag)


def split_rows(tag):
    return [s for t in (0, 1) for half in (0, 1) for s in (("act", "x_hi", (tag, t, half)), ("dve", "x_lo", (tag, t, half)))]


def order():
    out = [("pool", "load", (x,)) for x in ("x", "gain_ffn0", "const", "small", "tab1")] + [("pool", "zero", ())]
    out += [("act", "wab_hi", ()), ("dve", "wab_lo", ())] + splits(*range(SLOTS))
    out += ffn_steps(0) + ffn_tail(0)
    conv = {p + 0: [("act", "tap", (p,)), ("dve", "conv", (p,)), ("act", "conv_silu", (p,))] for p in range(6)}
    out += norm_steps("mix0") + panel_steps("in0", conv, 0, 10)
    out += [("pe", "ab_mm", ()), ("act", "logs", ()), ("act", "ab_exp", ()), ("dve", "ab", ())]
    out += weave(delta_rounds(), panel_list("in0", None, 10), 4)
    out += sum(merge(delta_end(), retention_rounds()), [])
    out += [("pool", "load", ("gain_ffn1",)), ("pool", "load", ("tab2",))] + panel_steps("out0")
    out += ffn_steps(1) + ffn_tail(1) + ffn_steps(2) + ffn_tail(2) + norm_steps("mix1") + panel_steps("in1", None, 0, 4)
    out += [("dve", "lam_mul", ()), ("pe", "lam_sum", ()), ("act", "lam_exp", ()), ("dve", "lam", ())]
    out += weave(rounds(ROPE, [("r64b", g) for g in (0, 2, 1, 3)]) + rounds(ATTEND, [("dif", h) for h in range(4)]),
                 panel_list("in1", None, 4), 1)
    out += sum(merge(rounds(NORM_COLS, [("fo", 0), ("fo", 1)]), rounds(ROPE, [("r128", g) for g in (0, 2, 1, 3)])), [])
    out += lagged(ATTEND, [("dil", h) for h in range(4)])
    out += [("dve", "gate_out", (("dil", g),)) for g in (0, 1)]
    out += [("pool", "load", ("tab3",)), ("pool", "load", ("pos",))] + panel_steps("out1")
    out += [("dve", "angle", ()), ("act", "sines", ())]
    out += ffn_steps(3) + mem_norm(0)[:5]
    product, *late, last = ffn_tail(3)
    out += mem_norm(0)[5:] + [product] + late + split_rows("mem0") + [last]
    first, *others = panel_list("mem0")
    for t in range(TILES):
        out += [("dve", "residual", ("ffn3", t)), ("act", "sumsq", ("final", t)), ("act", "rstd", ("final", t))]
    out += [("dve", "scale", ("final", t, half)) for t in (0, 1) for half in (0, 1)] + next_gain("final")
    out += splits(*range(*LATE["ffn3"])) + first
    out += [("act", k, ("pre0", t)) for t in (0, 1) for k in ("sumsq", "rstd")]
    for l in range(2):
        out += others[0] + others[1]
        out += [("dve", "scale", (f"pre{l}", t, half)) for t in (0, 1) for half in (0, 1)] + next_gain(f"pre{l}")
        out += others[2] + [("pe", "turn_x", (f"pre{l}", t, half)) for t in (0, 1) for half in (0, 1)] + split_rows(f"pre{l}")
        out += panel_steps(f"in2_{l}", None, 0, 12) + [("act", "logs", ())]
        qk = rounds(NORM_ROPE, [(f"mq{l}", 0), (f"mk{l}", 0), (f"mq{l}", 1), (f"mk{l}", 1)])
        mem_qk = rounds(NORM_COLS, [(f"sk{l}", 0), (f"sk{l}", 1), (f"sq{l}", 0), (f"sq{l}", 1)])
        heads = rounds(ATTEND, [(f"moba{l}", h) for h in range(8)] + [(f"matt{l}", h) for h in range(4)])
        gates = [[]] * 17 + [[("dve", "gate_out", ((f"moba{l}", g),)) for g in (0, 1)]]
        f = [[]] * 18 + [[("dve", "f_abs", (l,)), ("act", "f_ln", (l,))], [("dve", "f_log", (l,))]]
        if l:
            f += [[("act", "f_ln2", (l,)), ("dve", "f_log2", (l,))]]
        out += weave(merge(qk, [[]] * 4 + mem_qk, gates, [[]] * 6 + heads, f), panel_list(f"in2_{l}", None, 12), 2)
        out += [("dve", "gate_out", ((f"matt{l}", g),)) for g in (0, 1)]
        out += hgrn_steps(l)
        out += [(e, k, (l, b)) for b in (0, 2, 8, 10) for e, k in (("act", "y_hi"), ("dve", "y_lo"))]
        if l == 0:
            out += mem_norm(1) + panel_steps("out2_0") + split_rows("mem1")
            first, *others = panel_list("mem1")
            out += [("dve", "residual", ("out2_0", t)) for t in range(TILES)]
            out += [("act", k, ("pre1", t)) for t in (0, 1) for k in ("sumsq", "rstd")]
            out += splits(*range(*LATE["out2_0"])) + first
        else:
            out += panel_steps("out2_1")
    for t in range(TILES):
        out += [("dve", "residual", ("out2_1", t)), ("pool", "store", (t,))]
    return out


ORDER = order()
COUNT_AT = {}
_counts = {}
for _e, _k, _a in ORDER:
    if _k not in UNCOUNTED:
        _counts[_e] = _counts.get(_e, 0) + 1
        assert (_e, _k, _a) not in COUNT_AT, (_e, _k, _a)
        COUNT_AT[_e, _k, _a] = _counts[_e]


def at(engine, kind, *args):
    return COUNT_AT[engine, kind, args]


def build(nc, x_in, mem_in, pos_in, panels, gains, small_in, tab0, tab1, tab2, tab3, out):
    with ExitStack() as ctx:
        def sb(name, shape, dt=F32):
            return ctx.enter_context(nc.sbuf_tensor(name, shape, dt))

        def sem(name):
            return ctx.enter_context(nc.semaphore(name))

        raw = sb("raw", [P, SLOTS, PANEL])
        w_hi = sb("w_hi", [P, SLOTS, PANEL], F32R)
        w_lo = sb("w_lo", [P, SLOTS, PANEL], F32R)
        x = sb("x", [P, TILES, D])
        act_hi = sb("act_hi", [P, 12, SEQ], F32R)
        act_lo = sb("act_lo", [P, 12, SEQ], F32R)
        g_hi = sb("g_hi", [P, 2, 2, SEQ], F32R)
        g_lo = sb("g_lo", [P, 2, 2, SEQ], F32R)
        pair = sb("pair", [P, 2048])
        xn = sb("xn", [P, TILES * D])
        gain = sb("gain", [P, D])
        const = sb("const", [P, tab0.shape[1]])
        table = sb("table", [P, TABLE_W])
        small = sb("small", [P, SMALL_W])
        wab_h = sb("wab_h", [P, 64], F32R)
        wab_l = sb("wab_l", [P, 64], F32R)
        stat = sb("stat", [P, 98])
        work = sb("work", [P, WORK])
        ps = ctx.enter_context(nc.psum_tensor("ps", [P, 8, 512], F32))

        silu_buf, g32 = pair[:, 0:512], pair[:, 512:1024]
        sq = [pair[:, 0:512], pair[:, 512:1024]]
        rs = [pair[:, 1024:1536], pair[:, 1536:2048]]
        y32 = xn[:, 0:512]

        def cst(name):
            a, n = PLACES[0][name]
            return const[:, a:a + n]

        def tab(s, name):
            a, n = PLACES[s][name]
            return table[:, a:a + n]

        def sm(name, j=0, n=1):
            a, _ = SMALL[name]
            return small[:, a + j:a + j + n]

        def region(a, *shape):
            n = int(np.prod(shape))
            v = work[:, a:a + n]
            if len(shape) == 2:
                return v.rearrange("p (a b) -> p a b", a=shape[0])
            if len(shape) == 3:
                return v.rearrange("p (a b c) -> p a b c", a=shape[0], b=shape[1])
            return v

        def grid(ap, a):
            return ap.rearrange("p (a b) -> p a b", a=a)

        def spread(ap, n):
            return ap.rearrange("p (a b) -> p a b", a=1).broadcast_to([P, n, ap.shape[1]])

        def along(ap, n):
            return ap.rearrange("p (b o) -> p b o", o=1).broadcast_to([P, ap.shape[1], n])

        ident = cst("ident")

        raw_qkv = region(0, 12, 260)
        qk = region(3120, 8, SEQ)
        vc = region(5168, 4, SEQ)
        z0 = region(6192, 4, SEQ)
        rqk = region(7216, 4, SEQ)
        rv = region(8240, TILES, 512)
        rg = region(9264, 4, SEQ)
        a_low = region(10288, TILES, 4, P)
        decay_t = region(11312, TILES, 4, P)
        pw_a = region(12336, TILES, 4, P)
        pw_n = region(13360, TILES, 4, P)
        assert 14384 <= WORK
        pw_a4 = region(5168, TILES, 4, P)
        pw_n4 = region(1024, TILES, 4, P)
        t_mat = xn[:, 1024:2048].rearrange("p (t h n) -> p t h n", t=TILES, h=4)
        m_mat = region(14384, TILES, 4, P)
        v_beta = region(0, TILES, 4, P)
        v_new = region(1024, TILES, 4, P)
        state = region(2048, 4, P)
        k_dec = region(2560, 4, P)
        q_dec = gain[:, 0:512].rearrange("p (h n) -> p h n", h=4)
        ret_p = region(12336, 4, 384)

        cqk = region(0, 8, SEQ)
        cv = region(2048, TILES, 512)
        dqk = region(3072, 8, SEQ)
        dv = region(5120, TILES, 512)
        mo_qk = region(0, 8, SEQ)
        mo_v = region(2048, TILES, 512)
        qm = region(3072, 4, SEQ)
        km = region(4096, 4, SEQ)
        vm = region(5120, TILES, 512)
        probs = region(6144, 2, 2, 512)
        p_t = region(8192, 2, 512)
        qh = region(9216, 4, SEQ)
        fh = region(10240, 4, SEQ)
        ih = region(11264, TILES, 512)
        z2 = region(12288, 12, SEQ)
        assert 15360 <= WORK
        hg = [region(1024 * i, 4, SEQ) for i in range(9)]
        k_g, dec_f, q_l, k_l = hg[0], (hg[1], hg[2]), (hg[3], hg[4]), (hg[5], hg[6])
        h_s = region(7 * 1024, TILES, 4, P)
        h_s01 = region(8 * 1024, 4, P)
        positions = region(0, SEQ).bitcast(I32)
        cos_a = table[:, TABLE_W - 512:TABLE_W - 256]
        sin_a = table[:, TABLE_W - 256:TABLE_W]
        ang, turns = region(1024, SEQ), region(2048, SEQ)

        sumsq, rstd = stat[:, 0:2], stat[:, 2:4]
        b_exp, beta, xa, e_sp = (stat[:, 4 + 8 * i:12 + 8 * i] for i in range(4))
        g_col, gc, e_gc, bge = (stat[:, 36 + 8 * i:44 + 8 * i] for i in range(4))
        e_alog, e_kd = stat[:, 68:72], stat[:, 72:76]
        nmax = (stat[:, 76:80], stat[:, 80:84])
        dens = (stat[:, 84:88], stat[:, 88:92])
        lam_c = stat[:, 92:96]
        dgain = stat[:, 96:97]
        zero4 = stat[:, 97:98]
        lbd, lbn, lbl = stat[:, 4:12], stat[:, 12:20], stat[:, 20:28]

        done = {e: sem(f"{e}_done") for e in ("pe", "act", "dve", "pool")}
        pe_done, act_done, dve_done, pool_done = (done[e] for e in ("pe", "act", "dve", "pool"))
        act_chain, dve_chain = sem("act_chain"), sem("dve_chain")
        panel_loaded = [sem(f"panel_loaded_{i}") for i in range(SLOTS)]
        panel_hi, panel_lo, panel_used = sem("panel_hi"), sem("panel_lo"), sem("panel_used")
        silu_done, gate_read, gate_hi, gate_ready = (sem(n) for n in ("silu_done", "gate_read", "gate_hi", "gate_ready"))
        loads = [a[0] for e, k, a in ORDER if k == "load"]
        loaded = {n: sem(f"loaded_{n}") for n in loads}
        stored = sem("stored")
        tile_ready = sem("tile_ready")

        def evac(name, k):
            return ("act", "evacuate", name, k)

        ropes = {}
        for g in range(2):
            ropes["r64", g] = (rqk[:, 2 * g:2 * g + 2], tab(1, "swap64"), tab(1, "cos64"), tab(1, "sin64"), 4 + g, evac("in0", 13))
        for g in range(4):
            ropes["r128", g] = (cqk[:, 2 * g:2 * g + 2], tab(2, "swap128"), tab(2, "cos128"), tab(2, "sin128"), 4 + g // 2,
                                evac("in1", 11))
            ropes["r64b", g] = (dqk[:, 2 * g:2 * g + 2], tab(2, "swap64"), tab(2, "cos64"), tab(2, "sin64"), 6 + g // 2,
                                evac("in1", g))
            for l in range(2):
                unit_ = ((f"mq{l}", f"mk{l}")[g // 2], g % 2)
                ropes[unit_] = (mo_qk[:, 2 * g:2 * g + 2], tab(3, "swapp"), cos_a, sin_a, 2 + g // 2, ("dve", "cn_use", unit_))
        rope_list = [a for e, k, a in ORDER if k == "swap"]
        rope_index = {a[0]: i for i, a in enumerate(rope_list)}

        norms = {}
        for g in range(2):
            s2 = slice(2 * g, 2 * g + 2)
            s4 = slice(4 + 2 * g, 6 + 2 * g)
            ones, ones64 = cst("ones"), cst("ones64")
            norms["dq", g] = (qk[:, s2], ones, 1.0, P ** -0.5, qk[:, s2], None, None, g, ("act", "conv_silu", g))
            norms["dk", g] = (qk[:, s4], ones, 1.0, 1.0, qk[:, s4], None, None, g, ("act", "conv_silu", 2 + g))
            norms["do", g] = (grid(ps[:, 6 + g], 2), ones, 1 / P, sm("gdn"), None, z0[:, s2], 2 * g, g, ("pe", "delta_out", g))
            norms["ro", g] = (grid(ps[:, 2 + g], 2), ones, 1 / P, 1.0, None, rg[:, s2], 4 + 2 * g, 4 + g, ("pe", "ret_out", 2 * g + 1))
            norms["fo", g] = (grid(ps[:, 6 + g], 2), ones, 1 / P, dgain, None, None, 4 + 2 * g, 2 + g, ("pe", "attend", ("dif", 2 * g + 1)))
            for l in range(2):
                norms[f"mq{l}", g] = (mo_qk[:, s2], ones64, 1 / 64, sm(f"mq{l}"), mo_qk[:, s2], None, None, 6, evac(f"in2_{l}", 8 + g))
                norms[f"mk{l}", g] = (mo_qk[:, s4], ones64, 1 / 64, sm(f"mk{l}"), mo_qk[:, s4], None, None, 7, evac(f"in2_{l}", 10 + g))
                norms[f"sq{l}", g] = (qm[:, s2], ones, 1 / P, sm(f"sq{l}"), qm[:, s2], None, None, 6 + g, evac(f"in2_{l}", 12 + g))
                norms[f"sk{l}", g] = (km[:, s2], ones, 1 / P, sm(f"sk{l}"), km[:, s2], None, None, 6 + g, evac(f"mem{l}", g))
                norms[f"ho{l}", g] = (grid(ps[:, 6 + g], 2), ones, 1 / P, sm(f"ho{l}"), None, z2[:, 4 + 2 * g:6 + 2 * g], 4 + 2 * g, g,
                                      ("pe", "hgrn_out", l, g))
        norm_list = [a[0] for e, k, a in ORDER if k == "cn_sum"]
        norm_index = {u: i for i, u in enumerate(norm_list)}

        atts = {}
        for h in range(4):
            o = lambda b, j: ps[:, b, SEQ * j:SEQ * (j + 1)]
            col = slice(P * h, P * h + P)
            atts["dil", h] = ([(cqk[:, h], cqk[:, 4 + h])], cv[:, :, col], o(4 + h // 2, h % 2), False, tab(2, "union"),
                              tab(2, "times"), P ** -0.5, ("dve", "rope", ("r128", 3)))
            atts["dif", h] = ([(dqk[0:64, h], dqk[0:64, 4 + h]), (dqk[64:128, h], dqk[64:128, 4 + h])], dv[:, :, col],
                              o(6 + h // 2, h % 2), False, tab(2, "causal"), None, 0.125,
                              ("dve", "rope", ("r64b", 2 + h // 2)))
            for l in range(2):
                atts[f"matt{l}", h] = ([(qm[:, h], km[:, h])], vm[:, :, col], o(6 + h // 2, h % 2), True, None, None, P ** -0.5,
                                       ("dve", "cn_use", (f"sq{l}", 1)))
        for h in range(8):
            r = slice(64 * (h % 2), 64 * (h % 2) + 64)
            for l in range(2):
                atts[f"moba{l}", h] = ([(mo_qk[r, h // 2], mo_qk[r, 4 + h // 2])], mo_v[:, :, 64 * h:64 * h + 64],
                                       ps[r, 6 + h // 4, SEQ * (h // 2 % 2):SEQ * (h // 2 % 2) + SEQ], False, tab(3, "causal"), None, 0.125,
                                       ("dve", "rope", (f"mk{l}", h // 4)))
        att_list = [a[0] for e, k, a in ORDER if k == "scores"]
        att_index = {u: i for i, u in enumerate(att_list)}
        gates = {}
        for g in range(2):
            gates["dil", g] = (None, 4 + g, ("dil", 2 * g + 1))
            for l in range(2):
                gates[f"moba{l}", g] = (z2[:, 2 * g:2 * g + 2], 6 + g, (f"moba{l}", 4 * g + 3))
                gates[f"matt{l}", g] = (z2[:, 8 + 2 * g:10 + 2 * g], 6 + g, (f"matt{l}", 2 * g + 1))

        def score_bank(unit, m, back=False):
            i = att_index[unit]
            two = lambda u_: len(atts[u_][0]) == 2
            if back:
                return 1 if two(unit) or (i and two(att_list[i - 1])) else 2
            return m if two(unit) else i % 2

        def spans(full):
            return [(0, 256), (256, 512)] if full else [(0, 128), (128, 384)]

        dest = {}
        for k in range(6):
            dest["in0", k] = (raw_qkv[:, 2 * k:2 * k + 2, 4:260], "cols", ACT.Copy)
        rows = lambda r, k: r[:, :, UPW * k:UPW * (k + 1)]
        blocks = lambda r, k: r[:, 2 * k:2 * k + 2]
        for k in range(2):
            dest["in0", 6 + k] = (blocks(z0, k), "cols", ACT.Silu)
            dest["in0", 8 + k] = (blocks(rg, k), "cols", ACT.Silu)
            dest["in0", 10 + k] = (blocks(rqk, k), "cols", ACT.Copy)
            dest["in0", 12 + k] = (rows(rv, k), "rows", ACT.Copy)
            dest["in1", 4 + k] = (rows(dv, k), "rows", ACT.Copy)
            dest["in1", 10 + k] = (rows(cv, k), "rows", ACT.Copy)
            for l in range(2):
                dest[f"in2_{l}", 6 + k] = (blocks(qh, k), "cols", ACT.Silu)
                dest[f"in2_{l}", 12 + k] = (blocks(qm, k), "cols", ACT.Copy)
                dest[f"in2_{l}", 14 + k] = (rows(mo_v, k), "rows", ACT.Copy)
                dest[f"in2_{l}", 16 + k] = (blocks(fh, k), "cols", ACT.Copy)
                dest[f"in2_{l}", 18 + k] = (rows(ih, k), "rows", ACT.Copy)
                dest[f"mem{l}", k] = (blocks(km, k), "cols", ACT.Copy)
                dest[f"mem{l}", 2 + k] = (rows(vm, k), "rows", ACT.Copy)
        for k in range(4):
            dest["in1", k] = (blocks(dqk, k), "cols", ACT.Copy)
            dest["in1", 6 + k] = (blocks(cqk, k), "cols", ACT.Copy)
            for l in range(2):
                dest[f"in2_{l}", 8 + k] = (blocks(mo_qk, k), "cols", ACT.Copy)
        for k in range(6):
            for l in range(2):
                dest[f"in2_{l}", k] = (blocks(z2, k), "cols", ACT.Silu)

        def bank_of(name, k):
            return 4 + (BASE[name] + k) % 2

        def source_of(tag, t):
            if tag == "ffn0":
                return x, ("load", "x")
            if tag.startswith("mem"):
                return xn[:, :].rearrange("p (t d) -> p t d", t=TILES), ("load", tag)
            return x, (("dve", "scale", "final", t, 1) if tag == "pre0" else ("dve", "residual", RESIDUALS[tag], t))

        xn_rows = xn[:, :].rearrange("p (t d) -> p t d", t=TILES)
        last_use = {}
        for i, g in enumerate(GAINS[1:]):
            last_use["gain_" + g] = ("dve", "scale", GAINS[i], 1, 1)
        last_use["tab2"] = ("dve", "cn_use", ("ro", 1))
        last_use["tab3"] = last_use["pos"] = ("dve", "gate_out", ("dil", 1))
        last_use["mem0"] = ("dve", "x_lo", "ffn3", 1, 1)
        last_use["mem1"] = ("dve", "cn_use", ("ho0", 1))
        last_use["gain_ffn1"] = ("dve", "cn_use", ("ro", 1))

        def of(j, const, step):
            return const if j is None else j * step + const

        def steps(engine, handlers):
            for e, kind, args in ORDER:
                if e == engine:
                    handlers[kind](*args)

        def delta_bank(t, i):
            return (0, 1, 2, 3, 6, 7)[3 * t + i]

        def turn_bank(tag, t, half):
            return (4 if tag.startswith("mem") else 0) + 2 * t + half

        def both_banks(t):
            return ps[:, 2 * t:2 * t + 2].rearrange("p b n -> p (b n)")

        def conv_out(b):
            return qk[:, b] if b < 8 else vc[:, b - 8]

        block = ctx.enter_context(nc.Block())

        @block.sync
        def _(sp):
            def load_panel(s, g):
                if isinstance(g, int) and g == 0:
                    sp.dma_start(raw[:, s], panels[s]).then_inc(panel_loaded[s], 16)
                    return
                sp.wait_ge(panel_lo, g * SLOTS + (s + 1 - SLOTS))
                sp.dma_start(raw[:, s], panels[g * SLOTS + s]).then_inc(panel_loaded[s], 16)

            for s in range(SLOTS):
                load_panel(s, 0)
            with sp.Fori(1, PANELS // SLOTS) as g:
                for s in range(SLOTS):
                    load_panel(s, g)
            for s in range(PANELS % SLOTS):
                load_panel(s, PANELS // SLOTS)

        @block.gpsimd
        def _(pool):
            places = {"x": (x[:], x_in), "const": (const[:], tab0), "small": (small[:], small_in),
                      "tab1": (table[:, 0:tab1.shape[1]], tab1), "tab2": (table[:, 0:tab2.shape[1]], tab2),
                      "tab3": (table[:, 0:tab3.shape[1]], tab3),
                      "pos": (positions, pos_in.rearrange("(a n) -> a n", a=1).broadcast_to([P, SEQ])),
                      "mem0": (xn_rows, mem_in), "mem1": (xn_rows, mem_in)}
            for i, g in enumerate(GAINS):
                places["gain_" + g] = (gain[:], gains[i:i + 1].broadcast_to([P, D]))

            def load(tag):
                if tag in last_use:
                    pool.wait_ge(done[last_use[tag][0]], at(*last_use[tag]))
                to, of_ = places[tag]
                pool.dma_start(to, of_).then_inc(loaded[tag], 16)

            def zero():
                nc.gpsimd.memset(raw_qkv[:, :, 0:4], 0.0)
                nc.gpsimd.memset(zero4, 0.0).then_inc(pool_done, 1)

            def k_level(l, v):
                if v == 0:
                    pool.wait_ge(act_done, at("act", "k_gate", l))
                pool.wait_ge(act_done, at("act", "decay_f", l, v))
                if v >= 2:
                    pool.wait_ge(pe_done, at("pe", "level", l, v - 2))
                nc.gpsimd.tensor_tensor(k_l[v % 2], k_g, dec_f[v % 2], ALU.mult).then_inc(pool_done, 1)

            def store(t):
                pool.wait_ge(dve_done, at("dve", "residual", "out2_1", t))
                pool.dma_start(out[:, t], x[:, t]).then_inc(stored, 16)
                if t == TILES - 1:
                    pool.wait_ge(stored, 16 * TILES)

            steps("pool", {"load": load, "zero": zero, "k_level": k_level, "store": store})

        @block.tensor
        def _(pe):
            def three(o, l, r, start, stop):
                pe.matmul(o, l[0], r[0], start=start, stop=False)
                pe.matmul(o, l[0], r[1], start=False, stop=False)
                return pe.matmul(o, l[1], r[0], start=False, stop=stop)

            def weight(slot, c, a, n, width):
                return [w[:, slot, c * width + a:c * width + a + n] for w in (w_hi, w_lo)]

            def up(slot, bank, form, n, j=None, step=0, tag=None):
                pe.wait_ge(panel_lo, of(j, n + 1, step))
                for half in range(2):
                    o = ps[:, bank, SEQ * half:SEQ * (half + 1)]
                    for c in range(DC):
                        if tag and half == 0 and c % 4 == 0:
                            pe.wait_ge(dve_done, at("dve", "x_lo", tag, 1, c // 4))
                        if form == "cols":
                            l = weight(slot, c, P * half, P, UPW)
                            r = [a[:, c, :] for a in (act_hi, act_lo)]
                        else:
                            l = [a[:, c, P * half:P * half + P] for a in (act_hi, act_lo)]
                            r = weight(slot, c, 0, UPW, UPW)
                        ins = three(o, l, r, c == 0, c == DC - 1)
                ins.then_inc(panel_used, 1)

            def down(slot, parts, first, last, n, j=None, step=0):
                pe.wait_ge(panel_lo, of(j, n + 1, step))
                for t in range(TILES):
                    for half in range(2):
                        for c in range(2):
                            l = [a[:, c, P * t:P * t + P] for a in parts]
                            ins = three(ps[:, 2 * t + half], l, weight(slot, c, 512 * half, 512, D),
                                        first and c == 0, last and c == 1)
                    if last and t == 0:
                        ins.then_inc(tile_ready, 1)
                ins.then_inc(panel_used, 1)

            def ffn(f):
                b, c = BASE[f"ffn{f}"], f * UPS
                tag = f"ffn{f}"

                def gate_up(i, j=None):
                    n = b + (0 if i == 0 else 3 * i - 1)
                    if i:
                        pe.wait_ge(gate_read, of(j, c + i, 2))
                    up(n % SLOTS, 4, "cols", n, j, 6, None if i else tag)
                    up((n + 1) % SLOTS, 5, "cols", n + 1, j, 6)

                def down_of(i, j=None):
                    n = b + (3 * i + 4 if i < UPS - 1 else 3 * UPS - 1)
                    pe.wait_ge(gate_ready, of(j, c + i + 1, 2))
                    down(n % SLOTS, (g_hi[:, i % 2], g_lo[:, i % 2]), i == 0, i == UPS - 1, n, j, 6)

                gate_up(0)
                gate_up(1)
                down_of(0)
                with pe.Fori(0, (UPS - 3) // 2) as j:
                    for i in (2, 3):
                        gate_up(i, j)
                        down_of(i - 1, j)
                gate_up(UPS - 1)

            def ffn_down(f, i):
                b, c = BASE[f"ffn{f}"], f * UPS
                n = b + (3 * i + 4 if i < UPS - 1 else 3 * UPS - 1)
                pe.wait_ge(gate_ready, c + i + 1)
                down(n % SLOTS, (g_hi[:, i % 2], g_lo[:, i % 2]), i == 0, i == UPS - 1, n)

            def panel(name, k):
                n = BASE[name] + k
                if name.startswith("out"):
                    if k == 0:
                        last = {"out0": ("cn_use", ("ro", 1)), "out1": ("gate_out", ("dil", 1)),
                                "out2_0": ("y_lo", 0, 10), "out2_1": ("y_lo", 1, 10)}[name]
                        pe.wait_ge(dve_done, at("dve", *last))
                    parts = (act_hi[:, 2 * k:2 * k + 2], act_lo[:, 2 * k:2 * k + 2])
                    down(n % SLOTS, parts, k == 0, k == N_OF[name] - 1, n)
                else:
                    tag = {"in0": "mix0", "in1": "mix1", "in2_0": "pre0", "in2_1": "pre1"}.get(name, name)
                    if k >= 2:
                        pe.wait_ge(act_done, at("act", "evacuate", name, k - 2))
                    up(n % SLOTS, bank_of(name, k), dest[name, k][1], n, tag=None if k else tag)

            def turn_x(tag, t, half):
                pe.wait_ge(dve_done, at("dve", "scale", tag, t, half))
                pe.wait_ge(loaded["const"], 16)
                if tag == "mem0":
                    pe.wait_ge(gate_read, 4 * UPS)
                for c in range(4 * half, 4 * half + 4):
                    ins = pe.transpose(ps[:, turn_bank(tag, t, half), P * (c % 4):P * (c % 4) + P], xn_rows[:, t, P * c:P * c + P], ident)
                ins.then_inc(pe_done, 1)

            def ab_mm():
                pe.wait_ge(dve_done, at("dve", "wab_lo"))
                for t in range(TILES):
                    for c in range(DC):
                        l = [a[:, c, P * t:P * t + P] for a in (act_hi, act_lo)]
                        ins = three(ps[:, 6, 8 * t:8 * t + 8], l, [w[:, 8 * c:8 * c + 8] for w in (wab_h, wab_l)], c == 0, c == DC - 1)
                ins.then_inc(pe_done, 1)

            def heads(o, lhs, rhs, turn=False):
                for h in range(4):
                    oh = o[:, P * h:P * h + P]
                    ins = pe.transpose(oh, lhs(h), ident) if turn else pe.matmul(oh, lhs(h), rhs(h), start=True, stop=True)
                return ins

            def cumsum():
                pe.wait_ge(dve_done, at("dve", "g"))
                pe.wait_ge(loaded["tab1"], 16)
                up_ = tab(1, "upper")
                for t in range(TILES):
                    pe.matmul(ps[:, 6, 4 * t:4 * t + 4], up_, g_col[:, 4 * t:4 * t + 4], start=True, stop=True)
                for t in range(TILES):
                    ins = heads(ps[:, 2 + t], lambda h: g_col[:, 4 * t + h:4 * t + h + 1].broadcast_to([P, P]), lambda h: up_)
                ins.then_inc(pe_done, 1)

            tok = lambda t: slice(P * t, P * t + P)

            def turn_v(t):
                pe.wait_ge(act_done, at("act", "conv_silu", 5))
                pe.wait_ge(dve_done, at("dve", "decay_mask", 1))
                heads(ps[:, t], lambda h: vc[:, h, tok(t)], None, turn=True).then_inc(pe_done, 1)

            def turn_k():
                pe.wait_ge(dve_done, at("dve", "v_beta", 0))
                heads(ps[:, 2], lambda h: qk[:, 4 + h, tok(0)], None, turn=True).then_inc(pe_done, 1)

            def kk(t):
                pe.wait_ge(dve_done, at("dve", "k_decayed"))
                heads(ps[:, delta_bank(t, 0)], lambda h: qk[:, 4 + h, tok(t)], lambda h: qk[:, 4 + h, tok(t)]).then_inc(pe_done, 1)

            def turn_a(t):
                pe.wait_ge(dve_done, at("dve", "a_low", t))
                heads(ps[:, delta_bank(t, 1)], lambda h: a_low[:, t, h], None, turn=True).then_inc(pe_done, 1)

            def pow2(t):
                pe.wait_ge(dve_done, at("dve", "base16", t))
                heads(ps[:, delta_bank(t, 0)], lambda h: pw_a4[:, t, h], lambda h: t_mat[:, t, h])
                heads(ps[:, delta_bank(t, 1)], lambda h: t_mat[:, t, h], lambda h: pw_a4[:, t, h]).then_inc(pe_done, 1)

            def pow4(t):
                pe.wait_ge(act_done, at("act", "pow2_n", t))
                pe.wait_ge(dve_done, at("dve", "pow2_a", t))
                heads(ps[:, delta_bank(t, 0)], lambda h: pw_a[:, t, h], lambda h: pw_n[:, t, h])
                heads(ps[:, delta_bank(t, 1)], lambda h: pw_n[:, t, h], lambda h: pw_a[:, t, h])
                heads(ps[:, delta_bank(t, 2)], lambda h: pw_a[:, t, h], lambda h: m_mat[:, t, h]).then_inc(pe_done, 1)

            def pow8(t):
                pe.wait_ge(act_done, at("act", "pow4_n", t))
                pe.wait_ge(dve_done, at("dve", "pow4_a", t))
                heads(ps[:, delta_bank(t, 0)], lambda h: pw_n4[:, t, h], lambda h: pw_a4[:, t, h])
                heads(ps[:, delta_bank(t, 2)], lambda h: pw_a4[:, t, h], lambda h: m_mat[:, t, h]).then_inc(pe_done, 1)

            def pow16(t):
                pe.wait_ge(act_done, at("act", "pow8_a", t))
                pe.wait_ge(dve_done, at("dve", "pow8_m", t))
                heads(ps[:, delta_bank(t, 2)], lambda h: pw_a[:, t, h], lambda h: m_mat[:, t, h]).then_inc(pe_done, 1)

            def turn_m(t):
                pe.wait_ge(dve_done, at("dve", "pow16_m", t))
                heads(ps[:, delta_bank(t, 0)], lambda h: m_mat[:, t, h], None, turn=True).then_inc(pe_done, 1)

            def kq(t):
                pe.wait_ge(dve_done, at("dve", "k_decayed"))
                heads(ps[:, 6 + t], lambda h: qk[:, 4 + h, tok(t)], lambda h: qk[:, h, tok(t)]).then_inc(pe_done, 1)

            def double_y(s, t):
                pe.wait_ge(act_done, at("act", "t_rows", t))
                pe.wait_ge(dve_done, at("dve", "corner", s, t))
                heads(ps[:, delta_bank(t, 0)], lambda h: pw_n[:, t, h], lambda h: m_mat[:, t, h]).then_inc(pe_done, 1)

            def double(s, t):
                pe.wait_ge(act_done, at("act", "y", s, t))
                ins = heads(ps[:, delta_bank(t, 1)], lambda h: t_mat[:, t, h], lambda h: pw_a[:, t, h])
                if s < 2:
                    ins = heads(ps[:, delta_bank(t, 2)], lambda h: pw_a[:, t, h], lambda h: t_mat[:, t, h])
                ins.then_inc(pe_done, 1)

            def u(t):
                if t == 0:
                    pe.wait_ge(dve_done, at("dve", "doubled", 2, 1))
                else:
                    pe.wait_ge(dve_done, at("dve", "v_less"))
                heads(ps[:, t], lambda h: m_mat[:, t, h], lambda h: v_beta[:, t, h]).then_inc(pe_done, 1)

            def state_mm():
                pe.wait_ge(act_done, at("act", "v_new", 0))
                heads(ps[:, 0], lambda h: k_dec[:, h], lambda h: v_new[:, 0, h]).then_inc(pe_done, 1)

            def from_state():
                pe.wait_ge(act_done, at("act", "state_copy"))
                heads(ps[:, 1], lambda h: qk[:, 4 + h, tok(1)], lambda h: state[:, h]).then_inc(pe_done, 1)

            def delta_out(g):
                pe.wait_ge(act_done, at("act", "v_new", 1))
                pe.wait_ge(dve_done, at("dve", "q_decayed"))
                for i in range(2):
                    h, o = 2 * g + i, ps[:, 6 + g, SEQ * i:SEQ * i + SEQ]
                    pe.matmul(o[:, 0:P], v_new[:, 0, h], decay_t[:, 0, h], start=True, stop=True)
                    pe.matmul(o[:, P:SEQ], v_new[:, 1, h], decay_t[:, 1, h], start=True, stop=False)
                    ins = pe.matmul(o[:, P:SEQ], state[:, h], q_dec[:, h], start=False, stop=True)
                ins.then_inc(pe_done, 1)

            def ret_scores(h):
                pe.wait_ge(dve_done, at("dve", "rope", ("r64", 1)))
                if h >= 2:
                    pe.wait_ge(dve_done, at("dve", "ret_decay", h - 2))
                r = slice(64 * (h % 2), 64 * (h % 2) + 64)
                q, k = rqk[r, h // 2], rqk[r, 2 + h // 2]
                pe.matmul(ps[:, 4 + h % 2, 0:SEQ], k[:, 0:P], q, start=True, stop=True)
                pe.matmul(ps[:, 4 + h % 2, SEQ:384], k[:, P:SEQ], q[:, P:SEQ], start=True, stop=True).then_inc(pe_done, 1)

            def weighted(o, v0, v1, first, second, full=False):
                pe.matmul(o, v0, first, start=True, stop=False, skip_group_check=True)
                return pe.matmul(o if full else o[:, P:SEQ], v1, second, start=False, stop=True, skip_group_check=True)

            def ret_out(h):
                pe.wait_ge(dve_done, at("dve", "ret_decay", h))
                weighted(ps[:, 2 + h // 2, SEQ * (h % 2):SEQ * (h % 2) + SEQ], rv[:, 0, P * h:P * h + P], rv[:, 1, P * h:P * h + P],
                         ret_p[:, h, 0:SEQ], ret_p[:, h, SEQ:384]).then_inc(pe_done, 1)

            def swap(unit):
                values, matrix, _, _, bank, ready = ropes[unit]
                pe.wait_ge(done[ready[0]], at(*ready))
                if rope_index[unit] >= 2:
                    pe.wait_ge(dve_done, at("dve", "rope", rope_list[rope_index[unit] - 2][0]))
                for t_ in ("tab1", "tab2", "tab3"):
                    if unit[0] in {"tab1": ("r64",), "tab2": ("r128", "r64b"), "tab3": ("mq0", "mk0", "mq1", "mk1")}[t_]:
                        pe.wait_ge(loaded[t_], 16)
                pe.matmul(ps[:, bank], matrix, values, start=True, stop=True).then_inc(pe_done, 1)

            def cn_sum(unit):
                src, ones, _, _, _, _, _, bank, _ = norms[unit]
                pe.wait_ge(act_done, at("act", "cn_sq", unit))
                pe.matmul(ps[:, bank], ones, sq[norm_index[unit] % 2], start=True, stop=True).then_inc(pe_done, 1)

            def scores(unit):
                maps, _, _, full, _, _, _, ready = atts[unit]
                pe.wait_ge(done[ready[0]], at(*ready))
                i = att_index[unit]
                back = score_bank(unit, 0, True)
                if i >= back:
                    pe.wait_ge(dve_done, at("dve", "mask_max", att_list[i - back]))
                for m, (q, k) in enumerate(maps):
                    bank = ps[:, score_bank(unit, m)]
                    pe.matmul(bank[:, 0:SEQ if full else P], q[:, 0:P], k if full else k[:, 0:P], start=True, stop=True)
                    a = SEQ if full else P
                    ins = pe.matmul(bank[:, a:a + SEQ], q[:, P:SEQ], k, start=True, stop=True)
                ins.then_inc(pe_done, 1)

            def turn_p(unit):
                i, full = att_index[unit], atts[unit][3]
                pe.wait_ge(dve_done, at("dve", "divide", unit))
                if i >= 2:
                    pe.wait_ge(act_done, at("act", "p_cols", att_list[i - 2]))
                p, bank = probs[:, i % 2, 0], ps[:, 2 + i % 2]
                second = SEQ if full else P
                pe.transpose(bank[:, 0:P], p[:, 0:P], ident)
                pe.transpose(bank[:, P:SEQ], p[:, second:second + P], ident)
                if full:
                    pe.transpose(bank[:, SEQ:384], p[:, P:SEQ], ident)
                    ins = pe.transpose(bank[:, 384:512], p[:, 384:512], ident)
                else:
                    ins = pe.transpose(bank[:, SEQ:384], p[:, second + P:second + SEQ], ident)
                ins.then_inc(pe_done, 1)

            def attend(unit):
                _, v, o, full, *_ = atts[unit]
                i = att_index[unit]
                pe.wait_ge(act_done, at("act", "p_cols", unit))
                if unit[0].startswith("matt") and unit[1] == 0:
                    pe.wait_ge(dve_done, at("dve", "gate_out", ("moba" + unit[0][4:], 1)))
                p = p_t[:, i % 2]
                weighted(o, v[:, 0], v[:, 1], p[:, 0:SEQ], p[:, SEQ:512] if full else p[:, SEQ:384], full).then_inc(pe_done, 1)

            def lam_sum():
                pe.wait_ge(dve_done, at("dve", "lam_mul"))
                pe.matmul(ps[:, 3, 0:2], cst("ones")[0:64, :], lam_c[0:64, 0:2], start=True, stop=True).then_inc(pe_done, 1)

            def diagonal(l):
                pe.wait_ge(act_done, at("act", "k_gate", l))
                for t in range(TILES):
                    ins = heads(ps[:, 4 + t], lambda h: k_g[:, h, tok(t)], lambda h: qh[:, h, tok(t)])
                ins.then_inc(pe_done, 1)

            def level(l, v):
                pe.wait_ge(dve_done, at("dve", "q_level", l, v))
                pe.wait_ge(pool_done, at("pool", "k_level", l, v))
                if v >= 2:
                    pe.wait_ge(dve_done, at("dve", "level_in", l, v - 2))
                k, q = k_l[v % 2], q_l[v % 2]
                if v < 7:
                    for t in range(TILES):
                        ins = heads(ps[:, 2 * (v % 2) + t], lambda h: k[:, h, tok(t)], lambda h: q[:, h, tok(t)])
                else:
                    ins = heads(ps[:, 2], lambda h: k[:, h, tok(0)], lambda h: q[:, h, tok(1)])
                ins.then_inc(pe_done, 1)

            def hgrn_out(l, g):
                pe.wait_ge(dve_done, at("dve", "level_in", l, 7))
                for i in range(2):
                    h, o = 2 * g + i, ps[:, 6 + g, SEQ * i:SEQ * i + SEQ]
                    v0, v1 = ih[:, 0, P * h:P * h + P], ih[:, 1, P * h:P * h + P]
                    pe.matmul(o[:, 0:P], v0, h_s[:, 0, h], start=True, stop=True)
                    pe.matmul(o[:, P:SEQ], v0, h_s01[:, h], start=True, stop=False)
                    ins = pe.matmul(o[:, P:SEQ], v1, h_s[:, 1, h], start=False, stop=True)
                ins.then_inc(pe_done, 1)

            steps("pe", {"ffn": ffn, "ffn_down": ffn_down, "panel": panel, "turn_x": turn_x, "ab_mm": ab_mm, "cumsum": cumsum, "turn_v": turn_v,
                         "turn_k": turn_k, "kk": kk, "turn_a": turn_a, "pow2": pow2, "pow4": pow4, "pow8": pow8, "pow16": pow16,
                         "turn_m": turn_m, "kq": kq, "double_y": double_y, "double": double, "u": u, "state": state_mm,
                         "from_state": from_state, "delta_out": delta_out, "ret_scores": ret_scores, "ret_out": ret_out,
                         "swap": swap, "cn_sum": cn_sum, "scores": scores, "turn_p": turn_p, "attend": attend,
                         "lam_sum": lam_sum, "diagonal": diagonal, "level": level, "hgrn_out": hgrn_out})

        @block.scalar
        def _(act):
            chained = [0]

            def step(ins):
                chained[0] += 1
                ins.then_inc(act_chain, 1)
                act.wait_ge(act_chain, chained[0])

            def split_hi(n, j=None, step_=0):
                s = n % SLOTS
                act.wait_ge(panel_loaded[s], of(j, 16 * (n // SLOTS + 1), 16 * step_ // SLOTS))
                if n >= SLOTS:
                    act.wait_ge(panel_used, of(j, n - SLOTS + 1, step_))
                nc.scalar.activation(w_hi[:, s], raw[:, s], ACT.Copy).then_inc(panel_hi, 1)

            def ffn(f):
                b, c = BASE[f"ffn{f}"], f * UPS

                def gate_up(i, j=None):
                    n = b + (0 if i == 0 else 3 * i - 1)
                    split_hi(n + 3, j, 6)
                    act.wait_ge(panel_used, of(j, n + 2, 6))
                    nc.scalar.activation(silu_buf, ps[:, 4], ACT.Silu).then_inc(silu_done, 1)
                    split_hi(n + 4, j, 6)

                def down_of(i, j=None):
                    split_hi(b + (3 * i + 4 if i < UPS - 1 else 3 * UPS - 1) + 3, j, 6)

                gate_up(0)
                gate_up(1)
                down_of(0)
                with act.Fori(0, (UPS - 3) // 2) as j:
                    for i in (2, 3):
                        gate_up(i, j)
                        down_of(i - 1, j)
                gate_up(UPS - 1)
                logs_and_exps()

            def wab_hi():
                act.wait_ge(loaded["small"], 16)
                nc.scalar.activation(wab_h[:], sm("wab", 0, 64), ACT.Copy).then_inc(act_done, 1)

            def sumsq_(tag, t):
                src, (e, *ready) = source_of(tag, t)
                if e == "load":
                    act.wait_ge(loaded[ready[0]], 16)
                else:
                    act.wait_ge(done[e], at(e, *ready))
                squares = work[:, 6144:8192] if tag in ("mem0", "mem1") else pair
                step(nc.scalar.activation(squares[:, D * t:D * t + D], src[:, t], ACT.Square, accum_out=sumsq[:, t:t + 1]))
                act.sem_inc(act_done, 1)

            def rstd_(tag, t):
                act.wait_ge(loaded["const"], 16)
                step(nc.scalar.activation(rstd[:, t:t + 1], sumsq[:, t:t + 1], ACT.Ln, bias=cst("eps"), scale=1 / D))
                nc.scalar.activation(rstd[:, t:t + 1], rstd[:, t:t + 1], ACT.Exp, scale=-0.5).then_inc(act_done, 1)

            def x_hi(tag, t, half):
                act.wait_ge(pe_done, at("pe", "turn_x", tag, t, half))
                to = act_hi[:, 4 * half:4 * half + 4, P * t:P * t + P]
                if tag in ("mem0", "mem1"):
                    act.wait_ge(panel_used, BASE["ffn3"] + 3 * UPS - 2 if tag == "mem0" else BASE["out2_0"] + N_OF["out2_0"])
                if tag in ("pre0", "pre1"):
                    act.wait_ge(panel_used, BASE["mem" + tag[3]] + N_OF["mem0"])
                nc.scalar.activation(to, grid(ps[:, turn_bank(tag, t, half)], 4), ACT.Copy).then_inc(act_done, 1)

            def evacuate(name, k):
                to, form, func = dest[name, k]
                act.wait_ge(panel_used, BASE[name] + k + 1)
                nc.scalar.activation(to, grid(ps[:, bank_of(name, k)], 2), func).then_inc(act_done, 1)

            def tap(p):
                act.wait_ge(pool_done, at("pool", "zero"))
                act.wait_ge(loaded["small"], 16)
                act.wait_ge(act_done, at("act", "evacuate", "in0", p))
                for i in range(2):
                    b = 2 * p + i
                    ins = nc.scalar.activation(conv_out(b), raw_qkv[:, b, 4:260], ACT.Copy, scale=sm("conv", 4 * b + 3))
                ins.then_inc(act_done, 1)

            def conv_silu(p):
                act.wait_ge(dve_done, at("dve", "conv", p))
                for i in range(2):
                    ins = nc.scalar.activation(conv_out(2 * p + i), conv_out(2 * p + i), ACT.Silu)
                ins.then_inc(act_done, 1)

            def logs_and_exps():
                nc.scalar.preload_act_table_set("natural_log_exp_and_others")

            def ab_exp():
                act.wait_ge(pe_done, at("pe", "ab_mm"))
                ab = grid(ps[:, 6, 0:16], 2)
                nc.scalar.activation(grid(b_exp, 2), ab[:, :, 0:4], ACT.Exp, scale=-1.0).then_inc(act_done, 1)

            def softplus():
                act.wait_ge(dve_done, at("dve", "ab"))
                step(nc.scalar.activation(e_sp, e_sp, ACT.Exp))
                nc.scalar.activation(e_sp, e_sp, ACT.Ln, bias=cst("one"))
                nc.scalar.activation(e_alog, sm("alog", 0, 4), ACT.Exp).then_inc(act_done, 1)

            def decay(t):
                act.wait_ge(dve_done, at("dve", "gap", t))
                nc.scalar.activation(decay_t[:, t], decay_t[:, t], ACT.Exp)
                ins = nc.scalar.activation(a_low[:, t], a_low[:, t], ACT.Exp, scale=-1.0)
                if t == 0:
                    nc.scalar.activation(e_gc, gc, ACT.Exp)
                    ins = nc.scalar.activation(e_kd, e_kd, ACT.Exp)
                else:
                    ins = nc.scalar.activation(q_dec, grid(ps[:, 3], 4), ACT.Exp)
                ins.then_inc(act_done, 1)

            def copy_back(to, bank, n=4):
                return nc.scalar.activation(to, grid(ps[:, bank], n), ACT.Copy).then_inc(act_done, 1)

            def pow2_n(t):
                act.wait_ge(pe_done, at("pe", "pow2", t))
                copy_back(pw_n[:, t], delta_bank(t, 0))

            def pow4_n(t):
                act.wait_ge(pe_done, at("pe", "pow4", t))
                copy_back(pw_n4[:, t], delta_bank(t, 0))

            def pow8_a(t):
                act.wait_ge(pe_done, at("pe", "pow8", t))
                copy_back(pw_a[:, t], delta_bank(t, 0))

            def t_rows(t):
                act.wait_ge(pe_done, at("pe", "turn_m", t))
                copy_back(t_mat[:, t], delta_bank(t, 0))

            def y(s, t):
                act.wait_ge(pe_done, at("pe", "double_y", s, t))
                copy_back(pw_a[:, t], delta_bank(t, 0))

            def v_new_(t):
                act.wait_ge(pe_done, at("pe", "u", t))
                copy_back(v_new[:, t], t)

            def state_copy():
                act.wait_ge(pe_done, at("pe", "state"))
                copy_back(state, 0)

            def cn_sq(unit):
                src, *_, ready = norms[unit]
                act.wait_ge(done[ready[0]], at(*ready))
                nc.scalar.activation(grid(sq[norm_index[unit] % 2], 2), src, ACT.Square).then_inc(act_done, 1)

            def cn_rstd(unit):
                _, _, inv, _, _, _, _, bank, _ = norms[unit]
                i = norm_index[unit]
                act.wait_ge(pe_done, at("pe", "cn_sum", unit))
                if i >= 2:
                    act.wait_ge(dve_done, at("dve", "cn_use", norm_list[i - 2]))
                step(nc.scalar.activation(rs[i % 2], ps[:, bank], ACT.Ln, bias=cst("eps"), scale=inv))
                nc.scalar.activation(rs[i % 2], rs[i % 2], ACT.Exp, scale=-0.5).then_inc(act_done, 1)

            def exp_(unit):
                maps, _, _, full, *_ = atts[unit]
                i = att_index[unit]
                act.wait_ge(dve_done, at("dve", "mask_max", unit))
                for m in range(len(maps)):
                    for q, (a, b) in enumerate(spans(full)):
                        p = probs[:, i % 2, m, a:b]
                        c = 2 * m + q
                        ins = nc.scalar.activation(p, p, ACT.Exp, bias=nmax[i % 2][:, c:c + 1], scale=-1.0,
                                                   accum_out=dens[i % 2][:, c:c + 1])
                step(ins)
                act.sem_inc(act_done, 1)

            def p_cols(unit):
                i, full = att_index[unit], atts[unit][3]
                act.wait_ge(pe_done, at("pe", "turn_p", unit))
                if i >= 2:
                    act.wait_ge(pe_done, at("pe", "attend", att_list[i - 2]))
                n = 512 if full else 384
                nc.scalar.activation(p_t[:, i % 2, 0:n], ps[:, 2 + i % 2, 0:n], ACT.Copy).then_inc(act_done, 1)

            def y_hi(l, b):
                act.wait_ge(dve_done, at("dve", "gate_out", (f"matt{l}", 1)))
                act.wait_ge(panel_used, BASE[f"in2_{l}"] + N_OF[f"in2_{l}"])
                nc.scalar.activation(act_hi[:, b:b + 2], z2[:, b:b + 2], ACT.Copy).then_inc(act_done, 1)

            def lam_exp():
                act.wait_ge(pe_done, at("pe", "lam_sum"))
                nc.scalar.activation(lam_c[:, 2:4], ps[:, 3, 0:2], ACT.Exp).then_inc(act_done, 1)

            def sines():
                act.wait_ge(dve_done, at("dve", "angle"))
                nc.scalar.activation(sin_a, sin_a, ACT.Sin)
                nc.scalar.activation(cos_a, cos_a, ACT.Sin).then_inc(act_done, 1)

            def f_ln(l):
                act.wait_ge(dve_done, at("dve", "f_abs", l))
                step(nc.scalar.activation(hg[1], hg[1], ACT.Exp))
                ins = nc.scalar.activation(hg[1], hg[1], ACT.Ln, bias=cst("one"))
                if l:
                    step(nc.scalar.activation(lbn, lbn, ACT.Exp))
                    ins = nc.scalar.activation(lbn, lbn, ACT.Ln, bias=cst("one"))
                ins.then_inc(act_done, 1)

            def f_ln2(l):
                act.wait_ge(dve_done, at("dve", "f_log", l))
                step(nc.scalar.activation(hg[2], hg[2], ACT.Exp))
                nc.scalar.activation(hg[2], hg[2], ACT.Ln, bias=cst("one")).then_inc(act_done, 1)

            def k_gate(l):
                act.wait_ge(dve_done, at("dve", "f_log2" if l else "f_log", l))
                nc.scalar.activation(k_g, k_g, ACT.Exp).then_inc(act_done, 1)

            def decay_f(l, v):
                act.wait_ge(dve_done, at("dve", "gap_f", l, v))
                nc.scalar.activation(dec_f[v % 2], dec_f[v % 2], ACT.Exp).then_inc(act_done, 1)

            steps("act", {"split_hi": split_hi, "ffn": ffn, "wab_hi": wab_hi, "sumsq": sumsq_, "rstd": rstd_, "x_hi": x_hi,
                          "evacuate": evacuate, "logs": logs_and_exps, "tap": tap, "conv_silu": conv_silu, "ab_exp": ab_exp, "softplus": softplus,
                          "decay": decay, "pow2_n": pow2_n, "pow4_n": pow4_n, "pow8_a": pow8_a, "t_rows": t_rows, "y": y,
                          "v_new": v_new_, "state_copy": state_copy, "cn_sq": cn_sq, "cn_rstd": cn_rstd, "exp": exp_,
                          "p_cols": p_cols, "y_hi": y_hi, "lam_exp": lam_exp, "sines": sines, "f_ln": f_ln, "f_ln2": f_ln2,
                          "k_gate": k_gate, "decay_f": decay_f})

        @block.vector
        def _(dve):
            chained = [0]

            def step(ins):
                chained[0] += 1
                ins.then_inc(dve_chain, 1)
                dve.wait_ge(dve_chain, chained[0])

            tt = nc.vector.tensor_tensor
            ts = nc.vector.tensor_scalar
            stt = nc.vector.scalar_tensor_tensor

            def finish(ins):
                finished[0] += 1
                ins.then_inc(dve_done, 1)
                dve.wait_ge(dve_done, finished[0])

            finished = [0]

            def split_lo(n, j=None, step_=0):
                s = n % SLOTS
                dve.wait_ge(panel_hi, of(j, n + 1, step_))
                tt(w_lo[:, s], raw[:, s], w_hi[:, s].bitcast(F32), ALU.subtract).then_inc(panel_lo, 1)

            def ffn(f):
                b, c = BASE[f"ffn{f}"], f * UPS

                def gate_up(i, j=None):
                    n = b + (0 if i == 0 else 3 * i - 1)
                    split_lo(n + 3, j, 6)
                    dve.wait_ge(silu_done, of(j, c + i + 1, 2))
                    if c + i:
                        dve.wait_ge(gate_ready, of(j, c + i, 2))
                    tt(g32, silu_buf, ps[:, 5], ALU.mult).then_inc(gate_read, 1)
                    dve.wait_ge(gate_read, of(j, c + i + 1, 2))
                    nc.vector.tensor_copy(g_hi[:, i % 2], grid(g32, 2)).then_inc(gate_hi, 1)
                    dve.wait_ge(gate_hi, of(j, c + i + 1, 2))
                    tt(g_lo[:, i % 2], grid(g32, 2), g_hi[:, i % 2].bitcast(F32), ALU.subtract).then_inc(gate_ready, 1)
                    split_lo(n + 4, j, 6)

                def down_of(i, j=None):
                    split_lo(b + (3 * i + 4 if i < UPS - 1 else 3 * UPS - 1) + 3, j, 6)

                gate_up(0)
                gate_up(1)
                down_of(0)
                with dve.Fori(0, (UPS - 3) // 2) as j:
                    for i in (2, 3):
                        gate_up(i, j)
                        down_of(i - 1, j)
                gate_up(UPS - 1)

            def wab_lo():
                dve.wait_ge(act_done, at("act", "wab_hi"))
                finish(tt(wab_l[:], sm("wab", 0, 64), wab_h[:].bitcast(F32), ALU.subtract))

            def residual(name, t):
                if t == 0:
                    dve.wait_ge(tile_ready, DOWNS.index(name) + 1)
                else:
                    dve.wait_ge(panel_used, BASE[name] + N_OF[name])
                if name == "ffn0":
                    dve.wait_ge(loaded["x"], 16)
                k = 0.5 if name.startswith("ffn") else 1.0
                finish(stt(x[:, t], both_banks(t), k, x[:, t], ALU.mult, ALU.add))

            def scale(tag, t, half):
                src, _ = source_of(tag, t)
                dve.wait_ge(act_done, at("act", "rstd", tag, t))
                dve.wait_ge(loaded["gain_" + tag], 16)
                to = x if tag == "final" else xn_rows
                c = slice(512 * half, 512 * half + 512)
                finish(stt(to[:, t, c], src[:, t, c], rstd[:, t:t + 1], gain[:, c], ALU.mult, ALU.mult))

            def x_lo(tag, t, half):
                dve.wait_ge(act_done, at("act", "x_hi", tag, t, half))
                b, c = slice(4 * half, 4 * half + 4), slice(P * t, P * t + P)
                finish(tt(act_lo[:, b, c], grid(ps[:, turn_bank(tag, t, half)], 4), act_hi[:, b, c].bitcast(F32), ALU.subtract))

            def conv(p):
                dve.wait_ge(act_done, at("act", "tap", p))
                for k in (2, 1, 0):
                    for i in range(2):
                        b = 2 * p + i
                        ins = stt(conv_out(b), raw_qkv[:, b, 1 + k:1 + k + SEQ], sm("conv", 4 * b + k), conv_out(b), ALU.mult, ALU.add)
                    (step if k else finish)(ins)

            def ab():
                dve.wait_ge(act_done, at("act", "ab_exp"))
                step(ts(b_exp, b_exp, 1.0, None, ALU.add))
                nc.vector.reciprocal(beta, b_exp)
                step(tt(grid(xa, 2), grid(ps[:, 6, 0:16], 2)[:, :, 4:8], spread(sm("dt", 0, 4), 2), ALU.add))
                step(ts(e_sp, xa, -1.0, None, ALU.mult))
                finish(tt(e_sp, xa, e_sp, ALU.min))

            def g():
                dve.wait_ge(act_done, at("act", "softplus"))
                step(stt(g_col, xa, 0.0, e_sp, ALU.max, ALU.add))
                finish(stt(grid(g_col, 2), grid(g_col, 2), -1.0, spread(e_alog, 2), ALU.mult, ALU.mult))

            def gc_():
                dve.wait_ge(pe_done, at("pe", "cumsum"))
                step(nc.vector.tensor_copy(gc, ps[:, 6, 0:8]))
                finish(tt(e_kd.rearrange("p (a b) -> p a b", b=1), grid(ps[:, 2], 4)[:, :, P - 1:P], gc[:, 0:4].rearrange("p (a b) -> p a b", b=1),
                          ALU.subtract))

            def gap(t):
                step(tt(decay_t[:, t], grid(ps[:, 2 + t], 4), along(gc[:, 4 * t:4 * t + 4], P), ALU.subtract))
                step(ts(a_low[:, t], decay_t[:, t], 0.0, None, ALU.max))
                finish(ts(decay_t[:, t], decay_t[:, t], 0.0, None, ALU.min))

            def decay_mask(t):
                dve.wait_ge(act_done, at("act", "decay", t))
                tt(decay_t[:, t], decay_t[:, t], spread(tab(1, "upper"), 4), ALU.mult)
                step(tt(a_low[:, t], a_low[:, t], spread(tab(1, "strict"), 4), ALU.mult))
                if t:
                    tt(bge[:, 0:4], beta[:, 4:8], e_gc[:, 4:8], ALU.mult)
                finish(tt(a_low[:, t], a_low[:, t], along(beta[:, 4 * t:4 * t + 4], P), ALU.mult))

            def q_decayed():
                finish(tt(q_dec, q_dec, qk[:, 0:4, P:SEQ], ALU.mult))

            def v_beta_(t):
                dve.wait_ge(pe_done, at("pe", "turn_v", t))
                finish(tt(v_beta[:, t], grid(ps[:, t], 4), along(beta[:, 4 * t:4 * t + 4], P), ALU.mult))

            def k_decayed():
                dve.wait_ge(pe_done, at("pe", "turn_k"))
                finish(tt(k_dec, grid(ps[:, 2], 4), along(e_kd, P), ALU.mult))

            def a_low_(t):
                dve.wait_ge(pe_done, at("pe", "kk", t))
                finish(tt(a_low[:, t], a_low[:, t], grid(ps[:, delta_bank(t, 0)], 4), ALU.mult))

            def base16(t):
                dve.wait_ge(pe_done, at("pe", "turn_a", t))
                m16 = spread(tab(1, "diag16"), 4)
                step(tt(t_mat[:, t], grid(ps[:, delta_bank(t, 1)], 4), m16, ALU.mult))
                tt(pw_a4[:, t], a_low[:, t], m16, ALU.mult)
                finish(tt(m_mat[:, t], spread(ident, 4), t_mat[:, t], ALU.subtract))

            def add_to(to, bank, op=ALU.add):
                return tt(to, to, grid(ps[:, bank], 4), op)

            def pow2_a(t):
                dve.wait_ge(pe_done, at("pe", "pow2", t))
                finish(nc.vector.tensor_copy(pw_a[:, t], grid(ps[:, delta_bank(t, 1)], 4)))

            def pow4_a(t):
                dve.wait_ge(pe_done, at("pe", "pow4", t))
                nc.vector.tensor_copy(pw_a4[:, t], grid(ps[:, delta_bank(t, 1)], 4))
                finish(add_to(m_mat[:, t], delta_bank(t, 2)))

            def pow8_m(t):
                dve.wait_ge(pe_done, at("pe", "pow8", t))
                finish(add_to(m_mat[:, t], delta_bank(t, 2)))

            def pow16_m(t):
                dve.wait_ge(pe_done, at("pe", "pow16", t))
                finish(add_to(m_mat[:, t], delta_bank(t, 2)))

            def qk_decay(t):
                dve.wait_ge(pe_done, at("pe", "kq", t))
                finish(tt(decay_t[:, t], decay_t[:, t], grid(ps[:, 6 + t], 4), ALU.mult))

            def corner(s, t):
                dve.wait_ge(pe_done, at("pe", "double", s - 1, t) if s else at("pe", "turn_m", t))
                finish(tt(pw_n[:, t], a_low[:, t], spread(tab(1, ("e16", "e32", "e64")[s]), 4), ALU.mult))

            def doubled(s, t):
                dve.wait_ge(pe_done, at("pe", "double", s, t))
                if s < 2:
                    add_to(t_mat[:, t], delta_bank(t, 2), ALU.subtract)
                finish(add_to(m_mat[:, t], delta_bank(t, 1), ALU.subtract))

            def v_less():
                dve.wait_ge(pe_done, at("pe", "from_state"))
                tmp = grid(xn[:, 0:512], 4)
                step(tt(tmp, grid(ps[:, 1], 4), along(bge[:, 0:4], P), ALU.mult))
                finish(tt(v_beta[:, 1], v_beta[:, 1], tmp, ALU.subtract))

            def ret_decay(h):
                dve.wait_ge(pe_done, at("pe", "ret_scores", h))
                a, _ = PLACES[1]["ret"]
                finish(tt(ret_p[:, h], ps[:, 4 + h % 2, 0:384], table[:, a + 384 * h:a + 384 * h + 384], ALU.mult))

            def rope(unit):
                values, _, cos, sin, bank, _ = ropes[unit]
                dve.wait_ge(pe_done, at("pe", "swap", unit))
                if unit[0][0] == "m":
                    dve.wait_ge(act_done, at("act", "sines"))
                tmp = grid(xn[:, 512:1024], 2)
                step(tt(tmp, grid(ps[:, bank], 2), spread(sin, 2), ALU.mult))
                step(tt(values, values, spread(cos, 2), ALU.mult))
                finish(tt(values, values, tmp, ALU.add))

            def split_out(b):
                step(nc.vector.tensor_copy(act_hi[:, b:b + 2], grid(y32, 2)))
                finish(tt(act_lo[:, b:b + 2], grid(y32, 2), act_hi[:, b:b + 2].bitcast(F32), ALU.subtract))

            def cn_use(unit):
                src, _, _, k, to, gate, b, _, _ = norms[unit]
                dve.wait_ge(act_done, at("act", "cn_rstd", unit))
                r = grid(rs[norm_index[unit] % 2], 2)
                if to is not None:
                    finish(stt(to, src, k, r, ALU.mult, ALU.mult))
                    return
                step(stt(grid(y32, 2), src, k, r, ALU.mult, ALU.mult))
                if gate is not None:
                    step(tt(grid(y32, 2), grid(y32, 2), gate, ALU.mult))
                split_out(b)

            def gate_out(unit):
                gate, bank, last = gates[unit]
                dve.wait_ge(pe_done, at("pe", "attend", last))
                src = grid(ps[:, bank], 2)
                if gate is None:
                    step(nc.vector.tensor_copy(grid(y32, 2), src))
                    split_out(2 * unit[1])
                else:
                    finish(tt(gate, src, gate, ALU.mult))

            def y_lo(l, b):
                dve.wait_ge(act_done, at("act", "y_hi", l, b))
                finish(tt(act_lo[:, b:b + 2], z2[:, b:b + 2], act_hi[:, b:b + 2].bitcast(F32), ALU.subtract))

            def mask_max(unit):
                maps, _, _, full, mask, _, k, _ = atts[unit]
                i = att_index[unit]
                dve.wait_ge(pe_done, at("pe", "scores", unit))
                if i >= 2:
                    dve.wait_ge(pe_done, at("pe", "turn_p", att_list[i - 2]))
                for m in range(len(maps)):
                    for q, (a, b) in enumerate(spans(full)):
                        to, s = probs[:, i % 2, m, a:b], ps[:, score_bank(unit, m), a:b]
                        low = nmax[i % 2][:, 2 * m + q:2 * m + q + 1]
                        if full:
                            ins = ts(to, s, -k, None, ALU.mult, ALU.min, accum_out=low)
                        else:
                            ins = nc.vector.tensor_tensor_reduce(to, s, mask[:, a:b], -k, 3e38, ALU.add, ALU.min, low)
                finish(ins)

            def divide(unit):
                maps, _, _, full, _, times, _, _ = atts[unit]
                i = att_index[unit]
                p, den = probs[:, i % 2], dens[i % 2]
                dve.wait_ge(act_done, at("act", "exp", unit))
                if times is not None:
                    for q, (a, b) in enumerate(spans(full)):
                        ins = nc.vector.tensor_tensor_reduce(p[:, 0, a:b], p[:, 0, a:b], times[:, a:b], 1.0, 0.0, ALU.mult, ALU.add,
                                                             den[:, q:q + 1])
                    step(ins)
                step(nc.vector.reciprocal(den[:, 0:2 * len(maps)], den[:, 0:2 * len(maps)]))
                if len(maps) == 2:
                    step(ts(den[:, 2:4], den[:, 2:4], lam_c[:, 3:4], None, ALU.mult))
                for q, (a, b) in enumerate(spans(full)):
                    ins = ts(p[:, 0, a:b], p[:, 0, a:b], den[:, q:q + 1], None, ALU.mult)
                if len(maps) == 2:
                    step(ins)
                    for q, (a, b) in enumerate(spans(full)):
                        ins = stt(p[:, 0, a:b], p[:, 1, a:b], den[:, 2 + q:3 + q], p[:, 0, a:b], ALU.mult, ALU.add)
                finish(ins)

            def lam_mul():
                v = sm("lam", 0, 4)[0:64, :]
                step(tt(lam_c[0:64, 0:2], v[:, 0:2], v[:, 2:4], ALU.mult))
                finish(ts(dgain, sm("diff"), 1.0 - LAMBDA_INIT, None, ALU.mult))

            def lam():
                dve.wait_ge(act_done, at("act", "lam_exp"))
                step(tt(lam_c[:, 3:4], lam_c[:, 3:4], lam_c[:, 2:3], ALU.subtract))
                finish(ts(lam_c[:, 3:4], lam_c[:, 3:4], LAMBDA_INIT, None, ALU.subtract))

            def angle():
                dve.wait_ge(loaded["pos"], 16)
                dve.wait_ge(loaded["tab3"], 16)
                step(nc.vector.tensor_copy(ang, positions))
                step(ts(ang, ang, tab(3, "freq"), None, ALU.mult))
                for to, quarter in ((sin_a, 0.0), (cos_a, 0.25)):
                    step(ts(turns, ang, 1 / (2 * math.pi), quarter, ALU.mult, ALU.add))
                    step(ts(turns, turns, MAGIC, None, ALU.add))
                    step(ts(turns, turns, MAGIC, None, ALU.subtract))
                    step(stt(to, turns, -TWO_PI[0], ang, ALU.mult, ALU.add))
                    step(stt(to, turns, -TWO_PI[1], to, ALU.mult, ALU.add))
                    step(stt(to, turns, -TWO_PI[2], to, ALU.mult, ALU.add))
                    if quarter:
                        step(ts(to, to, math.pi / 2, None, ALU.add))
                    ins = ts(to, to, -PI_IN, PI_IN, ALU.max, ALU.min)
                    (finish if quarter else step)(ins)

            def f_abs(l):
                dve.wait_ge(act_done, at("act", "evacuate", f"in2_{l}", 17))
                dve.wait_ge(pe_done, at("pe", "scores", (f"matt{l}", 3)))
                step(ts(hg[1], fh, -1.0, None, ALU.mult))
                step(tt(hg[1], fh, hg[1], ALU.min))
                if l:
                    a, b = sm("lb", 0, 4), sm("lb", 4, 4)
                    tt(lbd[:, 0:4], b, a, ALU.subtract)
                    step(tt(lbd[:, 4:8], a, b, ALU.subtract))
                    step(tt(lbn[:, 0:4], lbd[:, 0:4], lbd[:, 4:8], ALU.min))
                    step(tt(lbn[:, 4:8], lbd[:, 0:4], lbd[:, 4:8], ALU.min))
                finish(nc.vector.memset(zero4, 0.0))

            def f_log(l):
                dve.wait_ge(act_done, at("act", "f_ln", l))
                step(stt(hg[1], fh, 0.0, hg[1], ALU.min, ALU.subtract))
                if l:
                    step(stt(lbl, lbd, 0.0, lbn, ALU.min, ALU.subtract))
                    step(tt(hg[1], hg[1], along(lbl[:, 4:8], SEQ), ALU.add))
                    step(tt(hg[2], hg[1], along(lbl[:, 0:4], SEQ), ALU.subtract))
                    step(ts(hg[3], hg[2], -1.0, None, ALU.mult))
                    step(tt(hg[2], hg[2], hg[3], ALU.min))
                finish(tt(k_g, hg[1], fh, ALU.subtract))

            def f_log2(l):
                dve.wait_ge(act_done, at("act", "f_ln2", l))
                step(tt(hg[1], hg[1], along(lbl[:, 0:4], SEQ), ALU.max))
                finish(tt(hg[1], hg[1], hg[2], ALU.add))

            def cum_f(l):
                for h in range(4):
                    ins = nc.vector.tensor_tensor_scan(fh[:, h], tab(3, "keep"), hg[1][:, h], 0.0, ALU.mult, ALU.add)
                finish(ins)

            def diagonal_in(l):
                dve.wait_ge(pe_done, at("pe", "diagonal", l))
                for t in range(TILES):
                    ins = tt(h_s[:, t], grid(ps[:, 4 + t], 4), spread(ident, 4), ALU.mult)
                finish(ins)

            def gap_f(l, v):
                if v >= 2:
                    dve.wait_ge(pool_done, at("pool", "k_level", l, v - 2))
                to = dec_f[v % 2]
                if v < 7:
                    b = 64 >> v
                    split = lambda r: r.rearrange("p h (n c) -> p (h n) c", c=2 * b)
                    a_, t_ = split(fh), split(to)
                    edge = a_[:, :, b - 1:b].broadcast_to([P, 4 * SEQ // (2 * b), b])
                    tt(t_[:, :, b:2 * b], a_[:, :, b:2 * b], edge, ALU.subtract)
                    finish(tt(t_[:, :, 0:b], edge, a_[:, :, 0:b], ALU.subtract))
                else:
                    tt(to[:, :, 0:P], fh[:, :, P - 1:P].broadcast_to([P, 4, P]), fh[:, :, 0:P], ALU.subtract)
                    finish(nc.vector.tensor_copy(to[:, :, P:SEQ], fh[:, :, P:SEQ]))

            def q_level(l, v):
                dve.wait_ge(act_done, at("act", "decay_f", l, v))
                if v >= 2:
                    dve.wait_ge(pe_done, at("pe", "level", l, v - 2))
                finish(tt(q_l[v % 2], qh, dec_f[v % 2], ALU.mult))

            def level_in(l, v):
                dve.wait_ge(pe_done, at("pe", "level", l, v))
                if v < 7:
                    a, _ = PLACES[3]["levels"]
                    mask = spread(table[:, a + P * v:a + P * v + P], 4)
                    for t in range(TILES):
                        ins = nc.vector.copy_predicated(h_s[:, t], mask.bitcast(U32), grid(ps[:, 2 * (v % 2) + t], 4))
                else:
                    ins = nc.vector.tensor_copy(h_s01, grid(ps[:, 2], 4))
                finish(ins)

            steps("dve", {"split_lo": split_lo, "ffn": ffn, "wab_lo": wab_lo, "residual": residual, "scale": scale, "x_lo": x_lo,
                          "conv": conv, "ab": ab, "g": g, "gc": gc_, "gap": gap, "decay_mask": decay_mask, "q_decayed": q_decayed,
                          "v_beta": v_beta_, "k_decayed": k_decayed, "a_low": a_low_, "base16": base16, "pow2_a": pow2_a,
                          "pow4_a": pow4_a, "pow8_m": pow8_m, "pow16_m": pow16_m, "qk_decay": qk_decay, "corner": corner,
                          "doubled": doubled, "v_less": v_less, "ret_decay": ret_decay, "rope": rope, "cn_use": cn_use,
                          "gate_out": gate_out, "y_lo": y_lo, "mask_max": mask_max, "divide": divide, "lam_mul": lam_mul, "lam": lam,
                          "angle": angle, "f_abs": f_abs, "f_log": f_log, "f_log2": f_log2, "cum_f": cum_f,
                          "diagonal_in": diagonal_in, "gap_f": gap_f, "q_level": q_level, "level_in": level_in})


def kernel(**inputs):
    import concourse.bacc as bacc
    from concourse.bass_utils import run_bass_kernel_spmd as run

    a = {k: np.asarray(v) for k, v in inputs.items()}

    def up(w, cols):
        return [w[:, c:c + UPW].reshape(DC, P, UPW).transpose(1, 0, 2).reshape(P, PANEL) for c in cols]

    def down(w):
        return [w[r:r + 2 * P].reshape(2, P, D).transpose(1, 0, 2).reshape(P, PANEL) for r in range(0, w.shape[0], 2 * P)]

    def ffn(name):
        w = a[name + "_w_up"]
        gate, upper = up(w, range(0, D_FF, UPW)), up(w, range(D_FF, 2 * D_FF, UPW))
        low = down(a[name + "_w_down"])
        order = [gate[0], upper[0]]
        for i in range(1, UPS):
            order += [gate[i], upper[i], low[i - 1]]
        return order + [low[-1]]

    in0 = list(range(0, 2048, UPW)) + [3080, 3336] + list(range(2056, 3080, UPW))
    in1 = list(range(1536, 3072, UPW)) + list(range(0, 1536, UPW))
    in2 = [c for a_, b_ in ((3584, 5120), (1536, 2048), (0, 1024), (3072, 3584), (1024, 1536), (2048, 3072)) for c in range(a_, b_, UPW)]
    stream = ffn("l0_ffn1") + up(a["l0_w_in"], in0) + down(a["l0_w_out"]) + ffn("l0_ffn2")
    stream += ffn("l1_ffn1") + up(a["l1_w_in"], in1) + down(a["l1_w_out"]) + ffn("l1_ffn2")
    for l in range(2):
        stream += up(a["w_mem_kv_2"][l], range(0, D, UPW)) + up(a["w_in_2"][l], in2) + down(a["w_out_2"][l])
    panels = np.stack(stream)
    gains = np.stack([a["l0_ffn1_norm"], a["l0_mix_norm"], a["l0_ffn2_norm"], a["l1_ffn1_norm"], a["l1_mix_norm"],
                      a["l1_ffn2_norm"], a["mem_norm_g_2"][0], a["final_norm"], a["norm_g_2"][0], a["mem_norm_g_2"][1],
                      a["norm_g_2"][1]])
    small = np.zeros((P, SMALL_W), np.float32)

    def put(name, v):
        at_, n = SMALL[name]
        small[:v.shape[0], at_:at_ + n] = v

    put("conv", a["l0_conv_w"].reshape(4, 12, P).transpose(2, 1, 0).reshape(P, 48))
    put("wab", a["l0_w_in"][:, 2048:2056].reshape(DC, P, 8).transpose(1, 0, 2).reshape(P, 64))
    put("alog", np.broadcast_to(a["l0_a_log"], (P, 4)))
    put("dt", np.broadcast_to(a["l0_dt_bias"], (P, 4)))
    put("gdn", a["l0_gdn_norm"][:, None])
    put("diff", a["l1_diff_norm"][:, None])
    put("lam", np.stack([a["l1_lambda_q1"], a["l1_lambda_q2"], a["l1_lambda_k1"], a["l1_lambda_k2"]], axis=1))
    put("lb", a["hgrn_lb_logits_2"].reshape(2, 4, P).transpose(2, 0, 1).reshape(P, 8))
    for l in range(2):
        put(f"mq{l}", np.tile(a["moba_q_norm_2"][l], 2)[:, None])
        put(f"mk{l}", np.tile(a["moba_k_norm_2"][l], 2)[:, None])
        put(f"sq{l}", a["mem_q_norm_2"][l][:, None])
        put(f"sk{l}", a["mem_k_norm_2"][l][:, None])
        put(f"ho{l}", a["hgrn_o_norm_2"][l][:, None])

    def tiles(v):
        return np.ascontiguousarray(v.reshape(TILES, P, D).transpose(1, 0, 2))

    arrays = {"x_in": tiles(a["x"]), "mem_in": tiles(a["mem_2"]), "pos_in": np.ascontiguousarray(a["positions_2"].reshape(SEQ)),
              "panels": panels, "gains": gains, "small_in": small}
    arrays.update({f"tab{i}": t for i, t in enumerate(TABLES)})
    nc = bacc.Bacc("TRN2", target_bir_lowering=False, num_devices=1)
    aps = {k: nc.dram_tensor(k, v.shape, mybir.dt.from_np(v.dtype), kind="ExternalInput").ap() for k, v in arrays.items()}
    out = nc.dram_tensor("out", (P, TILES, D), F32, kind="ExternalOutput").ap()
    build(nc, **aps, out=out)
    r = run(nc, [arrays], core_ids=[0])
    got = np.asarray(r.results[0]["out"])
    return got.transpose(1, 0, 2).reshape(1, SEQ, D)
```

```python
import math
from contextlib import ExitStack

import numpy as np

import concourse.bass as bass
from concourse import mybir

F32 = mybir.dt.float32
F32R = mybir.dt.float32r
I32 = mybir.dt.int32
U32 = mybir.dt.uint32
ALU = mybir.AluOpType
ACT = mybir.ActivationFunctionType
AX = mybir.AxisListType.X

P = 128
SEQ = 256
TILES = SEQ // P
D = 1024
DC = D // P
D_FF = 2816
UPW = 256
UPS = D_FF // UPW
PANEL = DC * UPW
SLOTS = 3
EPS = 1e-6
LAMBDA_INIT = 0.8 - 0.6 * math.exp(-0.3)
MAGIC = 12582912.0
TWO_PI = (6.28125, 0.0019354820251464844, -1.7484556025237907e-07)
PI_IN = 3.1415925
WORK = 15408

COUNTS = [("ffn0", 3 * UPS), ("in0", 14), ("out0", 4), ("ffn1", 3 * UPS), ("ffn2", 3 * UPS),
          ("in1", 12), ("out1", 4), ("ffn3", 3 * UPS), ("mem0", 4), ("in2_0", 20), ("out2_0", 6),
          ("mem1", 4), ("in2_1", 20), ("out2_1", 6)]
BASE = {}
PANELS = 0
for _name, _n in COUNTS:
    BASE[_name] = PANELS
    PANELS += _n
N_OF = dict(COUNTS)

GAINS = ["ffn0", "mix0", "ffn1", "ffn2", "mix1", "ffn3", "mem0", "final", "pre0", "mem1", "pre1"]

SMALL = {}
_at = 0
for _name, _n in [("conv", 48), ("wab", 64), ("alog", 4), ("dt", 4), ("gdn", 1), ("diff", 1), ("lam", 4),
                  ("lb", 8), ("mq0", 1), ("mk0", 1), ("sq0", 1), ("sk0", 1), ("ho0", 1),
                  ("mq1", 1), ("mk1", 1), ("sq1", 1), ("sk1", 1), ("ho1", 1)]:
    SMALL[_name] = (_at, _n)
    _at += _n
SMALL_W = _at


def tables():
    i = np.arange(P)
    part, free = i[:, None], i[None, :]
    f = np.float32
    upper = (part <= free).astype(f)
    strict_low = (part > free).astype(f)

    def swap(n, half, signs=True, width=None):
        m = np.zeros((P, P), f)
        for g in range(0, P, n):
            for d in range(half):
                m[g + d + half, g + d] = -1.0
                m[g + d, g + d + half] = 1.0
        return m

    def rope(dim):
        inv = (np.float32(10000.0) ** (-np.arange(0, dim, 2, dtype=f) / f(dim))).astype(f)
        ang = (np.arange(SEQ, dtype=f)[None, :] * inv[:, None]).astype(f)
        reps = P // (dim // 2)
        return np.tile(np.cos(ang), (reps, 1)).astype(f), np.tile(np.sin(ang), (reps, 1)).astype(f)

    q0 = part - free
    q1 = part + P - np.arange(SEQ)[None, :]
    dist = np.concatenate([q0, q1], axis=1)
    causal = np.where(dist >= 0, 0.0, -1e38).astype(f)
    times = ((dist >= 0) & (dist <= 128)).astype(f)
    for r in (4, 16):
        times = times + ((dist >= 0) & (dist % r == 0)).astype(f)
    union = np.where(times > 0, 0.0, -1e38).astype(f)
    rel = np.concatenate([np.arange(SEQ)[None, :] - part, free - part], axis=1).astype(np.float64)
    ret = [np.where(rel >= 0, np.exp(np.maximum(rel, 0) * math.log(1 - 2.0 ** (-5 - h))), 0.0) * 0.125
           for h in range(4)]
    cos64, sin64 = rope(64)
    cos128, sin128 = rope(128)
    diag16 = (part // 16 == free // 16).astype(f)

    def below(b):
        return ((part // (2 * b) == free // (2 * b)) & (part % (2 * b) >= b) & (free % (2 * b) < b)).astype(f)

    levels = [((part // (2 * b) == free // (2 * b)) & (part % (2 * b) < b) & (free % (2 * b) >= b)).astype(f)
              for b in (64, 32, 16, 8, 4, 2, 1)]
    keep = np.ones((P, SEQ), f)
    keep[:, ::P] = 0
    half = 8
    inv2 = (f(500000.0) ** (-np.arange(half, dtype=f) / f(half))).astype(f)
    freq = np.zeros((P, 1), f)
    for g in (0, 64):
        freq[g:g + half, 0] = inv2
        freq[g + half:g + 2 * half, 0] = inv2
    sets = [
        [("ident", np.eye(P)), ("ones", np.ones((P, P))), ("ones64", part // 64 == free // 64),
         ("eps", np.full((P, 1), EPS)), ("one", np.ones((P, 1)))],
        [("upper", upper), ("strict", strict_low), ("diag16", diag16), ("e16", below(16)), ("e32", below(32)),
         ("e64", below(64)), ("ret", np.concatenate(ret, axis=1)), ("cos64", cos64), ("sin64", sin64),
         ("swap64", swap(64, 32))],
        [("causal", causal), ("times", times), ("union", union), ("cos64", cos64), ("sin64", sin64),
         ("swap64", swap(64, 32)), ("cos128", cos128), ("sin128", sin128), ("swap128", swap(128, 64))],
        [("causal", causal), ("swapp", swap(64, 8)), ("levels", np.concatenate(levels, axis=1)),
         ("keep", keep), ("freq", freq)],
    ]
    arrays, places = [], []
    for s in sets:
        where, at_ = {}, 0
        for name, a in s:
            where[name] = (at_, a.shape[1])
            at_ += a.shape[1]
        arrays.append(np.ascontiguousarray(np.concatenate([np.asarray(a, f) for _, a in s], axis=1)))
        places.append(where)
    return arrays, places


TABLES, PLACES = tables()
TABLE_W = max(t.shape[1] for t in TABLES[1:])

RESIDUALS = {"mix0": "ffn0", "ffn1": "out0", "ffn2": "ffn1", "mix1": "ffn2", "ffn3": "out1", "final": "ffn3",
             "pre1": "out2_0", "end": "out2_1"}
DOWNS = list(RESIDUALS.values())
LATE = {name: (BASE[name] + N_OF[name] + SLOTS - 1, min(BASE[name] + N_OF[name] + SLOTS, PANELS)) for name in DOWNS}
UNCOUNTED = {"half", "ffn_down", "logs", "split_hi", "split_lo", "ffn", "panel", "load", "store"}


def rounds(steps, units):
    return [[(engine, kind, (units[r - lag],)) for engine, kind, lag in steps if 0 <= r - lag < len(units)]
            for r in range(len(units) + max(lag for _, _, lag in steps))]


def lagged(steps, units):
    return sum(rounds(steps, units), [])


def merge(*chains):
    return [sum((c[i] for c in chains if i < len(c)), []) for i in range(max(map(len, chains)))]


def weave(chain, pieces, places):
    out, rest = [], []
    pieces = sorted(zip(places, range(len(pieces)), pieces))
    for i, r in enumerate(chain):
        out += r + rest
        rest = []
        while pieces and pieces[0][0] <= i:
            out += rest
            first, *rest = pieces.pop(0)[2]
            out.append(first)
    return out + rest + sum((p[2] for p in pieces), [])


def halves(panels):
    out = []
    panels = panels[:-2] + [p[:2] for p in panels[-2:]]
    for (_, _, args), *rest in panels:
        out += [[("pe", "half", (*args, 0))], [("pe", "half", (*args, 1)), *rest]]
    return out


NORM_COLS = [("pe", "cn_sum", 1), ("act", "cn_sq", 0), ("act", "cn_rstd", 1), ("dve", "cn_use", 1)]
ATTEND = [("pe", "turn_p", 2), ("pe", "scores", 0), ("pe", "attend", 3), ("act", "p_cols", 2), ("dve", "divide", 1),
          ("dve", "mask_max", 0), ("act", "exp", 0)]
ATTEND_TWO = ATTEND[:4] + [ATTEND[5], ATTEND[4], ATTEND[6]]
ROPE = [("pe", "swap", 0), ("dve", "rope", 0)]
NORM_ROPE = NORM_COLS + [("pe", "swap", 2), ("dve", "rope", 2)]


BESIDE_0 = [0, 0, 0, 1, 2, 3, 4, 5, 5, 8, 10, 12, 14, 16, 18, 20]
BESIDE_1 = [0, 0, 1, 1, 2, 3, 4, 5]
BESIDE_2 = [-13, -13, -12, -12, -11, -11, -10, -10, -9, -9, -8, -8, -7, -7, -6, -6, -5, -5, -4, -4, -3, -3, -2, -2,
            -1, 0, 1, 2, 3, 4, 5, 6]


def next_gain(tag):
    i = GAINS.index(tag) + 1
    if tag == "mix0":
        return []
    return [("pool", "load", ("gain_" + GAINS[i],))] if i < len(GAINS) else []


def norm_steps(tag):
    out = []
    before = RESIDUALS.get(tag) if tag != "pre1" else None
    for t in range(TILES):
        for half in range(2):
            out += [("dve", "residual", (before, t, half))] if before else []
            out += [("act", "sumsq", (tag, t, half))]
        out += [("act", "rstd", (tag, t))]
    for t in range(TILES):
        for half in range(2):
            out += [(e, k, (tag, t, half)) for e, k in (("dve", "scale"), ("pe", "turn_x"))]
    for t in range(TILES):
        for half in range(2):
            out += [("act", "x_hi", (tag, t, half)), ("dve", "x_lo", (tag, t, half))]
    if before:
        out += [("dve", "split_lo", (LATE[before][0] - 1,))]
    for n in range(*LATE.get(before, (0, 0))):
        out += [("act", "split_hi", (n,)), ("dve", "split_lo", (n,))]
    return out + next_gain(tag)


def panel_steps(name, extra=None, start=0, stop=None):
    return sum(panel_list(name, extra, start, stop), [])


def panel_list(name, extra=None, start=0, stop=None):
    all_ = []
    for k in range(start, N_OF[name] if stop is None else stop):
        out = []
        all_.append(out)
        n = BASE[name] + k
        out.append(("pe", "panel", (name, k)))
        if not name.startswith("out"):
            out.append(("act", "evacuate", (name, k)))
        late = LATE.get(name, (0, 0))
        if n + SLOTS < PANELS and not late[0] <= n + SLOTS < late[1]:
            out += splits(n + SLOTS)[:1 if n + SLOTS == late[0] - 1 else 2]
        out += (extra or {}).get(k, [])
    return all_


def ffn_tail(f):
    return [("pe", "ffn_down", (f, UPS - 2)), ("act", "split_hi", (BASE[f"ffn{f}"] + N_OF["ffn0"] + 1,)), ("pe", "ffn_down", (f, UPS - 1))]


def ffn_steps(f):
    return norm_steps(f"ffn{f}") + [(e, "ffn", (f,)) for e in ("pe", "act", "dve")]


def delta_rounds():
    both = lambda *steps: [(e, k, (*a, t)) for t in range(TILES) for e, k, *a in steps]
    out = [[("act", "softplus", ()), ("dve", "g", ())]]
    out += merge([[("pe", "cumsum", ())], [("dve", "gc", ())] + both(("dve", "gap"), ("act", "decay")), both(("dve", "decay_mask"))],
                 rounds(NORM_COLS, [("dq", 0), ("dq", 1), ("dk", 0), ("dk", 1)]))
    out += [[("dve", "q_decayed", ()), ("pe", "turn_v", (0,)), ("pe", "turn_v", (1,)), ("dve", "v_beta", (0,)), ("dve", "v_beta", (1,)),
             ("pe", "turn_k", ()), ("dve", "k_decayed", ())],
            both(("pe", "kq"), ("dve", "qk_decay")),
            both(("pe", "kk"), ("dve", "a_low")) + [("act", "silu", ("in0", 9)), ("act", "logs", ())], both(("pe", "turn_a"), ("dve", "base16")),
            both(("pe", "pow2"), ("act", "pow2_n"), ("dve", "pow2_a")), both(("pe", "pow4"), ("act", "pow4_n"), ("dve", "pow4_a")),
            both(("pe", "pow8"), ("act", "pow8_a"), ("dve", "pow8_m")), both(("pe", "pow16"), ("dve", "pow16_m")),
            both(("pe", "turn_m"), ("act", "t_rows"), ("pool", "corner", 0))]
    for s in range(3):
        out += [both(("pe", "double_y", s), ("act", "y", s)),
                both(("pe", "double", s), ("dve", "doubled", s), *([("pool", "corner", s + 1)] if s < 2 else []))]
    return out


def delta_end():
    return [[("pe", "u", (0,)), ("act", "v_new", (0,))], [("pe", "state", ()), ("act", "state_copy", ())],
            [("pe", "from_state", ()), ("dve", "v_less", ())], [("pe", "u", (1,)), ("act", "v_new", (1,))],
            [("pe", "delta_out", (0,))]] + merge([[("pe", "delta_out", (1,))]], rounds(NORM_COLS, [("do", 0), ("do", 1)]))


def retention_rounds():
    return (rounds(ROPE, [("r64", 0), ("r64", 1)])
            + rounds([("pe", "ret_out", 1), ("pe", "ret_scores", 0), ("dve", "ret_decay", 0)], [0, 1, 2, 3])
            + rounds(NORM_COLS, [("ro", 0), ("ro", 1)]))


def hgrn_rounds(l):
    out = [[("dve", "f_abs", (l,)), ("act", "f_ln", (l,))], [("dve", "f_log", (l,))]]
    if l:
        out += [[("act", "f_ln2", (l,)), ("dve", "f_log2", (l,))]]
    out += [[("act", "k_gate", (l,)), ("dve", "cum_f", (l,))], [("pe", "diagonal", (l,)), ("dve", "diagonal_in", (l,))]]
    ahead = len(out)
    for r in range(8 + 2):
        out.append([(e, k, (l, v)) for e, k, v in
                    [("dve", "gap_f", r), ("act", "decay_f", r), ("dve", "q_level", r - 1), ("pool", "k_level", r - 1),
                     ("pe", "level", r - 2), ("dve", "level_in", r - 2)] if 0 <= v < 8])
    return out + [[("pe", "hgrn_out", (l, g)) for g in (0, 1)]], ahead


def last_mixer(l):
    hgrn, ahead = hgrn_rounds(l)
    hgrn[ahead + 9] += [("act", "silu", (f"in2_{l}", 15)), ("act", "logs", ())]
    n = ahead + 9
    qk = [(f"mq{l}", 0), (f"mk{l}", 0), (f"mq{l}", 1), (f"mk{l}", 1)]
    h = n + 7
    chains = [rounds(NORM_COLS, [(f"sk{l}", 0), (f"sk{l}", 1)]), hgrn,
              [[]] * n + rounds(NORM_COLS, qk + [(f"ho{l}", 0), (f"ho{l}", 1), (f"sq{l}", 0), (f"sq{l}", 1)]),
              [[]] * (n + 2) + rounds(ROPE, qk),
              [[]] * (h + 11) + [[("dve", "gate_out", ((f"moba{l}", g),)) for g in (0, 1)]],
              [[]] * h + rounds(ATTEND, [(f"moba{l}", i) for i in range(8)] + [(f"matt{l}", i) for i in range(4)]),
              [[]] * (h + 13) + [y_splits(l, 0), y_splits(l, 2)]]
    if l == 0:
        load, *stats = mem_norm(1)
        chains += [[[]] * (h + 1) + [[load]] + [[]] * 3 + [[s for s in stats if s[1] in ("sumsq", "rstd")]] +
                   [[s for s in stats if s[1] == "scale"] + next_gain("mem1")]]
    places = [n + r for r in BESIDE_2]
    out = weave(merge(*chains), halves(panel_list(f"in2_{l}", None, 4)), places)
    return (out + late_splits(f"in2_{l}") + [("dve", "gate_out", ((f"matt{l}", g),)) for g in (0, 1)]
            + y_splits(l, 8) + y_splits(l, 10))


def late_splits(name):
    n = BASE[name] + N_OF[name]
    return splits(n + 1, n + 2)


def y_splits(l, b):
    return [("act", "y_hi", (l, b)), ("dve", "y_lo", (l, b))]


def splits(*ns):
    return [(e, k, (n,)) for n in ns for e, k in (("act", "split_hi"), ("dve", "split_lo"))]


def row_stats(tag, t):
    return [("act", "sumsq", (tag, t, 0)), ("act", "sumsq", (tag, t, 1)), ("act", "rstd", (tag, t))]


def mem_norm(l):
    tag = f"mem{l}"
    return [("pool", "load", (tag,))] + row_stats(tag, 0) + row_stats(tag, 1) + \
        [(e, k, (tag, t, half)) for t in (0, 1) for half in (0, 1) for e, k in (("dve", "scale"), ("pe", "turn_x"))] + next_gain(tag)


def split_rows(tag):
    return [s for t in (0, 1) for half in (0, 1) for s in (("act", "x_hi", (tag, t, half)), ("dve", "x_lo", (tag, t, half)))]


def order():
    out = [("sp", "load", (x,)) for x in ("x", "gain_ffn0", "const", "small")]
    out += [("pool", "zero", ()), ("pool", "load", ("tab1",)), ("act", "logs", ())]
    i = norm_steps("ffn0").index(("act", "x_hi", ("ffn0", 0, 0)))
    out += norm_steps("ffn0")[:i] + splits(0) + norm_steps("ffn0")[i:] + splits(1, 2)
    out += [("act", "wab_hi", ()), ("dve", "wab_lo", ())] + ffn_steps(0)[-3:] + ffn_tail(0)
    out += norm_steps("mix0")
    for p, (product, evacuate, *late) in enumerate(panel_list("in0", None, 0, 6)):
        out += [product, evacuate, ("act", "tap", (p,)), ("dve", "conv", (p,))] + [("act", "conv_silu", (p - 1,))][:p] + late
        if p == 0:
            out += [("pe", "ab_mm", ())]
    out += [("act", "conv_silu", (5,)), ("act", "logs", ()), ("act", "ab_exp", ()), ("dve", "ab", ())]
    out += weave(delta_rounds(), halves(panel_list("in0", None, 6)), BESIDE_0)
    out += sum(merge(delta_end(), retention_rounds()), []) + late_splits("in0")
    out += [("pool", "load", ("gain_ffn1",)), ("pool", "load", ("tab2",))] + panel_steps("out0")
    out += ffn_steps(1) + ffn_tail(1) + ffn_steps(2) + ffn_tail(2) + norm_steps("mix1") + [("dve", "lam_mul", ())]
    out += panel_steps("in1", {0: [("pe", "lam_sum", ())], 1: [("act", "lam_exp", ()), ("dve", "lam", ())]}, 0, 4)
    out += weave(rounds(ROPE, [("r64b", g) for g in (0, 2, 1, 3)]), panel_list("in1", None, 4, 8), range(4))
    ropes = [[(e, k, (("r128", g),)) for g in pair for e, k, _ in ROPE] for pair in ((0, 2), (1, 3))]
    heads = rounds(ATTEND_TWO, [("dif", h) for h in range(4)] + [("dil", h) for h in range(4)])
    pair = lambda *steps: [(e, k, (("fo", g),)) for e, k in steps for g in (0, 1)]
    norms = [pair(("act", "cn_sq")), pair(("pe", "cn_sum"), ("act", "cn_rstd"), ("dve", "cn_use"))]
    out += weave(merge(ropes, heads, [[]] * 7 + norms, [[]] * 9 + [[("dve", "gate_out", (("dil", 0),))]]),
                 halves(panel_list("in1", None, 8)), BESIDE_1)
    out += late_splits("in1") + [("dve", "gate_out", (("dil", 1),))]
    out += [("pool", "load", ("tab3",)), ("pool", "load", ("pos",))] + panel_steps("out1")
    product, *late, last = ffn_tail(3)
    turns = [s for s in mem_norm(0) if s[1] == "turn_x"]
    out += ffn_steps(3) + [s for s in mem_norm(0) if s not in turns] + [product] + turns + late + split_rows("mem0") + [last]
    first, *others = panel_list("mem0")
    out += [("dve", "split_lo", (LATE["ffn3"][0] - 1,))]
    for t in range(TILES):
        out += [("dve", "residual", ("ffn3", t, half)) for half in (0, 1)] + row_stats("final", t)
    out += splits(*range(*LATE["ffn3"]))
    out += [("dve", "scale", ("final", t, half)) for t in (0, 1) for half in (0, 1)] + next_gain("final") + first
    out += row_stats("pre0", 0) + row_stats("pre0", 1)
    for l in range(2):
        product, *late = others[2]
        out += others[0] + [("dve", "scale", (f"pre{l}", t, half)) for t in (0, 1) for half in (0, 1)] + next_gain(f"pre{l}")
        out += others[1] + [product, late[0]]
        out += [("pe", "turn_x", (f"pre{l}", t, half)) for t in (0, 1) for half in (0, 1)] + split_rows(f"pre{l}") + late[1:]
        angles = {1: [("dve", "angle", ())], 3: [("act", "sines", ())]} if l == 0 else None
        out += panel_steps(f"in2_{l}", angles, 0, 4) + [("act", "logs", ())] + last_mixer(l)
        if l == 0:
            turns = [("pe", "turn_x", ("mem1", t, half)) for t in (0, 1) for half in (0, 1)]
            out += panel_steps("out2_0", None, 0, 4) + turns + panel_steps("out2_0", None, 4) + split_rows("mem1")
            first, *others = panel_list("mem1")
            out += [("dve", "residual", ("out2_0", t, half)) for t in (0, 1) for half in (0, 1)]
            out += row_stats("pre1", 0) + row_stats("pre1", 1)
            out += [("dve", "split_lo", (LATE["out2_0"][0] - 1,))] + splits(*range(*LATE["out2_0"])) + first
        else:
            out += panel_steps("out2_1")
    for t in range(TILES):
        for half in range(2):
            out += [("dve", "residual", ("out2_1", t, half)), ("pool", "store", (t, half))]
    return out


ORDER = order()
COUNT_AT = {}
_counts = {}
for _e, _k, _a in ORDER:
    if _k not in UNCOUNTED:
        _counts[_e] = _counts.get(_e, 0) + 1
        assert (_e, _k, _a) not in COUNT_AT, (_e, _k, _a)
        COUNT_AT[_e, _k, _a] = _counts[_e]


def at(engine, kind, *args):
    return COUNT_AT[engine, kind, args]


def build(nc, x_in, mem_in, pos_in, panels, gains, small_in, tab0, tab1, tab2, tab3, out):
    with ExitStack() as ctx:
        def sb(name, shape, dt=F32):
            return ctx.enter_context(nc.sbuf_tensor(name, shape, dt))

        def sem(name):
            return ctx.enter_context(nc.semaphore(name))

        raw = sb("raw", [P, SLOTS, PANEL])
        w_hi = sb("w_hi", [P, SLOTS, PANEL], F32R)
        w_lo = sb("w_lo", [P, SLOTS, PANEL], F32R)
        x = sb("x", [P, TILES, D])
        act_hi = sb("act_hi", [P, 12, SEQ], F32R)
        act_lo = sb("act_lo", [P, 12, SEQ], F32R)
        g_hi = sb("g_hi", [P, 2, 2, SEQ], F32R)
        g_lo = sb("g_lo", [P, 2, 2, SEQ], F32R)
        pair = sb("pair", [P, 2048])
        xn = sb("xn", [P, TILES * D])
        gain = sb("gain", [P, D])
        const = sb("const", [P, tab0.shape[1]])
        table = sb("table", [P, TABLE_W])
        small = sb("small", [P, SMALL_W])
        wab_h = sb("wab_h", [P, 64], F32R)
        wab_l = sb("wab_l", [P, 64], F32R)
        stat = sb("stat", [P, 102])
        work = sb("work", [P, WORK])
        ps = ctx.enter_context(nc.psum_tensor("ps", [P, 8, 512], F32))

        silu_buf, g32 = pair[:, 0:512], pair[:, 512:1024]
        sq = [pair[:, 0:512], pair[:, 512:1024]]
        rs = [pair[:, 1024:1536], pair[:, 1536:2048]]
        y32 = xn[:, 0:512]

        def cst(name):
            a, n = PLACES[0][name]
            return const[:, a:a + n]

        def tab(s, name):
            a, n = PLACES[s][name]
            return table[:, a:a + n]

        def sm(name, j=0, n=1):
            a, _ = SMALL[name]
            return small[:, a + j:a + j + n]

        def region(a, *shape):
            n = int(np.prod(shape))
            v = work[:, a:a + n]
            if len(shape) == 2:
                return v.rearrange("p (a b) -> p a b", a=shape[0])
            if len(shape) == 3:
                return v.rearrange("p (a b c) -> p a b c", a=shape[0], b=shape[1])
            return v

        def grid(ap, a):
            return ap.rearrange("p (a b) -> p a b", a=a)

        def spread(ap, n):
            return ap.rearrange("p (a b) -> p a b", a=1).broadcast_to([P, n, ap.shape[1]])

        def along(ap, n):
            return ap.rearrange("p (b o) -> p b o", o=1).broadcast_to([P, ap.shape[1], n])

        ident = cst("ident")

        raw_qkv = region(0, 12, 260)
        qk = region(3120, 8, SEQ)
        vc = region(5168, 4, SEQ)
        z0 = region(6192, 4, SEQ)
        rqk = region(7216, 4, SEQ)
        rv = region(8240, TILES, 512)
        rg = region(9264, 4, SEQ)
        a_low = region(10288, TILES, 4, P)
        decay_t = region(11312, TILES, 4, P)
        pw_a = region(12336, TILES, 4, P)
        pw_n = region(13360, TILES, 4, P)
        assert 14384 <= WORK
        pw_a4 = region(5168, TILES, 4, P)
        pw_n4 = region(1024, TILES, 4, P)
        t_mat = xn[:, 1024:2048].rearrange("p (t h n) -> p t h n", t=TILES, h=4)
        m_mat = region(14384, TILES, 4, P)
        v_beta = region(0, TILES, 4, P)
        v_new = region(1024, TILES, 4, P)
        state = region(2048, 4, P)
        k_dec = region(2560, 4, P)
        q_dec = gain[:, 0:512].rearrange("p (h n) -> p h n", h=4)
        ret_p = region(12336, 4, 384)

        cqk = region(0, 8, SEQ)
        cv = region(2048, TILES, 512)
        dv = region(3072, TILES, 512)
        dqk = region(7168, 8, SEQ)
        km = region(0, 4, SEQ)
        vm = region(1024, TILES, 512)
        mo_qk = region(2048, 8, SEQ)
        probs = region(4096, 2, 2, 512)
        p_t = region(6144, 2, 512)
        mem_squares = region(7168, TILES * D)
        qh = region(9216, 4, SEQ)
        fh = region(10240, 4, SEQ)
        mo_v = region(9216, TILES, 512)
        qm = region(10240, 4, SEQ)
        ih = region(11264, TILES, 512)
        z2 = region(12288, 12, SEQ)
        assert 15360 <= WORK
        hg = [region(4096 + 1024 * i, 4, SEQ) for i in range(4)]
        k_g, q_l = hg[0], (hg[1], hg[2])
        dec_f = [grid(pair[:, 1024 * i:1024 * i + 1024], 4) for i in range(2)]
        k_l = [grid(xn[:, 1024 * i:1024 * i + 1024], 4) for i in range(2)]
        h_s = region(7168, TILES, 4, P)
        h_s01 = region(8192, 4, P)
        positions = region(4096, SEQ).bitcast(I32)
        cos_a = table[:, TABLE_W - 512:TABLE_W - 256]
        sin_a = table[:, TABLE_W - 256:TABLE_W]
        ang, turns = region(5120, SEQ), region(6144, SEQ)

        half_mean, rstd, sumsq = stat[:, 0:2], stat[:, 2:4], stat[:, 98:102]
        b_exp, beta, xa, e_sp = (stat[:, 4 + 8 * i:12 + 8 * i] for i in range(4))
        g_col, gc, e_gc, bge = (stat[:, 36 + 8 * i:44 + 8 * i] for i in range(4))
        e_alog, e_kd = stat[:, 68:72], stat[:, 72:76]
        nmax = (stat[:, 76:80], stat[:, 80:84])
        dens = (stat[:, 84:88], stat[:, 88:92])
        lam_c = stat[:, 92:96]
        dgain = stat[:, 96:97]
        zero4 = stat[:, 97:98]
        lbd, lbn, lbl = stat[:, 4:12], stat[:, 12:20], stat[:, 20:28]

        done = {e: sem(f"{e}_done") for e in ("pe", "act", "dve", "pool")}
        pe_done, act_done, dve_done, pool_done = (done[e] for e in ("pe", "act", "dve", "pool"))
        act_chain, dve_chain = sem("act_chain"), sem("dve_chain")
        panel_loaded = [sem(f"panel_loaded_{i}") for i in range(SLOTS)]
        panel_hi, panel_lo, panel_used = sem("panel_hi"), sem("panel_lo"), sem("panel_used")
        silu_done, gate_read, gate_hi, gate_ready = (sem(n) for n in ("silu_done", "gate_read", "gate_hi", "gate_ready"))
        loads = [a[0] for e, k, a in ORDER if k == "load"]
        loaded = {n: sem(f"loaded_{n}") for n in loads}
        stored = sem("stored")
        bank_ready = sem("bank_ready")

        def evac(name, k):
            return ("act", "evacuate", name, k)

        ropes = {}
        for g in range(2):
            ropes["r64", g] = (rqk[:, 2 * g:2 * g + 2], tab(1, "swap64"), tab(1, "cos64"), tab(1, "sin64"), 2 + g, evac("in0", 13))
        for g in range(4):
            ropes["r128", g] = (cqk[:, 2 * g:2 * g + 2], tab(2, "swap128"), tab(2, "cos128"), tab(2, "sin128"), 6 + g // 2,
                                evac("in1", 4 + g))
            ropes["r64b", g] = (dqk[:, 2 * g:2 * g + 2], tab(2, "swap64"), tab(2, "cos64"), tab(2, "sin64"), 6 + g // 2,
                                evac("in1", g))
            for l in range(2):
                unit_ = ((f"mq{l}", f"mk{l}")[g // 2], g % 2)
                ropes[unit_] = (mo_qk[:, 2 * g:2 * g + 2], tab(3, "swapp"), cos_a, sin_a, 2 + g // 2, ("dve", "cn_use", unit_))
        rope_list = [a for e, k, a in ORDER if k == "swap"]
        rope_index = {a[0]: i for i, a in enumerate(rope_list)}

        norms = {}
        for g in range(2):
            s2 = slice(2 * g, 2 * g + 2)
            s4 = slice(4 + 2 * g, 6 + 2 * g)
            ones, ones64 = cst("ones"), cst("ones64")
            norms["dq", g] = (qk[:, s2], ones, 1.0, P ** -0.5, qk[:, s2], None, None, g, ("act", "conv_silu", g))
            norms["dk", g] = (qk[:, s4], ones, 1.0, 1.0, qk[:, s4], None, None, g, ("act", "conv_silu", 2 + g))
            norms["do", g] = (grid(ps[:, 6 + g], 2), ones, 1 / P, sm("gdn"), None, z0[:, s2], 2 * g, g, ("pe", "delta_out", g))
            norms["ro", g] = (grid(ps[:, 4 + g], 2), ones, 1 / P, 1.0, None, rg[:, s2], 4 + 2 * g, 2 + g, ("pe", "ret_out", 2 * g + 1))
            norms["fo", g] = (grid(ps[:, 6 + g], 2), ones, 1 / P, dgain, None, None, 4 + 2 * g, g, ("pe", "attend", ("dif", 2 * g + 1)))
            for l in range(2):
                norms[f"mq{l}", g] = (mo_qk[:, s2], ones64, 1 / 64, sm(f"mq{l}"), mo_qk[:, s2], None, None, 0, evac(f"in2_{l}", 6 + g))
                norms[f"mk{l}", g] = (mo_qk[:, s4], ones64, 1 / 64, sm(f"mk{l}"), mo_qk[:, s4], None, None, 1, evac(f"in2_{l}", 8 + g))
                norms[f"sq{l}", g] = (qm[:, s2], ones, 1 / P, sm(f"sq{l}"), qm[:, s2], None, None, 6 + g, evac(f"in2_{l}", 16 + g))
                norms[f"sk{l}", g] = (km[:, s2], ones, 1 / P, sm(f"sk{l}"), km[:, s2], None, None, 6 + g, evac(f"mem{l}", g))
                norms[f"ho{l}", g] = (grid(ps[:, 6 + g], 2), ones, 1 / P, sm(f"ho{l}"), None, z2[:, 4 + 2 * g:6 + 2 * g], 8 + 2 * g, g,
                                      ("pe", "hgrn_out", l, g))
        norm_list = [a[0] for e, k, a in ORDER if k == "cn_sum"]
        norm_index = {u: i for i, u in enumerate(norm_list)}

        atts = {}
        for h in range(4):
            o = lambda b, j: ps[:, b, SEQ * j:SEQ * (j + 1)]
            col = slice(P * h, P * h + P)
            atts["dil", h] = ([(cqk[:, h], cqk[:, 4 + h])], cv[:, :, col], o(4 + h // 2, h % 2), False, tab(2, "union"),
                              tab(2, "times"), P ** -0.5, ("dve", "rope", ("r128", 3)))
            atts["dif", h] = ([(dqk[0:64, h], dqk[0:64, 4 + h]), (dqk[64:128, h], dqk[64:128, 4 + h])], dv[:, :, col],
                              o(6 + h // 2, h % 2), False, tab(2, "causal"), None, 0.125,
                              ("dve", "rope", ("r64b", 2 + h // 2)))
            for l in range(2):
                atts[f"matt{l}", h] = ([(qm[:, h], km[:, h])], vm[:, :, col], o(6 + h // 2, h % 2), True, None, None, P ** -0.5,
                                       ("dve", "cn_use", (f"sq{l}", 1)))
        for h in range(8):
            r = slice(64 * (h % 2), 64 * (h % 2) + 64)
            for l in range(2):
                atts[f"moba{l}", h] = ([(mo_qk[r, h // 2], mo_qk[r, 4 + h // 2])], mo_v[:, :, 64 * h:64 * h + 64],
                                       ps[r, 6 + h // 4, SEQ * (h // 2 % 2):SEQ * (h // 2 % 2) + SEQ], False, tab(3, "causal"), None, 0.125,
                                       ("dve", "rope", (f"mk{l}", h // 4)))
        att_list = [a[0] for e, k, a in ORDER if k == "scores"]
        att_index = {u: i for i, u in enumerate(att_list)}
        gates = {}
        for g in range(2):
            gates["dil", g] = (None, 4 + g, ("dil", 2 * g + 1))
            for l in range(2):
                gates[f"moba{l}", g] = (z2[:, 2 * g:2 * g + 2], 6 + g, (f"moba{l}", 4 * g + 3))
                gates[f"matt{l}", g] = (z2[:, 8 + 2 * g:10 + 2 * g], 6 + g, (f"matt{l}", 2 * g + 1))

        def score_bank(unit, m, back=False):
            i = att_index[unit]
            two = lambda u_: len(atts[u_][0]) == 2
            if back:
                return 1 if two(unit) or (i and two(att_list[i - 1])) else 2
            return m if two(unit) else i % 2

        def spans(full):
            return [(0, 256), (256, 512)] if full else [(0, 128), (128, 384)]

        dest = {}
        for k in range(6):
            dest["in0", k] = (raw_qkv[:, 2 * k:2 * k + 2, 4:260], "cols", ACT.Copy)
        rows = lambda r, k: r[:, :, UPW * k:UPW * (k + 1)]
        blocks = lambda r, k: r[:, 2 * k:2 * k + 2]
        for k in range(2):
            dest["in0", 6 + k] = (blocks(z0, k), "cols", ACT.Copy)
            dest["in0", 8 + k] = (blocks(rg, k), "cols", ACT.Copy)
            dest["in0", 10 + k] = (blocks(rqk, k), "cols", ACT.Copy)
            dest["in0", 12 + k] = (rows(rv, k), "rows", ACT.Copy)
            dest["in1", 8 + k] = (rows(dv, k), "rows", ACT.Copy)
            dest["in1", 10 + k] = (rows(cv, k), "rows", ACT.Copy)
            for l in range(2):
                dest[f"in2_{l}", k] = (blocks(qh, k), "cols", ACT.Silu)
                dest[f"in2_{l}", 2 + k] = (blocks(fh, k), "cols", ACT.Copy)
                dest[f"in2_{l}", 4 + k] = (rows(ih, k), "rows", ACT.Copy)
                dest[f"in2_{l}", 16 + k] = (blocks(qm, k), "cols", ACT.Copy)
                dest[f"in2_{l}", 18 + k] = (rows(mo_v, k), "rows", ACT.Copy)
                dest[f"mem{l}", k] = (blocks(km, k), "cols", ACT.Copy)
                dest[f"mem{l}", 2 + k] = (rows(vm, k), "rows", ACT.Copy)
        for k in range(4):
            dest["in1", k] = (blocks(dqk, k), "cols", ACT.Copy)
            dest["in1", 4 + k] = (blocks(cqk, k), "cols", ACT.Copy)
            for l in range(2):
                dest[f"in2_{l}", 6 + k] = (blocks(mo_qk, k), "cols", ACT.Copy)
        for k in range(6):
            for l in range(2):
                dest[f"in2_{l}", 10 + k] = (blocks(z2, k), "cols", ACT.Copy)

        def bank_of(name, k):
            return 4 + (BASE[name] + k) % 2

        def source_of(tag, t, half):
            if tag == "ffn0":
                return x, ("load", "x")
            if tag.startswith("mem"):
                return xn[:, :].rearrange("p (t d) -> p t d", t=TILES), ("load", tag)
            return x, (("dve", "scale", "final", t, half) if tag == "pre0" else ("dve", "residual", RESIDUALS[tag], t, half))

        xn_rows = xn[:, :].rearrange("p (t d) -> p t d", t=TILES)
        last_use = {}
        for i, g in enumerate(GAINS[1:]):
            last_use["gain_" + g] = ("dve", "scale", GAINS[i], 1, 1)
        last_use["tab1"] = ("dve", "x_lo", "ffn0", 1, 1)
        last_use["tab2"] = ("dve", "cn_use", ("ro", 1))
        last_use["tab3"] = last_use["pos"] = ("dve", "gate_out", ("dil", 1))
        last_use["mem0"] = ("dve", "x_lo", "ffn3", 1, 1)
        last_use["mem1"] = ("dve", "cn_use", ("ho0", 1))
        last_use["gain_ffn1"] = ("dve", "cn_use", ("ro", 1))

        def of(j, const, step):
            return const if j is None else j * step + const

        def steps(engine, handlers):
            for e, kind, args in ORDER:
                if e == engine:
                    handlers[kind](*args)

        def delta_bank(t, i):
            return (0, 1, 2, 3, 6, 7)[3 * t + i]

        def turn_bank(tag, t, half):
            return (4 if tag.startswith("mem") else 0) + 2 * t + half

        def out_block(b):
            return slice(b, b + 2) if b < 4 else slice(b - 4, b - 2)

        def conv_out(b):
            return qk[:, b] if b < 8 else vc[:, b - 8]

        block = ctx.enter_context(nc.Block())

        places = {"x": (x[:], x_in), "const": (const[:], tab0), "small": (small[:], small_in),
                  "tab1": (table[:, 0:tab1.shape[1]], tab1), "tab2": (table[:, 0:tab2.shape[1]], tab2),
                  "tab3": (table[:, 0:tab3.shape[1]], tab3),
                  "pos": (positions, pos_in.rearrange("(a n) -> a n", a=1).broadcast_to([P, SEQ])),
                  "mem0": (xn_rows, mem_in), "mem1": (xn_rows, mem_in)}
        for i, g in enumerate(GAINS):
            places["gain_" + g] = (gain[:], gains[i:i + 1].broadcast_to([P, D]))

        @block.sync
        def _(sp):
            steps("sp", {"load": lambda tag: sp.dma_start(*places[tag]).then_inc(loaded[tag], 16)})

            def load_panel(s, g):
                if isinstance(g, int) and g == 0:
                    sp.dma_start(raw[:, s], panels[s]).then_inc(panel_loaded[s], 16)
                    return
                sp.wait_ge(panel_lo, g * SLOTS + (s + 1 - SLOTS))
                sp.dma_start(raw[:, s], panels[g * SLOTS + s]).then_inc(panel_loaded[s], 16)

            for s in range(SLOTS):
                load_panel(s, 0)
            with sp.Fori(1, PANELS // SLOTS) as g:
                for s in range(SLOTS):
                    load_panel(s, g)
            for s in range(PANELS % SLOTS):
                load_panel(s, PANELS // SLOTS)

        @block.gpsimd
        def _(pool):
            def load(tag):
                if tag in last_use:
                    pool.wait_ge(done[last_use[tag][0]], at(*last_use[tag]))
                to, of_ = places[tag]
                pool.dma_start(to, of_).then_inc(loaded[tag], 16)

            def zero():
                nc.gpsimd.memset(raw_qkv[:, :, 0:4], 0.0)
                nc.gpsimd.memset(zero4, 0.0).then_inc(pool_done, 1)

            def corner(s, t):
                pool.wait_ge(dve_done, at("dve", "base16", t))
                pool.wait_ge(pe_done, at("pe", "double_y", s - 1, t) if s else at("pe", "pow4", t))
                nc.gpsimd.tensor_tensor(pw_n[:, t], a_low[:, t], spread(tab(1, ("e16", "e32", "e64")[s]), 4), ALU.mult).then_inc(pool_done, 1)

            def k_level(l, v):
                if v == 0:
                    pool.wait_ge(act_done, at("act", "k_gate", l))
                pool.wait_ge(act_done, at("act", "decay_f", l, v))
                if v >= 2:
                    pool.wait_ge(pe_done, at("pe", "level", l, v - 2))
                nc.gpsimd.tensor_tensor(k_l[v % 2], k_g, dec_f[v % 2], ALU.mult).then_inc(pool_done, 1)

            def store(t, half):
                c = slice(512 * half, 512 * half + 512)
                pool.wait_ge(dve_done, at("dve", "residual", "out2_1", t, half))
                pool.dma_start(out[:, t, c], x[:, t, c]).then_inc(stored, 16)
                if (t, half) == (TILES - 1, 1):
                    pool.wait_ge(stored, 16 * TILES * 2)

            steps("pool", {"load": load, "zero": zero, "corner": corner, "k_level": k_level, "store": store})

        @block.tensor
        def _(pe):
            def three(o, l, r, start, stop):
                pe.matmul(o, l[0], r[0], start=start, stop=False)
                pe.matmul(o, l[0], r[1], start=False, stop=False)
                return pe.matmul(o, l[1], r[0], start=False, stop=stop)

            def weight(slot, c, a, n, width):
                return [w[:, slot, c * width + a:c * width + a + n] for w in (w_hi, w_lo)]

            def up(slot, bank, form, n, j=None, step=0, tag=None, parts=(0, 1)):
                pe.wait_ge(panel_lo, of(j, n + 1, step))
                for half in parts:
                    o = ps[:, bank, SEQ * half:SEQ * (half + 1)]
                    for c in range(DC):
                        if tag and half == 0 and c % 4 == 0:
                            pe.wait_ge(dve_done, at("dve", "x_lo", tag, 1, c // 4))
                        if form == "cols":
                            l = weight(slot, c, P * half, P, UPW)
                            r = [a[:, c, :] for a in (act_hi, act_lo)]
                        else:
                            l = [a[:, c, P * half:P * half + P] for a in (act_hi, act_lo)]
                            r = weight(slot, c, 0, UPW, UPW)
                        ins = three(o, l, r, c == 0, c == DC - 1)
                if parts[-1] == 1:
                    ins.then_inc(panel_used, 1)

            def down(slot, parts, first, last, n, j=None, step=0):
                pe.wait_ge(panel_lo, of(j, n + 1, step))
                for t in range(TILES):
                    for half in range(2):
                        for c in range(2):
                            l = [a[:, c, P * t:P * t + P] for a in parts]
                            ins = three(ps[:, 2 * t + half], l, weight(slot, c, 512 * half, 512, D),
                                        first and c == 0, last and c == 1)
                        if last and (t, half) != (TILES - 1, 1):
                            ins.then_inc(bank_ready, 1)
                ins.then_inc(panel_used, 1)

            def ffn(f):
                b, c = BASE[f"ffn{f}"], f * UPS
                tag = f"ffn{f}"

                def gate_up(i, j=None):
                    n = b + (0 if i == 0 else 3 * i - 1)
                    if i:
                        pe.wait_ge(gate_read, of(j, c + i, 2))
                    up(n % SLOTS, 4, "cols", n, j, 6, None if i else tag)
                    up((n + 1) % SLOTS, 5, "cols", n + 1, j, 6)

                def down_of(i, j=None):
                    n = b + (3 * i + 4 if i < UPS - 1 else 3 * UPS - 1)
                    pe.wait_ge(gate_ready, of(j, c + i + 1, 2))
                    down(n % SLOTS, (g_hi[:, i % 2], g_lo[:, i % 2]), i == 0, i == UPS - 1, n, j, 6)

                gate_up(0)
                gate_up(1)
                down_of(0)
                with pe.Fori(0, (UPS - 3) // 2) as j:
                    for i in (2, 3):
                        gate_up(i, j)
                        down_of(i - 1, j)
                gate_up(UPS - 1)

            def ffn_down(f, i):
                b, c = BASE[f"ffn{f}"], f * UPS
                n = b + (3 * i + 4 if i < UPS - 1 else 3 * UPS - 1)
                pe.wait_ge(gate_ready, c + i + 1)
                down(n % SLOTS, (g_hi[:, i % 2], g_lo[:, i % 2]), i == 0, i == UPS - 1, n)

            def panel(name, k, parts=(0, 1)):
                n = BASE[name] + k
                if name.startswith("out"):
                    last = {("out0", 0): ("cn_use", ("do", 1)), ("out0", 2): ("cn_use", ("ro", 1)), ("out1", 0): ("cn_use", ("fo", 1)), ("out1", 2): ("gate_out", ("dil", 1))}
                    for l in range(2):
                        last.update({(f"out2_{l}", 0): ("cn_use", (f"ho{l}", 1)), (f"out2_{l}", 2): ("y_lo", l, 2),
                                     (f"out2_{l}", 4): ("y_lo", l, 10)})
                    if (name, k) in last:
                        pe.wait_ge(dve_done, at("dve", *last[name, k]))
                    if (name, k) == ("out0", 0):
                        pe.wait_ge(act_done, at("act", "cn_rstd", ("ro", 1)))
                    b = {"out0": 2 * k, "out1": (2 * k + 4) % 8}.get(name, (2 * k + 8) % 12)
                    parts = (act_hi[:, b:b + 2], act_lo[:, b:b + 2])
                    down(n % SLOTS, parts, k == 0, k == N_OF[name] - 1, n)
                else:
                    tag = {"in0": "mix0", "in1": "mix1", "in2_0": "pre0", "in2_1": "pre1"}.get(name, name)
                    if k >= 2:
                        pe.wait_ge(act_done, at("act", "evacuate", name, k - 2))
                    up(n % SLOTS, bank_of(name, k), dest[name, k][1], n, tag=None if k else tag, parts=parts)

            def half_panel(name, k, half):
                panel(name, k, (half,))

            def turn_x(tag, t, half):
                pe.wait_ge(dve_done, at("dve", "scale", tag, t, half))
                pe.wait_ge(loaded["const"], 16)
                if tag == "mem0":
                    pe.wait_ge(gate_read, 4 * UPS)
                for c in range(4 * half, 4 * half + 4):
                    ins = pe.transpose(ps[:, turn_bank(tag, t, half), P * (c % 4):P * (c % 4) + P], xn_rows[:, t, P * c:P * c + P], ident)
                ins.then_inc(pe_done, 1)

            def ab_mm():
                pe.wait_ge(dve_done, at("dve", "wab_lo"))
                for t in range(TILES):
                    for c in range(DC):
                        l = [a[:, c, P * t:P * t + P] for a in (act_hi, act_lo)]
                        ins = three(ps[:, 6, 8 * t:8 * t + 8], l, [w[:, 8 * c:8 * c + 8] for w in (wab_h, wab_l)], c == 0, c == DC - 1)
                ins.then_inc(pe_done, 1)

            def heads(o, lhs, rhs, turn=False):
                for h in range(4):
                    oh = o[:, P * h:P * h + P]
                    ins = pe.transpose(oh, lhs(h), ident) if turn else pe.matmul(oh, lhs(h), rhs(h), start=True, stop=True)
                return ins

            def cumsum():
                pe.wait_ge(dve_done, at("dve", "g"))
                pe.wait_ge(loaded["tab1"], 16)
                up_ = tab(1, "upper")
                for t in range(TILES):
                    pe.matmul(ps[:, 6, 4 * t:4 * t + 4], up_, g_col[:, 4 * t:4 * t + 4], start=True, stop=True)
                for t in range(TILES):
                    ins = heads(ps[:, 2 + t], lambda h: g_col[:, 4 * t + h:4 * t + h + 1].broadcast_to([P, P]), lambda h: up_)
                ins.then_inc(pe_done, 1)

            tok = lambda t: slice(P * t, P * t + P)

            def turn_v(t):
                pe.wait_ge(act_done, at("act", "conv_silu", 5))
                pe.wait_ge(dve_done, at("dve", "cn_use", ("dk", 1)))
                heads(ps[:, t], lambda h: vc[:, h, tok(t)], None, turn=True).then_inc(pe_done, 1)

            def turn_k():
                pe.wait_ge(dve_done, at("dve", "v_beta", 0))
                heads(ps[:, 2], lambda h: qk[:, 4 + h, tok(0)], None, turn=True).then_inc(pe_done, 1)

            def kk(t):
                pe.wait_ge(dve_done, at("dve", "k_decayed"))
                heads(ps[:, delta_bank(t, 0)], lambda h: qk[:, 4 + h, tok(t)], lambda h: qk[:, 4 + h, tok(t)]).then_inc(pe_done, 1)

            def turn_a(t):
                pe.wait_ge(dve_done, at("dve", "a_low", t))
                heads(ps[:, delta_bank(t, 1)], lambda h: a_low[:, t, h], None, turn=True).then_inc(pe_done, 1)

            def pow2(t):
                pe.wait_ge(dve_done, at("dve", "base16", t))
                heads(ps[:, delta_bank(t, 0)], lambda h: pw_a4[:, t, h], lambda h: t_mat[:, t, h])
                heads(ps[:, delta_bank(t, 1)], lambda h: t_mat[:, t, h], lambda h: pw_a4[:, t, h]).then_inc(pe_done, 1)

            def pow4(t):
                pe.wait_ge(act_done, at("act", "pow2_n", t))
                pe.wait_ge(dve_done, at("dve", "pow2_a", t))
                heads(ps[:, delta_bank(t, 0)], lambda h: pw_a[:, t, h], lambda h: pw_n[:, t, h])
                heads(ps[:, delta_bank(t, 1)], lambda h: pw_n[:, t, h], lambda h: pw_a[:, t, h])
                heads(ps[:, delta_bank(t, 2)], lambda h: pw_a[:, t, h], lambda h: m_mat[:, t, h]).then_inc(pe_done, 1)

            def pow8(t):
                pe.wait_ge(act_done, at("act", "pow4_n", t))
                pe.wait_ge(dve_done, at("dve", "pow4_a", t))
                heads(ps[:, delta_bank(t, 0)], lambda h: pw_n4[:, t, h], lambda h: pw_a4[:, t, h])
                heads(ps[:, delta_bank(t, 2)], lambda h: pw_a4[:, t, h], lambda h: m_mat[:, t, h]).then_inc(pe_done, 1)

            def pow16(t):
                pe.wait_ge(act_done, at("act", "pow8_a", t))
                pe.wait_ge(dve_done, at("dve", "pow8_m", t))
                heads(ps[:, delta_bank(t, 2)], lambda h: pw_a[:, t, h], lambda h: m_mat[:, t, h]).then_inc(pe_done, 1)

            def turn_m(t):
                pe.wait_ge(dve_done, at("dve", "pow16_m", t))
                heads(ps[:, delta_bank(t, 0)], lambda h: m_mat[:, t, h], None, turn=True).then_inc(pe_done, 1)

            def kq(t):
                pe.wait_ge(dve_done, at("dve", "k_decayed"))
                heads(ps[:, 6 + t], lambda h: qk[:, 4 + h, tok(t)], lambda h: qk[:, h, tok(t)]).then_inc(pe_done, 1)

            def double_y(s, t):
                pe.wait_ge(act_done, at("act", "t_rows", t))
                pe.wait_ge(pool_done, at("pool", "corner", s, t))
                if s == 0:
                    pe.wait_ge(dve_done, at("dve", "pow16_m", t))
                else:
                    pe.wait_ge(dve_done, at("dve", "doubled", s - 1, t))
                heads(ps[:, delta_bank(t, 0)], lambda h: pw_n[:, t, h], lambda h: m_mat[:, t, h]).then_inc(pe_done, 1)

            def double(s, t):
                pe.wait_ge(act_done, at("act", "y", s, t))
                ins = heads(ps[:, delta_bank(t, 1)], lambda h: t_mat[:, t, h], lambda h: pw_a[:, t, h])
                if s < 2:
                    ins = heads(ps[:, delta_bank(t, 2)], lambda h: pw_a[:, t, h], lambda h: t_mat[:, t, h])
                ins.then_inc(pe_done, 1)

            def u(t):
                if t == 0:
                    pe.wait_ge(dve_done, at("dve", "doubled", 2, 1))
                else:
                    pe.wait_ge(dve_done, at("dve", "v_less"))
                heads(ps[:, t], lambda h: m_mat[:, t, h], lambda h: v_beta[:, t, h]).then_inc(pe_done, 1)

            def state_mm():
                pe.wait_ge(act_done, at("act", "v_new", 0))
                heads(ps[:, 0], lambda h: k_dec[:, h], lambda h: v_new[:, 0, h]).then_inc(pe_done, 1)

            def from_state():
                pe.wait_ge(act_done, at("act", "state_copy"))
                heads(ps[:, 1], lambda h: qk[:, 4 + h, tok(1)], lambda h: state[:, h]).then_inc(pe_done, 1)

            def delta_out(g):
                pe.wait_ge(act_done, at("act", "v_new", 1))
                pe.wait_ge(dve_done, at("dve", "q_decayed"))
                for i in range(2):
                    h, o = 2 * g + i, ps[:, 6 + g, SEQ * i:SEQ * i + SEQ]
                    pe.matmul(o[:, 0:P], v_new[:, 0, h], decay_t[:, 0, h], start=True, stop=True)
                    pe.matmul(o[:, P:SEQ], v_new[:, 1, h], decay_t[:, 1, h], start=True, stop=False)
                    ins = pe.matmul(o[:, P:SEQ], state[:, h], q_dec[:, h], start=False, stop=True)
                ins.then_inc(pe_done, 1)

            def ret_scores(h):
                pe.wait_ge(dve_done, at("dve", "rope", ("r64", 1)))
                if h >= 2:
                    pe.wait_ge(dve_done, at("dve", "ret_decay", h - 2))
                r = slice(64 * (h % 2), 64 * (h % 2) + 64)
                q, k = rqk[r, h // 2], rqk[r, 2 + h // 2]
                pe.matmul(ps[:, 2 + h % 2, 0:SEQ], k[:, 0:P], q, start=True, stop=True)
                pe.matmul(ps[:, 2 + h % 2, SEQ:384], k[:, P:SEQ], q[:, P:SEQ], start=True, stop=True).then_inc(pe_done, 1)

            def weighted(o, v0, v1, first, second, full=False):
                pe.matmul(o, v0, first, start=True, stop=False, skip_group_check=True)
                return pe.matmul(o if full else o[:, P:SEQ], v1, second, start=False, stop=True, skip_group_check=True)

            def ret_out(h):
                pe.wait_ge(dve_done, at("dve", "ret_decay", h))
                weighted(ps[:, 4 + h // 2, SEQ * (h % 2):SEQ * (h % 2) + SEQ], rv[:, 0, P * h:P * h + P], rv[:, 1, P * h:P * h + P],
                         ret_p[:, h, 0:SEQ], ret_p[:, h, SEQ:384]).then_inc(pe_done, 1)

            def swap(unit):
                values, matrix, _, _, bank, ready = ropes[unit]
                pe.wait_ge(done[ready[0]], at(*ready))
                if rope_index[unit] >= 2:
                    pe.wait_ge(dve_done, at("dve", "rope", rope_list[rope_index[unit] - 2][0]))
                for t_ in ("tab1", "tab2", "tab3"):
                    if unit[0] in {"tab1": ("r64",), "tab2": ("r128", "r64b"), "tab3": ("mq0", "mk0", "mq1", "mk1")}[t_]:
                        pe.wait_ge(loaded[t_], 16)
                pe.matmul(ps[:, bank], matrix, values, start=True, stop=True).then_inc(pe_done, 1)

            def cn_sum(unit):
                src, ones, _, _, _, _, _, bank, _ = norms[unit]
                pe.wait_ge(act_done, at("act", "cn_sq", unit))
                if unit[0] in ("mq0", "mq1") and unit[1] == 0:
                    pe.wait_ge(dve_done, at("dve", "level_in", int(unit[0][2]), 7))
                if unit[0] == "fo":
                    pe.wait_ge(dve_done, at("dve", "mask_max", ("dil", 3)))
                if unit[0][:2] == "sq":
                    pe.wait_ge(dve_done, at("dve", "cn_use", ("ho" + unit[0][2], unit[1])))
                pe.matmul(ps[:, bank], ones, sq[norm_index[unit] % 2], start=True, stop=True).then_inc(pe_done, 1)

            def scores(unit):
                maps, _, _, full, _, _, _, ready = atts[unit]
                pe.wait_ge(done[ready[0]], at(*ready))
                i = att_index[unit]
                if unit[0].startswith("moba") and unit[1] < 2:
                    pe.wait_ge(act_done, at("act", "cn_rstd", ("ho" + unit[0][4], 1)))
                back = score_bank(unit, 0, True)
                if i >= back:
                    pe.wait_ge(dve_done, at("dve", "mask_max", att_list[i - back]))
                for m, (q, k) in enumerate(maps):
                    bank = ps[:, score_bank(unit, m)]
                    pe.matmul(bank[:, 0:SEQ if full else P], q[:, 0:P], k if full else k[:, 0:P], start=True, stop=True)
                    a = SEQ if full else P
                    ins = pe.matmul(bank[:, a:a + SEQ], q[:, P:SEQ], k, start=True, stop=True)
                ins.then_inc(pe_done, 1)

            def turn_p(unit):
                i, full = att_index[unit], atts[unit][3]
                pe.wait_ge(dve_done, at("dve", "divide", unit))
                if i >= 2:
                    pe.wait_ge(act_done, at("act", "p_cols", att_list[i - 2]))
                p, bank = probs[:, i % 2, 0], ps[:, 2 + i % 2]
                second = SEQ if full else P
                pe.transpose(bank[:, 0:P], p[:, 0:P], ident)
                pe.transpose(bank[:, P:SEQ], p[:, second:second + P], ident)
                if full:
                    pe.transpose(bank[:, SEQ:384], p[:, P:SEQ], ident)
                    ins = pe.transpose(bank[:, 384:512], p[:, 384:512], ident)
                else:
                    ins = pe.transpose(bank[:, SEQ:384], p[:, second + P:second + SEQ], ident)
                ins.then_inc(pe_done, 1)

            def attend(unit):
                _, v, o, full, *_ = atts[unit]
                i = att_index[unit]
                pe.wait_ge(act_done, at("act", "p_cols", unit))
                if unit in (("dil", 0), ("dil", 2)):
                    pe.wait_ge(act_done, at("act", "evacuate", "in1", 11))
                if unit[0].startswith("matt") and unit[1] == 0:
                    pe.wait_ge(dve_done, at("dve", "gate_out", ("moba" + unit[0][4:], 1)))
                p = p_t[:, i % 2]
                weighted(o, v[:, 0], v[:, 1], p[:, 0:SEQ], p[:, SEQ:512] if full else p[:, SEQ:384], full).then_inc(pe_done, 1)

            def lam_sum():
                pe.wait_ge(dve_done, at("dve", "lam_mul"))
                pe.matmul(ps[:, 3, 0:2], cst("ones")[0:64, :], lam_c[0:64, 0:2], start=True, stop=True).then_inc(pe_done, 1)

            def diagonal(l):
                pe.wait_ge(act_done, at("act", "k_gate", l))
                for t in range(TILES):
                    ins = heads(ps[:, 6 + t], lambda h: k_g[:, h, tok(t)], lambda h: qh[:, h, tok(t)])
                ins.then_inc(pe_done, 1)

            def level(l, v):
                pe.wait_ge(dve_done, at("dve", "q_level", l, v))
                pe.wait_ge(pool_done, at("pool", "k_level", l, v))
                if v >= 2:
                    pe.wait_ge(dve_done, at("dve", "level_in", l, v - 2))
                k, q = k_l[v % 2], q_l[v % 2]
                if v < 7:
                    for t in range(TILES):
                        ins = heads(ps[:, 2 * (v % 2) + t], lambda h: k[:, h, tok(t)], lambda h: q[:, h, tok(t)])
                else:
                    ins = heads(ps[:, 2], lambda h: k[:, h, tok(0)], lambda h: q[:, h, tok(1)])
                ins.then_inc(pe_done, 1)

            def hgrn_out(l, g):
                pe.wait_ge(dve_done, at("dve", "level_in", l, 7))
                for i in range(2):
                    h, o = 2 * g + i, ps[:, 6 + g, SEQ * i:SEQ * i + SEQ]
                    v0, v1 = ih[:, 0, P * h:P * h + P], ih[:, 1, P * h:P * h + P]
                    pe.matmul(o[:, 0:P], v0, h_s[:, 0, h], start=True, stop=True)
                    pe.matmul(o[:, P:SEQ], v0, h_s01[:, h], start=True, stop=False)
                    ins = pe.matmul(o[:, P:SEQ], v1, h_s[:, 1, h], start=False, stop=True)
                ins.then_inc(pe_done, 1)

            steps("pe", {"ffn": ffn, "ffn_down": ffn_down, "panel": panel, "half": half_panel, "turn_x": turn_x, "ab_mm": ab_mm, "cumsum": cumsum, "turn_v": turn_v,
                         "turn_k": turn_k, "kk": kk, "turn_a": turn_a, "pow2": pow2, "pow4": pow4, "pow8": pow8, "pow16": pow16,
                         "turn_m": turn_m, "kq": kq, "double_y": double_y, "double": double, "u": u, "state": state_mm,
                         "from_state": from_state, "delta_out": delta_out, "ret_scores": ret_scores, "ret_out": ret_out,
                         "swap": swap, "cn_sum": cn_sum, "scores": scores, "turn_p": turn_p, "attend": attend,
                         "lam_sum": lam_sum, "diagonal": diagonal, "level": level, "hgrn_out": hgrn_out})

        @block.scalar
        def _(act):
            chained = [0]

            def step(ins):
                chained[0] += 1
                ins.then_inc(act_chain, 1)
                act.wait_ge(act_chain, chained[0])

            def split_hi(n, j=None, step_=0):
                s = n % SLOTS
                act.wait_ge(panel_loaded[s], of(j, 16 * (n // SLOTS + 1), 16 * step_ // SLOTS))
                if n >= SLOTS:
                    act.wait_ge(panel_used, of(j, n - SLOTS + 1, step_))
                nc.scalar.activation(w_hi[:, s], raw[:, s], ACT.Copy).then_inc(panel_hi, 1)

            def ffn(f):
                b, c = BASE[f"ffn{f}"], f * UPS

                def gate_up(i, j=None):
                    n = b + (0 if i == 0 else 3 * i - 1)
                    split_hi(n + 3, j, 6)
                    act.wait_ge(panel_used, of(j, n + 2, 6))
                    nc.scalar.activation(silu_buf, ps[:, 4], ACT.Silu).then_inc(silu_done, 1)
                    split_hi(n + 4, j, 6)

                def down_of(i, j=None):
                    split_hi(b + (3 * i + 4 if i < UPS - 1 else 3 * UPS - 1) + 3, j, 6)

                gate_up(0)
                gate_up(1)
                down_of(0)
                with act.Fori(0, (UPS - 3) // 2) as j:
                    for i in (2, 3):
                        gate_up(i, j)
                        down_of(i - 1, j)
                gate_up(UPS - 1)
                logs_and_exps()

            def wab_hi():
                act.wait_ge(loaded["small"], 16)
                nc.scalar.activation(wab_h[:], sm("wab", 0, 64), ACT.Copy).then_inc(act_done, 1)

            def sumsq_(tag, t, half):
                src, (e, *ready) = source_of(tag, t, half)
                if e == "load":
                    act.wait_ge(loaded[ready[0]], 16)
                else:
                    act.wait_ge(done[e], at(e, *ready))
                squares = mem_squares if tag in ("mem0", "mem1") else pair
                i, c = 2 * t + half, slice(512 * half, 512 * half + 512)
                step(nc.scalar.activation(squares[:, 512 * i:512 * i + 512], src[:, t, c], ACT.Square, accum_out=sumsq[:, i:i + 1]))
                if half == 0:
                    step(nc.scalar.activation(half_mean[:, t:t + 1], sumsq[:, i:i + 1], ACT.Copy, bias=EPS, scale=1 / D))
                act.sem_inc(act_done, 1)

            def rstd_(tag, t):
                step(nc.scalar.activation(rstd[:, t:t + 1], sumsq[:, 2 * t + 1:2 * t + 2], ACT.Ln, bias=half_mean[:, t:t + 1],
                                          scale=1 / D))
                nc.scalar.activation(rstd[:, t:t + 1], rstd[:, t:t + 1], ACT.Exp, scale=-0.5).then_inc(act_done, 1)

            def x_hi(tag, t, half):
                act.wait_ge(pe_done, at("pe", "turn_x", tag, t, half))
                to = act_hi[:, 4 * half:4 * half + 4, P * t:P * t + P]
                if tag in ("mem0", "mem1"):
                    act.wait_ge(panel_used, BASE["ffn3"] + 3 * UPS - 2 if tag == "mem0" else BASE["out2_0"] + N_OF["out2_0"])
                if tag in ("pre0", "pre1"):
                    act.wait_ge(panel_used, BASE["mem" + tag[3]] + N_OF["mem0"])
                nc.scalar.activation(to, grid(ps[:, turn_bank(tag, t, half)], 4), ACT.Copy).then_inc(act_done, 1)

            def evacuate(name, k):
                to, form, func = dest[name, k]
                act.wait_ge(panel_used, BASE[name] + k + 1)
                if name.startswith("in2") and k >= 16:
                    act.wait_ge(dve_done, at("dve", "gap_f" if k < 18 else "q_level", int(name[4]), 7))
                nc.scalar.activation(to, grid(ps[:, bank_of(name, k)], 2), func).then_inc(act_done, 1)

            def silu(name, k):
                act.wait_ge(act_done, at("act", "evacuate", name, k))
                for z in (z0, rg) if name == "in0" else (z2[:, 0:4], z2[:, 4:8], z2[:, 8:12]):
                    ins = nc.scalar.activation(z, z, ACT.Silu)
                ins.then_inc(act_done, 1)

            def tap(p):
                act.wait_ge(pool_done, at("pool", "zero"))
                act.wait_ge(loaded["small"], 16)
                act.wait_ge(act_done, at("act", "evacuate", "in0", p))
                for i in range(2):
                    b = 2 * p + i
                    ins = nc.scalar.activation(conv_out(b), raw_qkv[:, b, 4:260], ACT.Copy, scale=sm("conv", 4 * b + 3))
                ins.then_inc(act_done, 1)

            def conv_silu(p):
                act.wait_ge(dve_done, at("dve", "conv", p))
                for i in range(2):
                    ins = nc.scalar.activation(conv_out(2 * p + i), conv_out(2 * p + i), ACT.Silu)
                ins.then_inc(act_done, 1)

            def logs_and_exps():
                nc.scalar.preload_act_table_set("natural_log_exp_and_others")

            def ab_exp():
                act.wait_ge(pe_done, at("pe", "ab_mm"))
                ab = grid(ps[:, 6, 0:16], 2)
                nc.scalar.activation(grid(b_exp, 2), ab[:, :, 0:4], ACT.Exp, scale=-1.0).then_inc(act_done, 1)

            def softplus():
                act.wait_ge(dve_done, at("dve", "ab"))
                step(nc.scalar.activation(e_sp, e_sp, ACT.Exp))
                nc.scalar.activation(e_sp, e_sp, ACT.Ln, bias=cst("one"))
                nc.scalar.activation(e_alog, sm("alog", 0, 4), ACT.Exp).then_inc(act_done, 1)

            def decay(t):
                act.wait_ge(dve_done, at("dve", "gap", t))
                nc.scalar.activation(decay_t[:, t], decay_t[:, t], ACT.Exp)
                ins = nc.scalar.activation(a_low[:, t], a_low[:, t], ACT.Exp, scale=-1.0)
                if t == 0:
                    nc.scalar.activation(e_gc, gc, ACT.Exp)
                    ins = nc.scalar.activation(e_kd, e_kd, ACT.Exp)
                else:
                    ins = nc.scalar.activation(q_dec, grid(ps[:, 3], 4), ACT.Exp)
                ins.then_inc(act_done, 1)

            def copy_back(to, bank, n=4):
                return nc.scalar.activation(to, grid(ps[:, bank], n), ACT.Copy).then_inc(act_done, 1)

            def pow2_n(t):
                act.wait_ge(pe_done, at("pe", "pow2", t))
                copy_back(pw_n[:, t], delta_bank(t, 0))

            def pow4_n(t):
                act.wait_ge(pe_done, at("pe", "pow4", t))
                copy_back(pw_n4[:, t], delta_bank(t, 0))

            def pow8_a(t):
                act.wait_ge(pe_done, at("pe", "pow8", t))
                copy_back(pw_a[:, t], delta_bank(t, 0))

            def t_rows(t):
                act.wait_ge(pe_done, at("pe", "turn_m", t))
                copy_back(t_mat[:, t], delta_bank(t, 0))

            def y(s, t):
                act.wait_ge(pe_done, at("pe", "double_y", s, t))
                copy_back(pw_a[:, t], delta_bank(t, 0))

            def v_new_(t):
                act.wait_ge(pe_done, at("pe", "u", t))
                copy_back(v_new[:, t], t)

            def state_copy():
                act.wait_ge(pe_done, at("pe", "state"))
                copy_back(state, 0)

            def cn_sq(unit):
                src, *_, ready = norms[unit]
                act.wait_ge(done[ready[0]], at(*ready))
                if unit[0] in ("mq0", "mq1") and unit[1] == 0:
                    act.wait_ge(dve_done, at("dve", "q_level", int(unit[0][2]), 7))
                    act.wait_ge(pool_done, at("pool", "k_level", int(unit[0][2]), 7))
                nc.scalar.activation(grid(sq[norm_index[unit] % 2], 2), src, ACT.Square).then_inc(act_done, 1)

            def cn_rstd(unit):
                _, _, inv, _, _, _, _, bank, _ = norms[unit]
                i = norm_index[unit]
                act.wait_ge(pe_done, at("pe", "cn_sum", unit))
                if i >= 2:
                    act.wait_ge(dve_done, at("dve", "cn_use", norm_list[i - 2]))
                step(nc.scalar.activation(rs[i % 2], ps[:, bank], ACT.Ln, bias=cst("eps"), scale=inv))
                nc.scalar.activation(rs[i % 2], rs[i % 2], ACT.Exp, scale=-0.5).then_inc(act_done, 1)

            def exp_(unit):
                maps, _, _, full, *_ = atts[unit]
                i = att_index[unit]
                act.wait_ge(dve_done, at("dve", "mask_max", unit))
                for m in range(len(maps)):
                    for q, (a, b) in enumerate(spans(full)):
                        p = probs[:, i % 2, m, a:b]
                        c = 2 * m + q
                        ins = nc.scalar.activation(p, p, ACT.Exp, bias=nmax[i % 2][:, c:c + 1], scale=-1.0,
                                                   accum_out=dens[i % 2][:, c:c + 1])
                step(ins)
                act.sem_inc(act_done, 1)

            def p_cols(unit):
                i, full = att_index[unit], atts[unit][3]
                act.wait_ge(pe_done, at("pe", "turn_p", unit))
                if i >= 2:
                    act.wait_ge(pe_done, at("pe", "attend", att_list[i - 2]))
                n = 512 if full else 384
                nc.scalar.activation(p_t[:, i % 2, 0:n], ps[:, 2 + i % 2, 0:n], ACT.Copy).then_inc(act_done, 1)

            def y_hi(l, b):
                act.wait_ge(dve_done, at("dve", "gate_out", (f"moba{l}" if b < 4 else f"matt{l}", b // 2 % 4)))
                act.wait_ge(panel_used, BASE[f"in2_{l}"] + N_OF[f"in2_{l}"])
                nc.scalar.activation(act_hi[:, out_block(b)], z2[:, b:b + 2], ACT.Copy).then_inc(act_done, 1)

            def lam_exp():
                act.wait_ge(pe_done, at("pe", "lam_sum"))
                nc.scalar.activation(lam_c[:, 2:4], ps[:, 3, 0:2], ACT.Exp).then_inc(act_done, 1)

            def sines():
                act.wait_ge(dve_done, at("dve", "angle"))
                nc.scalar.activation(sin_a, sin_a, ACT.Sin)
                nc.scalar.activation(cos_a, cos_a, ACT.Sin).then_inc(act_done, 1)

            def f_ln(l):
                act.wait_ge(dve_done, at("dve", "f_abs", l))
                step(nc.scalar.activation(hg[1], hg[1], ACT.Exp))
                ins = nc.scalar.activation(hg[1], hg[1], ACT.Ln, bias=cst("one"))
                if l:
                    step(nc.scalar.activation(lbn, lbn, ACT.Exp))
                    ins = nc.scalar.activation(lbn, lbn, ACT.Ln, bias=cst("one"))
                ins.then_inc(act_done, 1)

            def f_ln2(l):
                act.wait_ge(dve_done, at("dve", "f_log", l))
                step(nc.scalar.activation(hg[2], hg[2], ACT.Exp))
                nc.scalar.activation(hg[2], hg[2], ACT.Ln, bias=cst("one")).then_inc(act_done, 1)

            def k_gate(l):
                act.wait_ge(dve_done, at("dve", "f_log2" if l else "f_log", l))
                nc.scalar.activation(k_g, k_g, ACT.Exp).then_inc(act_done, 1)

            def decay_f(l, v):
                act.wait_ge(dve_done, at("dve", "gap_f", l, v))
                nc.scalar.activation(dec_f[v % 2], dec_f[v % 2], ACT.Exp).then_inc(act_done, 1)

            steps("act", {"split_hi": split_hi, "ffn": ffn, "wab_hi": wab_hi, "sumsq": sumsq_, "rstd": rstd_, "x_hi": x_hi,
                          "evacuate": evacuate, "silu": silu, "logs": logs_and_exps, "tap": tap, "conv_silu": conv_silu, "ab_exp": ab_exp, "softplus": softplus,
                          "decay": decay, "pow2_n": pow2_n, "pow4_n": pow4_n, "pow8_a": pow8_a, "t_rows": t_rows, "y": y,
                          "v_new": v_new_, "state_copy": state_copy, "cn_sq": cn_sq, "cn_rstd": cn_rstd, "exp": exp_,
                          "p_cols": p_cols, "y_hi": y_hi, "lam_exp": lam_exp, "sines": sines, "f_ln": f_ln, "f_ln2": f_ln2,
                          "k_gate": k_gate, "decay_f": decay_f})

        @block.vector
        def _(dve):
            chained = [0]

            def step(ins):
                chained[0] += 1
                ins.then_inc(dve_chain, 1)
                dve.wait_ge(dve_chain, chained[0])

            tt = nc.vector.tensor_tensor
            ts = nc.vector.tensor_scalar
            stt = nc.vector.scalar_tensor_tensor

            def finish(ins):
                finished[0] += 1
                ins.then_inc(dve_done, 1)
                dve.wait_ge(dve_done, finished[0])

            finished = [0]

            def split_lo(n, j=None, step_=0):
                s = n % SLOTS
                dve.wait_ge(panel_hi, of(j, n + 1, step_))
                tt(w_lo[:, s], raw[:, s], w_hi[:, s].bitcast(F32), ALU.subtract).then_inc(panel_lo, 1)

            def ffn(f):
                b, c = BASE[f"ffn{f}"], f * UPS

                def gate_up(i, j=None):
                    n = b + (0 if i == 0 else 3 * i - 1)
                    split_lo(n + 3, j, 6)
                    dve.wait_ge(silu_done, of(j, c + i + 1, 2))
                    if c + i:
                        dve.wait_ge(gate_ready, of(j, c + i, 2))
                    tt(g32, silu_buf, ps[:, 5], ALU.mult).then_inc(gate_read, 1)
                    dve.wait_ge(gate_read, of(j, c + i + 1, 2))
                    nc.vector.tensor_copy(g_hi[:, i % 2], grid(g32, 2)).then_inc(gate_hi, 1)
                    dve.wait_ge(gate_hi, of(j, c + i + 1, 2))
                    tt(g_lo[:, i % 2], grid(g32, 2), g_hi[:, i % 2].bitcast(F32), ALU.subtract).then_inc(gate_ready, 1)
                    split_lo(n + 4, j, 6)

                def down_of(i, j=None):
                    split_lo(b + (3 * i + 4 if i < UPS - 1 else 3 * UPS - 1) + 3, j, 6)

                gate_up(0)
                gate_up(1)
                down_of(0)
                with dve.Fori(0, (UPS - 3) // 2) as j:
                    for i in (2, 3):
                        gate_up(i, j)
                        down_of(i - 1, j)
                gate_up(UPS - 1)

            def wab_lo():
                dve.wait_ge(act_done, at("act", "wab_hi"))
                finish(tt(wab_l[:], sm("wab", 0, 64), wab_h[:].bitcast(F32), ALU.subtract))

            def residual(name, t, half):
                if (t, half) != (TILES - 1, 1):
                    dve.wait_ge(bank_ready, 3 * DOWNS.index(name) + 2 * t + half + 1)
                else:
                    dve.wait_ge(panel_used, BASE[name] + N_OF[name])
                if name == "ffn0":
                    dve.wait_ge(loaded["x"], 16)
                k = 0.5 if name.startswith("ffn") else 1.0
                c = slice(512 * half, 512 * half + 512)
                finish(stt(x[:, t, c], ps[:, 2 * t + half], k, x[:, t, c], ALU.mult, ALU.add))

            def scale(tag, t, half):
                src, _ = source_of(tag, t, half)
                dve.wait_ge(act_done, at("act", "rstd", tag, t))
                dve.wait_ge(loaded["gain_" + tag], 16)
                to = x if tag == "final" else xn_rows
                c = slice(512 * half, 512 * half + 512)
                finish(stt(to[:, t, c], src[:, t, c], rstd[:, t:t + 1], gain[:, c], ALU.mult, ALU.mult))

            def x_lo(tag, t, half):
                dve.wait_ge(act_done, at("act", "x_hi", tag, t, half))
                b, c = slice(4 * half, 4 * half + 4), slice(P * t, P * t + P)
                finish(tt(act_lo[:, b, c], grid(ps[:, turn_bank(tag, t, half)], 4), act_hi[:, b, c].bitcast(F32), ALU.subtract))

            def conv(p):
                dve.wait_ge(act_done, at("act", "tap", p))
                for k in (2, 1, 0):
                    for i in range(2):
                        b = 2 * p + i
                        ins = stt(conv_out(b), raw_qkv[:, b, 1 + k:1 + k + SEQ], sm("conv", 4 * b + k), conv_out(b), ALU.mult, ALU.add)
                    (step if k else finish)(ins)

            def ab():
                dve.wait_ge(act_done, at("act", "ab_exp"))
                step(ts(b_exp, b_exp, 1.0, None, ALU.add))
                nc.vector.reciprocal(beta, b_exp)
                step(tt(grid(xa, 2), grid(ps[:, 6, 0:16], 2)[:, :, 4:8], spread(sm("dt", 0, 4), 2), ALU.add))
                step(ts(e_sp, xa, -1.0, None, ALU.mult))
                finish(tt(e_sp, xa, e_sp, ALU.min))

            def g():
                dve.wait_ge(act_done, at("act", "softplus"))
                step(stt(g_col, xa, 0.0, e_sp, ALU.max, ALU.add))
                finish(stt(grid(g_col, 2), grid(g_col, 2), -1.0, spread(e_alog, 2), ALU.mult, ALU.mult))

            def gc_():
                dve.wait_ge(pe_done, at("pe", "cumsum"))
                step(nc.vector.tensor_copy(gc, ps[:, 6, 0:8]))
                finish(tt(e_kd.rearrange("p (a b) -> p a b", b=1), grid(ps[:, 2], 4)[:, :, P - 1:P], gc[:, 0:4].rearrange("p (a b) -> p a b", b=1),
                          ALU.subtract))

            def gap(t):
                step(tt(decay_t[:, t], grid(ps[:, 2 + t], 4), along(gc[:, 4 * t:4 * t + 4], P), ALU.subtract))
                step(ts(a_low[:, t], decay_t[:, t], 0.0, None, ALU.max))
                finish(ts(decay_t[:, t], decay_t[:, t], 0.0, None, ALU.min))

            def decay_mask(t):
                dve.wait_ge(act_done, at("act", "decay", t))
                tt(decay_t[:, t], decay_t[:, t], spread(tab(1, "upper"), 4), ALU.mult)
                step(tt(a_low[:, t], a_low[:, t], spread(tab(1, "strict"), 4), ALU.mult))
                if t:
                    tt(bge[:, 0:4], beta[:, 4:8], e_gc[:, 4:8], ALU.mult)
                finish(tt(a_low[:, t], a_low[:, t], along(beta[:, 4 * t:4 * t + 4], P), ALU.mult))

            def q_decayed():
                finish(tt(q_dec, q_dec, qk[:, 0:4, P:SEQ], ALU.mult))

            def v_beta_(t):
                dve.wait_ge(pe_done, at("pe", "turn_v", t))
                finish(tt(v_beta[:, t], grid(ps[:, t], 4), along(beta[:, 4 * t:4 * t + 4], P), ALU.mult))

            def k_decayed():
                dve.wait_ge(pe_done, at("pe", "turn_k"))
                finish(tt(k_dec, grid(ps[:, 2], 4), along(e_kd, P), ALU.mult))

            def a_low_(t):
                dve.wait_ge(pe_done, at("pe", "kk", t))
                finish(tt(a_low[:, t], a_low[:, t], grid(ps[:, delta_bank(t, 0)], 4), ALU.mult))

            def base16(t):
                dve.wait_ge(pe_done, at("pe", "turn_a", t))
                m16 = spread(tab(1, "diag16"), 4)
                step(tt(t_mat[:, t], grid(ps[:, delta_bank(t, 1)], 4), m16, ALU.mult))
                tt(pw_a4[:, t], a_low[:, t], m16, ALU.mult)
                finish(tt(m_mat[:, t], spread(ident, 4), t_mat[:, t], ALU.subtract))

            def add_to(to, bank, op=ALU.add):
                return tt(to, to, grid(ps[:, bank], 4), op)

            def pow2_a(t):
                dve.wait_ge(pe_done, at("pe", "pow2", t))
                finish(nc.vector.tensor_copy(pw_a[:, t], grid(ps[:, delta_bank(t, 1)], 4)))

            def pow4_a(t):
                dve.wait_ge(pe_done, at("pe", "pow4", t))
                nc.vector.tensor_copy(pw_a4[:, t], grid(ps[:, delta_bank(t, 1)], 4))
                finish(add_to(m_mat[:, t], delta_bank(t, 2)))

            def pow8_m(t):
                dve.wait_ge(pe_done, at("pe", "pow8", t))
                finish(add_to(m_mat[:, t], delta_bank(t, 2)))

            def pow16_m(t):
                dve.wait_ge(pe_done, at("pe", "pow16", t))
                finish(add_to(m_mat[:, t], delta_bank(t, 2)))

            def qk_decay(t):
                dve.wait_ge(pe_done, at("pe", "kq", t))
                finish(tt(decay_t[:, t], decay_t[:, t], grid(ps[:, 6 + t], 4), ALU.mult))

            def doubled(s, t):
                dve.wait_ge(pe_done, at("pe", "double", s, t))
                if s < 2:
                    add_to(t_mat[:, t], delta_bank(t, 2), ALU.subtract)
                finish(add_to(m_mat[:, t], delta_bank(t, 1), ALU.subtract))

            def v_less():
                dve.wait_ge(pe_done, at("pe", "from_state"))
                tmp = grid(xn[:, 0:512], 4)
                step(tt(tmp, grid(ps[:, 1], 4), along(bge[:, 0:4], P), ALU.mult))
                finish(tt(v_beta[:, 1], v_beta[:, 1], tmp, ALU.subtract))

            def ret_decay(h):
                dve.wait_ge(pe_done, at("pe", "ret_scores", h))
                a, _ = PLACES[1]["ret"]
                finish(tt(ret_p[:, h], ps[:, 2 + h % 2, 0:384], table[:, a + 384 * h:a + 384 * h + 384], ALU.mult))

            def rope(unit):
                values, _, cos, sin, bank, _ = ropes[unit]
                dve.wait_ge(pe_done, at("pe", "swap", unit))
                if unit[0][0] == "m":
                    dve.wait_ge(act_done, at("act", "sines"))
                tmp = grid(xn[:, 512:1024], 2)
                step(tt(tmp, grid(ps[:, bank], 2), spread(sin, 2), ALU.mult))
                step(tt(values, values, spread(cos, 2), ALU.mult))
                finish(tt(values, values, tmp, ALU.add))

            def split_out(b):
                step(nc.vector.tensor_copy(act_hi[:, b:b + 2], grid(y32, 2)))
                finish(tt(act_lo[:, b:b + 2], grid(y32, 2), act_hi[:, b:b + 2].bitcast(F32), ALU.subtract))

            def cn_use(unit):
                src, _, _, k, to, gate, b, _, _ = norms[unit]
                dve.wait_ge(act_done, at("act", "cn_rstd", unit))
                r = grid(rs[norm_index[unit] % 2], 2)
                if to is not None:
                    finish(stt(to, src, k, r, ALU.mult, ALU.mult))
                    return
                step(stt(grid(y32, 2), src, k, r, ALU.mult, ALU.mult))
                if gate is not None:
                    step(tt(grid(y32, 2), grid(y32, 2), gate, ALU.mult))
                split_out(b)

            def gate_out(unit):
                gate, bank, last = gates[unit]
                dve.wait_ge(pe_done, at("pe", "attend", last))
                src = grid(ps[:, bank], 2)
                if gate is None:
                    step(nc.vector.tensor_copy(grid(y32, 2), src))
                    split_out(2 * unit[1])
                else:
                    finish(tt(gate, src, gate, ALU.mult))

            def y_lo(l, b):
                dve.wait_ge(act_done, at("act", "y_hi", l, b))
                finish(tt(act_lo[:, out_block(b)], z2[:, b:b + 2], act_hi[:, out_block(b)].bitcast(F32), ALU.subtract))

            def mask_max(unit):
                maps, _, _, full, mask, _, k, _ = atts[unit]
                i = att_index[unit]
                dve.wait_ge(pe_done, at("pe", "scores", unit))
                if i >= 2:
                    dve.wait_ge(pe_done, at("pe", "turn_p", att_list[i - 2]))
                for m in range(len(maps)):
                    for q, (a, b) in enumerate(spans(full)):
                        to, s = probs[:, i % 2, m, a:b], ps[:, score_bank(unit, m), a:b]
                        low = nmax[i % 2][:, 2 * m + q:2 * m + q + 1]
                        if full:
                            ins = ts(to, s, -k, None, ALU.mult, ALU.min, accum_out=low)
                        else:
                            ins = nc.vector.tensor_tensor_reduce(to, s, mask[:, a:b], -k, 3e38, ALU.add, ALU.min, low)
                finish(ins)

            def divide(unit):
                maps, _, _, full, _, times, _, _ = atts[unit]
                i = att_index[unit]
                p, den = probs[:, i % 2], dens[i % 2]
                dve.wait_ge(act_done, at("act", "exp", unit))
                if times is not None:
                    for q, (a, b) in enumerate(spans(full)):
                        ins = nc.vector.tensor_tensor_reduce(p[:, 0, a:b], p[:, 0, a:b], times[:, a:b], 1.0, 0.0, ALU.mult, ALU.add,
                                                             den[:, q:q + 1])
                    step(ins)
                step(nc.vector.reciprocal(den[:, 0:2 * len(maps)], den[:, 0:2 * len(maps)]))
                if len(maps) == 2:
                    step(ts(den[:, 2:4], den[:, 2:4], lam_c[:, 3:4], None, ALU.mult))
                for q, (a, b) in enumerate(spans(full)):
                    ins = ts(p[:, 0, a:b], p[:, 0, a:b], den[:, q:q + 1], None, ALU.mult)
                if len(maps) == 2:
                    step(ins)
                    for q, (a, b) in enumerate(spans(full)):
                        ins = stt(p[:, 0, a:b], p[:, 1, a:b], den[:, 2 + q:3 + q], p[:, 0, a:b], ALU.mult, ALU.add)
                finish(ins)

            def lam_mul():
                v = sm("lam", 0, 4)[0:64, :]
                step(tt(lam_c[0:64, 0:2], v[:, 0:2], v[:, 2:4], ALU.mult))
                finish(ts(dgain, sm("diff"), 1.0 - LAMBDA_INIT, None, ALU.mult))

            def lam():
                dve.wait_ge(act_done, at("act", "lam_exp"))
                step(tt(lam_c[:, 3:4], lam_c[:, 3:4], lam_c[:, 2:3], ALU.subtract))
                finish(ts(lam_c[:, 3:4], lam_c[:, 3:4], LAMBDA_INIT, None, ALU.subtract))

            def angle():
                dve.wait_ge(loaded["pos"], 16)
                dve.wait_ge(loaded["tab3"], 16)
                step(nc.vector.tensor_copy(ang, positions))
                step(ts(ang, ang, tab(3, "freq"), None, ALU.mult))
                for to, quarter in ((sin_a, 0.0), (cos_a, 0.25)):
                    step(ts(turns, ang, 1 / (2 * math.pi), quarter, ALU.mult, ALU.add))
                    step(ts(turns, turns, MAGIC, None, ALU.add))
                    step(ts(turns, turns, MAGIC, None, ALU.subtract))
                    step(stt(to, turns, -TWO_PI[0], ang, ALU.mult, ALU.add))
                    step(stt(to, turns, -TWO_PI[1], to, ALU.mult, ALU.add))
                    step(stt(to, turns, -TWO_PI[2], to, ALU.mult, ALU.add))
                    if quarter:
                        step(ts(to, to, math.pi / 2, None, ALU.add))
                    ins = ts(to, to, -PI_IN, PI_IN, ALU.max, ALU.min)
                    (finish if quarter else step)(ins)

            def f_abs(l):
                dve.wait_ge(act_done, at("act", "evacuate", f"in2_{l}", 3))
                step(ts(hg[1], fh, -1.0, None, ALU.mult))
                step(tt(hg[1], fh, hg[1], ALU.min))
                if l:
                    a, b = sm("lb", 0, 4), sm("lb", 4, 4)
                    tt(lbd[:, 0:4], b, a, ALU.subtract)
                    step(tt(lbd[:, 4:8], a, b, ALU.subtract))
                    step(tt(lbn[:, 0:4], lbd[:, 0:4], lbd[:, 4:8], ALU.min))
                    step(tt(lbn[:, 4:8], lbd[:, 0:4], lbd[:, 4:8], ALU.min))
                finish(nc.vector.memset(zero4, 0.0))

            def f_log(l):
                dve.wait_ge(act_done, at("act", "f_ln", l))
                step(stt(hg[1], fh, 0.0, hg[1], ALU.min, ALU.subtract))
                if l:
                    step(stt(lbl, lbd, 0.0, lbn, ALU.min, ALU.subtract))
                    step(tt(hg[1], hg[1], along(lbl[:, 4:8], SEQ), ALU.add))
                    step(tt(hg[2], hg[1], along(lbl[:, 0:4], SEQ), ALU.subtract))
                    step(ts(hg[3], hg[2], -1.0, None, ALU.mult))
                    step(tt(hg[2], hg[2], hg[3], ALU.min))
                finish(tt(k_g, hg[1], fh, ALU.subtract))

            def f_log2(l):
                dve.wait_ge(act_done, at("act", "f_ln2", l))
                step(tt(hg[1], hg[1], along(lbl[:, 0:4], SEQ), ALU.max))
                finish(tt(hg[1], hg[1], hg[2], ALU.add))

            def cum_f(l):
                for h in range(4):
                    ins = nc.vector.tensor_tensor_scan(fh[:, h], tab(3, "keep"), hg[1][:, h], 0.0, ALU.mult, ALU.add)
                finish(ins)

            def diagonal_in(l):
                dve.wait_ge(pe_done, at("pe", "diagonal", l))
                for t in range(TILES):
                    ins = tt(h_s[:, t], grid(ps[:, 6 + t], 4), spread(ident, 4), ALU.mult)
                finish(ins)

            def gap_f(l, v):
                if v >= 2:
                    dve.wait_ge(pool_done, at("pool", "k_level", l, v - 2))
                to = dec_f[v % 2]
                if v < 7:
                    b = 64 >> v
                    split = lambda r: r.rearrange("p h (n c) -> p (h n) c", c=2 * b)
                    a_, t_ = split(fh), split(to)
                    edge = a_[:, :, b - 1:b].broadcast_to([P, 4 * SEQ // (2 * b), b])
                    tt(t_[:, :, b:2 * b], a_[:, :, b:2 * b], edge, ALU.subtract)
                    finish(tt(t_[:, :, 0:b], edge, a_[:, :, 0:b], ALU.subtract))
                else:
                    tt(to[:, :, 0:P], fh[:, :, P - 1:P].broadcast_to([P, 4, P]), fh[:, :, 0:P], ALU.subtract)
                    finish(nc.vector.tensor_copy(to[:, :, P:SEQ], fh[:, :, P:SEQ]))

            def q_level(l, v):
                dve.wait_ge(act_done, at("act", "decay_f", l, v))
                if v >= 2:
                    dve.wait_ge(pe_done, at("pe", "level", l, v - 2))
                finish(tt(q_l[v % 2], qh, dec_f[v % 2], ALU.mult))

            def level_in(l, v):
                dve.wait_ge(pe_done, at("pe", "level", l, v))
                if v < 7:
                    a, _ = PLACES[3]["levels"]
                    mask = spread(table[:, a + P * v:a + P * v + P], 4)
                    for t in range(TILES):
                        ins = nc.vector.copy_predicated(h_s[:, t], mask.bitcast(U32), grid(ps[:, 2 * (v % 2) + t], 4))
                else:
                    ins = nc.vector.tensor_copy(h_s01, grid(ps[:, 2], 4))
                finish(ins)

            steps("dve", {"split_lo": split_lo, "ffn": ffn, "wab_lo": wab_lo, "residual": residual, "scale": scale, "x_lo": x_lo,
                          "conv": conv, "ab": ab, "g": g, "gc": gc_, "gap": gap, "decay_mask": decay_mask, "q_decayed": q_decayed,
                          "v_beta": v_beta_, "k_decayed": k_decayed, "a_low": a_low_, "base16": base16, "pow2_a": pow2_a,
                          "pow4_a": pow4_a, "pow8_m": pow8_m, "pow16_m": pow16_m, "qk_decay": qk_decay,
                          "doubled": doubled, "v_less": v_less, "ret_decay": ret_decay, "rope": rope, "cn_use": cn_use,
                          "gate_out": gate_out, "y_lo": y_lo, "mask_max": mask_max, "divide": divide, "lam_mul": lam_mul, "lam": lam,
                          "angle": angle, "f_abs": f_abs, "f_log": f_log, "f_log2": f_log2, "cum_f": cum_f,
                          "diagonal_in": diagonal_in, "gap_f": gap_f, "q_level": q_level, "level_in": level_in})


def kernel(**inputs):
    import concourse.bacc as bacc
    from concourse.bass_utils import run_bass_kernel_spmd as run

    a = {k: np.asarray(v) for k, v in inputs.items()}

    def up(w, cols):
        return [w[:, c:c + UPW].reshape(DC, P, UPW).transpose(1, 0, 2).reshape(P, PANEL) for c in cols]

    def down(w, order=None):
        return [w[2 * P * r:2 * P * (r + 1)].reshape(2, P, D).transpose(1, 0, 2).reshape(P, PANEL)
                for r in order or range(w.shape[0] // (2 * P))]

    def ffn(name):
        w = a[name + "_w_up"]
        gate, upper = up(w, range(0, D_FF, UPW)), up(w, range(D_FF, 2 * D_FF, UPW))
        low = down(a[name + "_w_down"])
        order = [gate[0], upper[0]]
        for i in range(1, UPS):
            order += [gate[i], upper[i], low[i - 1]]
        return order + [low[-1]]

    in0 = list(range(0, 2048, UPW)) + [3080, 3336] + list(range(2056, 3080, UPW))
    in1 = [c for a_, b_ in ((1536, 2560), (0, 1024), (2560, 3072), (1024, 1536)) for c in range(a_, b_, UPW)]
    in2 = [c for a_, b_ in ((1536, 3072), (0, 1024), (3584, 5120), (3072, 3584), (1024, 1536)) for c in range(a_, b_, UPW)]
    stream = ffn("l0_ffn1") + up(a["l0_w_in"], in0) + down(a["l0_w_out"]) + ffn("l0_ffn2")
    stream += ffn("l1_ffn1") + up(a["l1_w_in"], in1) + down(a["l1_w_out"], (2, 3, 0, 1)) + ffn("l1_ffn2")
    for l in range(2):
        stream += up(a["w_mem_kv_2"][l], range(0, D, UPW)) + up(a["w_in_2"][l], in2) + down(a["w_out_2"][l], (2, 3, 0, 1, 4, 5))
    panels = np.stack(stream)
    gains = np.stack([a["l0_ffn1_norm"], a["l0_mix_norm"], a["l0_ffn2_norm"], a["l1_ffn1_norm"], a["l1_mix_norm"],
                      a["l1_ffn2_norm"], a["mem_norm_g_2"][0], a["final_norm"], a["norm_g_2"][0], a["mem_norm_g_2"][1],
                      a["norm_g_2"][1]])
    small = np.zeros((P, SMALL_W), np.float32)

    def put(name, v):
        at_, n = SMALL[name]
        small[:v.shape[0], at_:at_ + n] = v

    put("conv", a["l0_conv_w"].reshape(4, 12, P).transpose(2, 1, 0).reshape(P, 48))
    put("wab", a["l0_w_in"][:, 2048:2056].reshape(DC, P, 8).transpose(1, 0, 2).reshape(P, 64))
    put("alog", np.broadcast_to(a["l0_a_log"], (P, 4)))
    put("dt", np.broadcast_to(a["l0_dt_bias"], (P, 4)))
    put("gdn", a["l0_gdn_norm"][:, None])
    put("diff", a["l1_diff_norm"][:, None])
    put("lam", np.stack([a["l1_lambda_q1"], a["l1_lambda_q2"], a["l1_lambda_k1"], a["l1_lambda_k2"]], axis=1))
    put("lb", a["hgrn_lb_logits_2"].reshape(2, 4, P).transpose(2, 0, 1).reshape(P, 8))
    for l in range(2):
        put(f"mq{l}", np.tile(a["moba_q_norm_2"][l], 2)[:, None])
        put(f"mk{l}", np.tile(a["moba_k_norm_2"][l], 2)[:, None])
        put(f"sq{l}", a["mem_q_norm_2"][l][:, None])
        put(f"sk{l}", a["mem_k_norm_2"][l][:, None])
        put(f"ho{l}", a["hgrn_o_norm_2"][l][:, None])

    def tiles(v):
        return np.ascontiguousarray(v.reshape(TILES, P, D).transpose(1, 0, 2))

    arrays = {"x_in": tiles(a["x"]), "mem_in": tiles(a["mem_2"]), "pos_in": np.ascontiguousarray(a["positions_2"].reshape(SEQ)),
              "panels": panels, "gains": gains, "small_in": small}
    arrays.update({f"tab{i}": t for i, t in enumerate(TABLES)})
    nc = bacc.Bacc("TRN2", target_bir_lowering=False, num_devices=1)
    aps = {k: nc.dram_tensor(k, v.shape, mybir.dt.from_np(v.dtype), kind="ExternalInput").ap() for k, v in arrays.items()}
    out = nc.dram_tensor("out", (P, TILES, D), F32, kind="ExternalOutput").ap()
    build(nc, **aps, out=out)
    r = run(nc, [arrays], core_ids=[0])
    got = np.asarray(r.results[0]["out"])
    return got.transpose(1, 0, 2).reshape(1, SEQ, D)
```
